# Optimizing a Trainium2 kernel written in Bass

```python
import jax, jax.numpy as jnp
from jax import lax
import numpy as np

D_MODEL = 1024
BATCH = 1
SEQ = 256
DEPTH = 1

ATTN_HEADS = 8
HEAD_DIM = D_MODEL // 16
ATTN_WIDTH = ATTN_HEADS * HEAD_DIM
ROPE_DIM = HEAD_DIM // 4
ROPE_THETA = 500000.0
MOBA_BLOCK = 256
MOBA_TOP_K = 3
QUERY_CHUNK = 64
POOL_WINDOWS = (2, 4, 8, 16)
POOL_GROUPS = len(POOL_WINDOWS)
POOL_WIDTH = D_MODEL // 2
POOL_GROUP_DIM = POOL_WIDTH // POOL_GROUPS
N_BRANCHES = 2
IN_WIDTH = 3 * ATTN_WIDTH + POOL_WIDTH + N_BRANCHES * D_MODEL
D_FF = 2816
CONV_WIDTH = 3
EPS = 1e-6
NEG_INF = -1e30


def rmsnorm(x, g):
    xf = x.astype(jnp.float32)
    y = xf * lax.rsqrt(jnp.mean(xf * xf, axis=-1, keepdims=True) + EPS)
    return (y * g.astype(jnp.float32)).astype(x.dtype)

def apply_partial_rotary(x, positions):
    half = ROPE_DIM // 2
    inv_freq = ROPE_THETA ** (-jnp.arange(half, dtype=jnp.float32) / half)
    ang = positions.astype(jnp.float32)[:, None] * inv_freq[None, :]
    cos = jnp.cos(ang).astype(x.dtype)
    sin = jnp.sin(ang).astype(x.dtype)
    x1 = x[..., :half]
    x2 = x[..., half:ROPE_DIM]
    return jnp.concatenate([x1 * cos - x2 * sin, x2 * cos + x1 * sin, x[..., ROPE_DIM:]], axis=-1)

def moba_attention(q, k, v):
    B, H, S, Dh = q.shape
    nb = -(-S // MOBA_BLOCK)
    pad = nb * MOBA_BLOCK - S
    k_p = jnp.pad(k, ((0, 0), (0, 0), (0, pad), (0, 0)))
    v_p = jnp.pad(v, ((0, 0), (0, 0), (0, pad), (0, 0)))
    k_blk = k_p.reshape(B, H, nb, MOBA_BLOCK, Dh)
    v_blk = v_p.reshape(B, H, nb, MOBA_BLOCK, Dh)
    k_mean = jnp.mean(k_blk.astype(jnp.float32), axis=3).astype(k.dtype)
    top_k = min(MOBA_TOP_K, nb)
    scale = Dh ** -0.5
    n_chunks = S // QUERY_CHUNK
    gather_blocks = jax.vmap(jax.vmap(lambda kb, idx: kb[idx]))

    def chunk(c):
        start = c * QUERY_CHUNK
        qc = lax.dynamic_slice_in_dim(q, start, QUERY_CHUNK, axis=2)
        q_pos = start + jnp.arange(QUERY_CHUNK)
        own = start // MOBA_BLOCK
        s_blk = jnp.einsum('bhqd,bhnd->bhqn', qc, k_mean).astype(jnp.float32)
        s_blk = jnp.where(jnp.arange(nb) < own, s_blk, -jnp.inf)
        _, sel = lax.top_k(s_blk, top_k)
        sel_valid = sel < own
        k_sel = gather_blocks(k_blk, sel)
        v_sel = gather_blocks(v_blk, sel)
        logit_sel = jnp.einsum('bhqd,bhqkld->bhqkl', qc, k_sel).astype(jnp.float32) * scale
        logit_sel = jnp.where(sel_valid[..., None], logit_sel, NEG_INF)
        k_own = lax.dynamic_index_in_dim(k_blk, own, axis=2, keepdims=False)
        v_own = lax.dynamic_index_in_dim(v_blk, own, axis=2, keepdims=False)
        logit_own = jnp.einsum('bhqd,bhld->bhql', qc, k_own).astype(jnp.float32) * scale
        k_pos_own = own * MOBA_BLOCK + jnp.arange(MOBA_BLOCK)
        logit_own = jnp.where(k_pos_own[None, :] <= q_pos[:, None], logit_own, NEG_INF)
        n_sel = top_k * MOBA_BLOCK
        logits = jnp.concatenate(
            [logit_sel.reshape(B, H, QUERY_CHUNK, n_sel), logit_own], axis=-1)
        p = jax.nn.softmax(logits, axis=-1).astype(v.dtype)
        p_sel = p[..., :n_sel].reshape(B, H, QUERY_CHUNK, top_k, MOBA_BLOCK)
        p_own = p[..., n_sel:]
        return (jnp.einsum('bhqkl,bhqkld->bhqd', p_sel, v_sel)
                + jnp.einsum('bhql,bhld->bhqd', p_own, v_own))

    outs = lax.map(chunk, jnp.arange(n_chunks))
    return outs.transpose(1, 2, 0, 3, 4).reshape(B, H, S, Dh)

def multiscale_pool_mixer(u, w_pool, pool_scale):
    B, S, _ = u.shape
    ug = u.reshape(B, S, POOL_GROUPS, POOL_GROUP_DIM).astype(jnp.float32)
    cs = jnp.cumsum(ug, axis=1)
    t = jnp.arange(S, dtype=jnp.float32)[None, :, None]
    groups = []
    for g, w in enumerate(POOL_WINDOWS):
        c = cs[:, :, g]
        c_prev = jnp.pad(c, ((0, 0), (w, 0), (0, 0)))[:, :S]
        count = jnp.minimum(t + 1.0, float(w))
        groups.append((c - c_prev) / count - ug[:, :, g])
    pooled = jnp.stack(groups, axis=2).astype(u.dtype)
    mixed = jnp.einsum('bsgc,gcd->bsgd', pooled, w_pool)
    return mixed.reshape(B, S, POOL_WIDTH) * pool_scale

def causal_depthwise_conv(u, w, b):
    S = u.shape[1]
    kw = w.shape[0]
    up = jnp.pad(u, ((0, 0), (kw - 1, 0), (0, 0)))
    out = up[:, 0:S] * w[0]
    for j in range(1, kw):
        out = out + up[:, j:j + S] * w[j]
    return out + b

def hybrid_layer(x, norm_mix_g, w_in, b_gate, q_norm_g, k_norm_g, w_pool, pool_scale,
                 w_branch_attn, w_branch_pool, w_out, norm_ffn_g, w_up, conv_w, conv_b, w_down):
    B, S, D = x.shape
    h = rmsnorm(x, norm_mix_g)
    proj = h @ w_in
    q, k, v, u_pool, gate_logits = jnp.split(
        proj, [ATTN_WIDTH, 2 * ATTN_WIDTH, 3 * ATTN_WIDTH, 3 * ATTN_WIDTH + POOL_WIDTH], axis=-1)

    def heads(t):
        return t.reshape(B, S, ATTN_HEADS, HEAD_DIM).transpose(0, 2, 1, 3)

    pos = jnp.arange(S)
    q = apply_partial_rotary(rmsnorm(heads(q), q_norm_g), pos)
    k = apply_partial_rotary(rmsnorm(heads(k), k_norm_g), pos)
    attn = moba_attention(q, k, heads(v)).transpose(0, 2, 1, 3).reshape(B, S, ATTN_WIDTH)
    pooled = multiscale_pool_mixer(u_pool, w_pool, pool_scale)

    gates = jax.nn.sigmoid(gate_logits + b_gate).reshape(B, S, N_BRANCHES, D)
    mixed = gates[:, :, 0] * (attn @ w_branch_attn) + gates[:, :, 1] * (pooled @ w_branch_pool)
    x = x + mixed @ w_out

    h2 = rmsnorm(x, norm_ffn_g)
    up = causal_depthwise_conv(h2 @ w_up, conv_w, conv_b)
    gate, val = jnp.split(up, 2, axis=-1)
    return x + (jax.nn.silu(gate) * val) @ w_down

def first_inputs(seed: int = 0) -> dict:
    key = jax.random.key(seed)
    ks = jax.random.split(key, 17)
    L = DEPTH
    f32 = jnp.float32

    def nrm(k, shape, scale):
        return jax.random.normal(k, shape, f32) * scale

    return {
        "x": nrm(ks[0], (BATCH, SEQ, D_MODEL), 1.0),
        "norm_mix_g": 1.0 + nrm(ks[1], (L, D_MODEL), 0.02),
        "w_in": nrm(ks[2], (L, D_MODEL, IN_WIDTH), D_MODEL ** -0.5),
        "b_gate": nrm(ks[3], (L, N_BRANCHES * D_MODEL), 0.1),
        "q_norm_g": 1.0 + nrm(ks[4], (L, HEAD_DIM), 0.02),
        "k_norm_g": 1.0 + nrm(ks[5], (L, HEAD_DIM), 0.02),
        "w_pool": nrm(ks[6], (L, POOL_GROUPS, POOL_GROUP_DIM, POOL_GROUP_DIM), POOL_GROUP_DIM ** -0.5),
        "pool_scale": 1.0 + nrm(ks[7], (L, POOL_WIDTH), 0.1),
        "w_branch_attn": nrm(ks[8], (L, ATTN_WIDTH, D_MODEL), ATTN_WIDTH ** -0.5),
        "w_branch_pool": nrm(ks[9], (L, POOL_WIDTH, D_MODEL), POOL_WIDTH ** -0.5),
        "w_out": nrm(ks[10], (L, D_MODEL, D_MODEL), D_MODEL ** -0.5),
        "norm_ffn_g": 1.0 + nrm(ks[11], (L, D_MODEL), 0.02),
        "w_up": nrm(ks[12], (L, D_MODEL, 2 * D_FF), D_MODEL ** -0.5),
        "conv_w": nrm(ks[13], (L, CONV_WIDTH, 2 * D_FF), CONV_WIDTH ** -0.5),
        "conv_b": nrm(ks[14], (L, 2 * D_FF), 0.02),
        "w_down": nrm(ks[15], (L, D_FF, D_MODEL), D_FF ** -0.5),
    }

def first_block(x, norm_mix_g, w_in, b_gate, q_norm_g, k_norm_g, w_pool, pool_scale,
              w_branch_attn, w_branch_pool, w_out, norm_ffn_g, w_up, conv_w, conv_b, w_down):
    for l in range(DEPTH):
        x = hybrid_layer(x, norm_mix_g[l], w_in[l], b_gate[l], q_norm_g[l], k_norm_g[l],
                         w_pool[l], pool_scale[l], w_branch_attn[l], w_branch_pool[l], w_out[l],
                         norm_ffn_g[l], w_up[l], conv_w[l], conv_b[l], w_down[l])
    return x


DEPTH_2 = 2

MLA_HEADS = 8
MLA_NOPE = 64
MLA_ROPE = 32
MLA_V = 64
Q_LORA = 384
KV_LORA = 256
ROPE_BASE = 10000.0
DSA_HEADS = 8
DSA_DIM = 64
IDX_HEADS = 8
IDX_DIM = 32
TOPK_MAX = 256
D_MIX = MLA_HEADS * MLA_V + DSA_HEADS * DSA_DIM
N_EXPERTS = 16
N_GROUPS = 4
EXPERTS_PER_GROUP = N_EXPERTS // N_GROUPS
TOP_K_EXPERTS = 2
GROUP_SCORE_K = 2
D_FF_EXPERT = 512
ALPHA = (2.0 * DEPTH_2) ** 0.25
BETA = (8.0 * DEPTH_2) ** -0.25
Q_BLOCK = 128
LN_EPS = 1e-5
RMS_EPS = 1e-6

SPLIT_SIZES = (Q_LORA, KV_LORA, MLA_ROPE, DSA_HEADS * DSA_DIM, DSA_DIM, DSA_DIM,
               IDX_HEADS * IDX_DIM, IDX_DIM, IDX_HEADS)
SPLIT_POINTS = tuple(int(v) for v in np.cumsum(SPLIT_SIZES)[:-1])
IN_COLS = int(sum(SPLIT_SIZES))
DSA_V_START = int(sum(SPLIT_SIZES[:5]))


def layer_norm(x, g, b):
    xf = x.astype(jnp.float32)
    mu = jnp.mean(xf, axis=-1, keepdims=True)
    var = jnp.mean(jnp.square(xf - mu), axis=-1, keepdims=True)
    y = (xf - mu) * lax.rsqrt(var + LN_EPS) * g.astype(jnp.float32) + b.astype(jnp.float32)
    return y.astype(x.dtype)

def rms_norm(x, g):
    xf = x.astype(jnp.float32)
    y = xf * lax.rsqrt(jnp.mean(jnp.square(xf), axis=-1, keepdims=True) + RMS_EPS)
    return (y * g.astype(jnp.float32)).astype(x.dtype)

def rope(x, pos):
    half = x.shape[-1] // 2
    inv = ROPE_BASE ** (-jnp.arange(half, dtype=jnp.float32) / half)
    ang = pos[:, None] * inv[None, :]
    cos = jnp.cos(ang)[None, :, None, :]
    sin = jnp.sin(ang)[None, :, None, :]
    xf = x.astype(jnp.float32)
    x1, x2 = xf[..., :half], xf[..., half:]
    return jnp.concatenate([x1 * cos - x2 * sin, x1 * sin + x2 * cos], axis=-1).astype(x.dtype)

def sweep_query_blocks(block_fn, seq_len):
    starts = jnp.arange(seq_len // Q_BLOCK, dtype=jnp.int32) * Q_BLOCK
    out = lax.map(block_fn, starts)
    nb, b, qb, h, d = out.shape
    return jnp.transpose(out, (1, 0, 2, 3, 4)).reshape(b, nb * qb, h * d)

def mla_group(qa, kva, kr, q_norm_g, w_q_up, kv_norm_g, w_uk, w_uv, pos):
    B, T, _ = qa.shape
    q = (rms_norm(qa, q_norm_g) @ w_q_up).reshape(B, T, MLA_HEADS, MLA_NOPE + MLA_ROPE)
    q = jnp.concatenate([q[..., :MLA_NOPE], rope(q[..., MLA_NOPE:], pos)], axis=-1)
    c_kv = rms_norm(kva, kv_norm_g)
    k_nope = (c_kv @ w_uk).reshape(B, T, MLA_HEADS, MLA_NOPE)
    v = (c_kv @ w_uv).reshape(B, T, MLA_HEADS, MLA_V)
    k_rope = rope(kr[:, :, None, :], pos)
    k = jnp.concatenate([k_nope, jnp.broadcast_to(k_rope, (B, T, MLA_HEADS, MLA_ROPE))], axis=-1)
    scale = (MLA_NOPE + MLA_ROPE) ** -0.5
    key_idx = jnp.arange(T, dtype=jnp.int32)

    def block(start):
        qb = lax.dynamic_slice_in_dim(q, start, Q_BLOCK, axis=1)
        s = jnp.einsum('bthd,bshd->bhts', qb, k).astype(jnp.float32) * scale
        tq = start + jnp.arange(Q_BLOCK, dtype=jnp.int32)
        s = jnp.where(key_idx[None, :] <= tq[:, None], s, -jnp.inf)
        p = jax.nn.softmax(s, axis=-1).astype(v.dtype)
        return jnp.einsum('bhts,bshd->bthd', p, v)

    return sweep_query_blocks(block, T)

def dsa_group(dq, dk, dv, iq, ik, iw, slopes, n_keep):
    B, T, _ = dq.shape
    q = dq.reshape(B, T, DSA_HEADS, DSA_DIM)
    iq = iq.reshape(B, T, IDX_HEADS, IDX_DIM)
    iw = iw * (IDX_HEADS ** -0.5)
    key_idx = jnp.arange(T, dtype=jnp.int32)
    scale = DSA_DIM ** -0.5
    gather = jax.vmap(lambda arr, idx: arr[idx])

    def block(start):
        qb = lax.dynamic_slice_in_dim(q, start, Q_BLOCK, axis=1)
        iqb = lax.dynamic_slice_in_dim(iq, start, Q_BLOCK, axis=1)
        iwb = lax.dynamic_slice_in_dim(iw, start, Q_BLOCK, axis=1)
        tq = start + jnp.arange(Q_BLOCK, dtype=jnp.int32)
        rel = jax.nn.relu(jnp.einsum('bthd,bsd->bths', iqb, ik) * (IDX_DIM ** -0.5))
        score = jnp.einsum('bths,bth->bts', rel, iwb).astype(jnp.float32)
        score = jnp.where(key_idx[None, None, :] <= tq[None, :, None], score, -jnp.inf)
        _, sel = lax.top_k(score, n_keep)
        k_sel = gather(dk, sel)
        v_sel = gather(dv, sel)
        dist = (tq[None, :, None] - sel).astype(jnp.float32)
        s = jnp.einsum('bthd,btkd->bhtk', qb, k_sel).astype(jnp.float32) * scale
        s = s - slopes[None, :, None, None] * dist[:, None, :, :]
        s = jnp.where((dist >= 0.0)[:, None, :, :], s, -jnp.inf)
        p = jax.nn.softmax(s, axis=-1).astype(v_sel.dtype)
        return jnp.einsum('bhtk,btkd->bthd', p, v_sel)

    return sweep_query_blocks(block, T)

def hybrid_mixer(h, w_in, q_norm_g, w_q_up, kv_norm_g, w_uk, w_uv, w_o, pos, slopes, n_keep):
    proj = h @ w_in
    qa, kva, kr, dq, dk, dv, iq, ik, iw = jnp.split(proj, SPLIT_POINTS, axis=-1)
    out_a = mla_group(qa, kva, kr, q_norm_g, w_q_up, kv_norm_g, w_uk, w_uv, pos)
    out_b = dsa_group(dq, dk, dv, iq, ik, iw, slopes, n_keep)
    return jnp.concatenate([out_a, out_b], axis=-1) @ w_o

def grouped_moe(h, router_w, router_bias, w_gate, w_up, w_down):
    B, T, D = h.shape
    xt = h.reshape(B * T, D)
    aff = jax.nn.sigmoid((xt @ router_w).astype(jnp.float32))
    biased = aff + router_bias.astype(jnp.float32)
    grouped = biased.reshape(-1, N_GROUPS, EXPERTS_PER_GROUP)
    group_score = jnp.sum(lax.top_k(grouped, GROUP_SCORE_K)[0], axis=-1)
    g_sel = jnp.argmax(group_score, axis=-1)
    in_group = (jnp.arange(N_EXPERTS) // EXPERTS_PER_GROUP)[None, :] == g_sel[:, None]
    _, e_idx = lax.top_k(jnp.where(in_group, biased, -jnp.inf), TOP_K_EXPERTS)
    wts = jnp.take_along_axis(aff, e_idx, axis=-1)
    wts = wts / jnp.sum(wts, axis=-1, keepdims=True)
    gates = jnp.sum(jax.nn.one_hot(e_idx, N_EXPERTS, dtype=jnp.float32) * wts[..., None], axis=1)
    hg = jnp.einsum('nd,edf->nef', xt, w_gate)
    hu = jnp.einsum('nd,edf->nef', xt, w_up)
    act = jax.nn.silu(hg) * hu * gates[:, :, None].astype(hg.dtype)
    out = jnp.einsum('nef,efd->nd', act, w_down)
    return out.reshape(B, T, D)

def second_inputs(seed: int = 0) -> dict:
    key = jax.random.key(seed)
    ks = jax.random.split(key, 20)
    f32 = jnp.float32
    nrm = lambda k, shape, s: jax.random.normal(k, shape, f32) * s
    col_scale = np.ones((IN_COLS,), np.float32)
    col_scale[DSA_V_START:DSA_V_START + DSA_DIM] = BETA
    w_in = nrm(ks[1], (DEPTH_2, D_MODEL, IN_COLS), D_MODEL ** -0.5) * jnp.asarray(col_scale)
    return {
        'x': jax.random.normal(ks[0], (BATCH, SEQ, D_MODEL), f32),
        'w_in': w_in,
        'q_norm_g': 1.0 + nrm(ks[2], (DEPTH_2, Q_LORA), 0.02),
        'w_q_up': nrm(ks[3], (DEPTH_2, Q_LORA, MLA_HEADS * (MLA_NOPE + MLA_ROPE)), Q_LORA ** -0.5),
        'kv_norm_g': 1.0 + nrm(ks[4], (DEPTH_2, KV_LORA), 0.02),
        'w_uk': nrm(ks[5], (DEPTH_2, KV_LORA, MLA_HEADS * MLA_NOPE), KV_LORA ** -0.5),
        'w_uv': nrm(ks[6], (DEPTH_2, KV_LORA, MLA_HEADS * MLA_V), BETA * KV_LORA ** -0.5),
        'w_o': nrm(ks[7], (DEPTH_2, D_MIX, D_MODEL), BETA * D_MIX ** -0.5),
        'ln1_g': 1.0 + nrm(ks[8], (DEPTH_2, D_MODEL), 0.02),
        'ln1_b': nrm(ks[9], (DEPTH_2, D_MODEL), 0.02),
        'router_w': nrm(ks[10], (D_MODEL, N_EXPERTS), D_MODEL ** -0.5),
        'router_bias': nrm(ks[11], (N_EXPERTS,), 0.01),
        'w_gate': nrm(ks[12], (DEPTH_2, N_EXPERTS, D_MODEL, D_FF_EXPERT), BETA * D_MODEL ** -0.5),
        'w_up': nrm(ks[13], (DEPTH_2, N_EXPERTS, D_MODEL, D_FF_EXPERT), BETA * D_MODEL ** -0.5),
        'w_down': nrm(ks[14], (DEPTH_2, N_EXPERTS, D_FF_EXPERT, D_MODEL), BETA * D_FF_EXPERT ** -0.5),
        'ln2_g': 1.0 + nrm(ks[15], (DEPTH_2, D_MODEL), 0.02),
        'ln2_b': nrm(ks[16], (DEPTH_2, D_MODEL), 0.02),
    }

def second_block(x, w_in, q_norm_g, w_q_up, kv_norm_g, w_uk, w_uv, w_o, ln1_g, ln1_b,
              router_w, router_bias, w_gate, w_up, w_down, ln2_g, ln2_b):
    T = x.shape[1]
    pos = jnp.arange(T, dtype=jnp.float32)
    n_keep = min(TOPK_MAX, T // 4)
    slopes = 2.0 ** (-8.0 * jnp.arange(1, DSA_HEADS + 1, dtype=jnp.float32) / DSA_HEADS)
    for l in range(DEPTH_2):
        mix = hybrid_mixer(x, w_in[l], q_norm_g[l], w_q_up[l], kv_norm_g[l], w_uk[l], w_uv[l],
                           w_o[l], pos, slopes, n_keep)
        x = layer_norm(ALPHA * x + mix, ln1_g[l], ln1_b[l])
        ffn = grouped_moe(x, router_w, router_bias, w_gate[l], w_up[l], w_down[l])
        x = layer_norm(ALPHA * x + ffn, ln2_g[l], ln2_b[l])
    return x


def setup_inputs(seed=0):
    out = dict(first_inputs(seed))
    for name, value in second_inputs(seed + 1).items():
        if name != "x":
            out[name + "_2"] = value
    return out


def reference(
    x, norm_mix_g, w_in, b_gate, q_norm_g, k_norm_g, w_pool, pool_scale, w_branch_attn,
    w_branch_pool, w_out, norm_ffn_g, w_up, conv_w, conv_b, w_down, w_in_2, q_norm_g_2,
    w_q_up_2, kv_norm_g_2, w_uk_2, w_uv_2, w_o_2, ln1_g_2, ln1_b_2, router_w_2, router_bias_2,
    w_gate_2, w_up_2, w_down_2, ln2_g_2, ln2_b_2,
):
    x = first_block(
        x, norm_mix_g, w_in, b_gate, q_norm_g, k_norm_g, w_pool, pool_scale, w_branch_attn,
        w_branch_pool, w_out, norm_ffn_g, w_up, conv_w, conv_b, w_down,
    )
    return second_block(
        x, w_in_2, q_norm_g_2, w_q_up_2, kv_norm_g_2, w_uk_2, w_uv_2, w_o_2, ln1_g_2, ln1_b_2,
        router_w_2, router_bias_2, w_gate_2, w_up_2, w_down_2, ln2_g_2, ln2_b_2,
    )


_drawn_inputs = setup_inputs


def setup_inputs(seed=0):
    import zlib

    import numpy as np

    out = dict(_drawn_inputs(seed))
    spreads = {}
    factors = {'norm_mix_g': 3.395,
     'q_norm_g': 8.0,
     'k_norm_g': 8.0,
     'norm_ffn_g': 2.992,
     'conv_b': 3.099,
     'q_norm_g_2': 8.0,
     'kv_norm_g_2': 8.0,
     'router_bias_2': 4.12}
    for name, (base, spread) in spreads.items():
        noise = np.random.default_rng([zlib.crc32(name.encode()), seed]).standard_normal(out[name].shape)
        drawn = base * np.exp(spread * noise) if base else spread * noise
        out[name] = __import__('jax').numpy.asarray(drawn.astype(out[name].dtype))
    for name, factor in factors.items():
        out[name] = (out[name] * factor).astype(out[name].dtype)
    return out
```

```python
from contextlib import ExitStack

import numpy as np

import concourse.bass as bass
from concourse import mybir

F32 = mybir.dt.float32
F32R = mybir.dt.float32r
BF16 = mybir.dt.bfloat16
ACT = mybir.ActivationFunctionType
ALU = mybir.AluOpType
AX = mybir.AxisListType

P = 128
SEQ, D = 256, 1024
HALVES = SEQ // P
DC = D // P
HEADS, HD = 8, 64
WIDTH = HEADS * HD
EPS_RMS, EPS_LN = 1e-6, 1e-5
NEG = -1e30

POOL_WINDOWS = (2, 4, 8, 16)
GROUPS = len(POOL_WINDOWS)
ROPE1 = HD // 4 // 2
FF = 2816
FFC = FF // P
TAPS = 3

LAYERS = 2
Q_LORA, KV_LORA, KR = 384, 256, 32
QC, KVC = Q_LORA // P, KV_LORA // P
ROPE2 = KR // 2
MLA_D = HD + KR
IDX_HEADS, IDX_D = 8, 32
KEEP = SEQ // 4
AT_KVA = Q_LORA
AT_KR = AT_KVA + KV_LORA
AT_DQ = AT_KR + KR
AT_DK = AT_DQ + WIDTH
AT_DV = AT_DK + HD
AT_IQ = AT_DV + HD
AT_IK = AT_IQ + IDX_HEADS * IDX_D
AT_IW = AT_IK + IDX_D
IN2 = AT_IW + IDX_HEADS
EXPERTS, EGROUPS, EPG, TOP_E = 16, 4, 4, 2
FFE = 512
ALPHA = (2.0 * LAYERS) ** 0.25
SLOPES = [2.0 ** (-8.0 * h / HEADS) for h in range(1, HEADS + 1)]
SC1 = HD ** -0.5
SC_MLA = MLA_D ** -0.5
SC_DSA = HD ** -0.5
N_PARAMS = 14
TAKEN = -3e38

RING = 3
SLAB = 2048

S_QK, S_VU, S_GATE, S_BA, S_BP, S_OUT = 0, 4, 8, 16, 18, 20
S_FFN = 24
S_FFN_LOOP = S_FFN + 2
N_FF = FFC // 2
S_BLOCK2 = S_FFN + 3 * N_FF
L_IN, L_IN_B, L_IN_C, L_QUP, L_UK, L_UV, L_O, L_MOE = 0, 4, 6, 7, 9, 10, 11, 15
PER_EXPERT = 6
PER_LAYER = L_MOE + PER_EXPERT * EXPERTS
S_END = S_BLOCK2 + LAYERS * PER_LAYER

C_ID = 0
C_MASK = C_ID + P
C_DIST = C_MASK + HALVES * SEQ
C_BAND = C_DIST + HALVES * SEQ
C_COS1 = C_BAND + GROUPS * HALVES * SEQ
C_SIN1 = C_COS1 + HALVES * ROPE1
C_COS2 = C_SIN1 + HALVES * ROPE1
C_SIN2 = C_COS2 + HALVES * ROPE2
C_TRI = C_SIN2 + HALVES * ROPE2
C_N = C_TRI + EPG * EPG

V_G1 = 0
V_BG = V_G1 + DC
V_G2 = V_BG + 2 * DC
V_PS = V_G2 + DC
V_QA = V_PS + GROUPS
V_KVA = V_QA + LAYERS * QC
V_N = V_KVA + LAYERS * KVC

SEMAPHORES = """x_in params_in ln_in out_stored
 raw_in0 raw_in1 raw_in2 hi_done lo_done slab_used
 fills_set turned_params params_copied
 squares_summed mean_square rstd_ready normed
 fm_turned fm_hi fm_lo
 qk_saved0 qk_saved1 vu_saved0 vu_saved1 gates_saved
 qk_squared qk_summed qk_scaled qk_gained rope_products rope_summed
 pairs_turned pairs_copied pooled_summed pooled_copied mixed_summed mixed_hi mixed_lo
 a_gated b_gated ab_summed x_updated
 scores logits bias_ready probs flipped probs_turned weighted sums_inverted heads_saved
 acc_closed tap2_g tap2_v tap1_g tap1_v taps_g taps_v silu_done up_gated act_ready act_hi act_lo
 in_saved0 in_saved1 qup_saved0 qup_saved1 uk_saved0 uk_saved1 uv_saved0 uv_saved1 pads_zero
 kr_spread turned_a copied_q copied_k stage_zero staged turned_b copied_even copied_odd
 idx_scores idx_relu idx_weights idx_added idx_masked topk_step sel_step
 ln_added ln_mean_step ln_centred ln_scaled ln_done
 router_logits router_exp router_step routed gates_spread gates_kept0 gates_kept1""".split()


def constants():
    c = np.zeros((P, C_N), np.float32)
    c[:, C_ID:C_ID + P] = np.eye(P)
    t = np.arange(SEQ)
    for half in range(HALVES):
        q = half * P + np.arange(P)
        at = half * SEQ
        c[:, C_MASK + at:C_MASK + at + SEQ] = np.where(t[None, :] <= q[:, None], 0.0, NEG)
        c[:, C_DIST + at:C_DIST + at + SEQ] = t[None, :] - q[:, None]
        for g, w in enumerate(POOL_WINDOWS):
            s = q
            inside = (s[:, None] <= t[None, :]) & (s[:, None] > t[None, :] - w)
            band = inside / np.minimum(t + 1.0, w)[None, :] - (s[:, None] == t[None, :])
            at = C_BAND + (g * HALVES + half) * SEQ
            c[:, at:at + SEQ] = band
        for n, theta, ccos, csin in ((ROPE1, 500000.0, C_COS1, C_SIN1), (ROPE2, 10000.0, C_COS2, C_SIN2)):
            inv = (np.float32(theta) ** (-np.arange(n, dtype=np.float32) / np.float32(n))).astype(np.float32)
            ang = q.astype(np.float32)[:, None] * inv[None, :]
            c[:, ccos + half * n:ccos + (half + 1) * n] = np.cos(ang)
            c[:, csin + half * n:csin + (half + 1) * n] = np.sin(ang)
    for e in range(EPG):
        for j in range(e):
            c[:, C_TRI + e * EPG + j] = 1.0
    return c


class Waits:

    def __init__(self, eng, sems):
        self.eng, self.sems, self.count = eng, sems, {}

    def next(self, name, k=1):
        self.count[name] = self.count.get(name, 0) + k
        self.eng.wait_ge(self.sems[name], self.count[name])

    def skip(self, name, k=1):
        self.count[name] = self.count.get(name, 0) + k

    def upto(self, name, n):
        if n > 0:
            self.eng.wait_ge(self.sems[name], n)


def build(nc, A, out):
    ctx = ExitStack()
    with ctx:
        def sb(name, shape, dt=F32):
            return ctx.enter_context(nc.sbuf_tensor(name, shape, dt))

        S = {name: ctx.enter_context(nc.semaphore(name)) for name in SEMAPHORES}
        bank = [ctx.enter_context(nc.psum_tensor(f"bank{i}", [P, 512], F32)) for i in range(8)]

        const = sb("const", [P, C_N])
        vec = sb("vec", [P, V_N])
        conv = sb("conv", [P, TAPS + 1, 2 * FFC])
        head_gain = sb("head_gain", [P, 2, HD])
        w_pool = sb("w_pool", [P, GROUPS, P])
        router_w = sb("router_w", [P, DC, EXPERTS])
        router_b = sb("router_b", [P, EXPERTS])
        power = sb("power", [P, HALVES * 2 * HEADS])
        zeros = sb("zeros", [P, 512], BF16)

        x = sb("x", [P, HALVES, D])
        xn = sb("xn", [P, HALVES, D])
        xs = sb("xs", [P, DC, 2 * SEQ], F32R)
        raw = sb("raw", [P, RING, SLAB])
        hi = sb("hi", [P, RING, SLAB], F32R)
        lo = sb("lo", [P, RING, SLAB], F32R)
        proj = sb("proj", [P, HALVES, IN2])
        gates = sb("gates", [P, 2 * DC, SEQ])
        wide_a = sb("wide_a", [P, HALVES * D])
        wide_b = sb("wide_b", [P, HALVES * D])
        value = sb("value", [P, HALVES, WIDTH])
        q_t = sb("q_t", [P, HEADS, SEQ])
        k_t = sb("k_t", [P, HEADS, SEQ])
        act_s = sb("act_s", [P, 2, 2, 2 * SEQ], F32R)
        logit = sb("logit", [P, 2, SEQ])
        prob = sb("prob", [P, 2, SEQ])
        prob_t = sb("prob_t", [P, 2, HALVES, P])
        bias_h = sb("bias_h", [P, 2, SEQ])
        row_min = sb("row_min", [P, 2 * HEADS])
        row_sum = sb("row_sum", [P, 2 * HEADS])
        row_inv = sb("row_inv", [P, 2 * HEADS])
        stat = sb("stat", [P, 3, HALVES * 2 * HEADS])
        best = sb("best", [P, 8])
        idx_w = sb("idx_w", [P, HALVES, IDX_HEADS])
        route = sb("route", [P, 8, HALVES * EXPERTS])
        route4 = sb("route4", [P, 2, HALVES * EGROUPS * EPG * EPG])

        ident = const[:, C_ID:C_ID + P]
        mask = const[:, C_MASK:C_DIST].rearrange("p (a t) -> p a t", a=HALVES)
        dist = const[:, C_DIST:C_BAND].rearrange("p (a t) -> p a t", a=HALVES)
        band = const[:, C_BAND:C_COS1].rearrange("p (g a t) -> p g a t", g=GROUPS, a=HALVES)

        def table(at, n):
            return const[:, at:at + HALVES * n].rearrange("p (a n) -> p a n", a=HALVES)

        cos1, sin1 = table(C_COS1, ROPE1), table(C_SIN1, ROPE1)
        cos2, sin2 = table(C_COS2, ROPE2), table(C_SIN2, ROPE2)
        tri = const[:, C_TRI:C_N].rearrange("p (e j) -> p e j", e=EPG)

        rows = gates[0:V_N, 0, 0:P]
        conv_rows = gates[0:2 * FFC, 2:4, :].rearrange("c a (b p) -> c (a b) p", p=P)
        qk = proj[:].rearrange("p a n -> p (a n)")[:, 0:HALVES * D].rearrange("p (a n) -> p a n", a=HALVES)
        vu = wide_a[:].rearrange("p (a n) -> p a n", a=HALVES)
        mix = wide_b[:].rearrange("p (c t) -> p c t", c=DC)
        pooled = value[:].rearrange("p a n -> p (a n)").rearrange("p (g t) -> p g t", g=GROUPS)
        q_up = wide_a[:].rearrange("p (a h d) -> p a h d", a=HALVES, h=HEADS)
        k_up = wide_b[:].rearrange("p (a h d) -> p a h d", a=HALVES, h=HEADS)
        ln_gb = wide_a[:].rearrange("p (g n) -> p g n", g=2)
        stage = wide_b[:, 0:HALVES * 6 * P].rearrange("p (a v n) -> p a v n", a=HALVES, v=6)
        T_DQ, T_DK, T_IK, T_IQ = 0, 4, 6, 10
        sparse_t = gates[:, 0:12, :]
        spare = gates[:, 12:16, :].rearrange("p a n -> p (a n)")
        sel_score = bias_h
        y = proj[:].rearrange("p a n -> p (a n)")[:, 0:4 * SEQ].rearrange("p (s c t) -> p s c t", s=2, c=2)

        def slab_of(tile, n, k):
            return lambda width: tile[:, n % RING, 0:k * width].rearrange("p (k n) -> p k n", k=k)

        def count(n, j=None, per=0):
            return n if j is None else j * per + n

        def layer_base(layer):
            return S_BLOCK2 + layer * PER_LAYER

        block = ctx.enter_context(nc.Block())

        @block.sync
        def _(sp):
            def load(n, src, j=None, per=0):
                k, width = src.shape[1], src.shape[2]
                if j is not None or n >= RING:
                    sp.wait_ge(S["lo_done"], count(n, j, per) - RING + 1)
                sp.dma_start(slab_of(raw, n, k)(width), src).then_inc(S[f"raw_in{n % RING}"], 16)

            def rows_of(w, k0, k, c0, width):
                return w[k0 * P:(k0 + k) * P, c0:c0 + width].rearrange("(k p) n -> p k n", p=P)

            w_in, w_up, w_down = A["w_in"][0], A["w_up"][0], A["w_down"][0]
            for i in range(HALVES):
                sp.dma_start(x[:, i, :], A["x"][0, i * P:(i + 1) * P, :]).then_inc(S["x_in"], 16)
            for g in range(2):
                for i in range(4):
                    load(S_QK + 4 * g + i, rows_of(w_in, 2 * i, 2, D * g, D))
            for i in range(8):
                load(S_GATE + i, rows_of(w_in, 0, DC, 2 * D + 256 * i, 256))
            for i in range(2):
                load(S_BA + i, rows_of(A["w_branch_attn"][0], 0, 4, 512 * i, 512))
            for i in range(2):
                load(S_BP + i, rows_of(A["w_branch_pool"][0], 0, 4, 512 * i, 512))
            for i in range(4):
                load(S_OUT + i, rows_of(A["w_out"][0], 2 * i, 2, 0, D))

            up_steps = w_up.rearrange("(k p) (s j n) -> s j p k n", p=P, s=2, j=N_FF)
            down_steps = w_down.rearrange("(j k p) n -> j p k n", p=P, k=2)
            load(S_FFN, up_steps[0, 0])
            load(S_FFN + 1, up_steps[1, 0])
            with sp.Fori(0, (N_FF - 1) // 2) as jj:
                for s in range(2):
                    n = S_FFN_LOOP + 3 * s
                    j = jj * 2 + (1 + s)
                    load(n, up_steps[0, j], jj, 6)
                    load(n + 1, up_steps[1, j], jj, 6)
                    load(n + 2, down_steps[jj * 2 + s], jj, 6)
            load(S_BLOCK2 - 1, down_steps[N_FF - 1])

            for layer in range(LAYERS):
                b = layer_base(layer)
                w = A["w_in_2"][layer]
                for i in range(4):
                    load(b + L_IN + i, rows_of(w, 2 * i, 2, 0, D))
                for i in range(2):
                    load(b + L_IN_B + i, rows_of(w, 4 * i, 4, D, 512))
                load(b + L_IN_C, rows_of(w, 0, DC, D + 512, IN2 - D - 512))
                for i in range(2):
                    load(b + L_QUP + i, rows_of(A["w_q_up_2"][layer], 0, QC, 4 * MLA_D * i, 4 * MLA_D))
                load(b + L_UK, rows_of(A["w_uk_2"][layer], 0, KVC, 0, WIDTH))
                load(b + L_UV, rows_of(A["w_uv_2"][layer], 0, KVC, 0, WIDTH))
                for i in range(4):
                    load(b + L_O + i, rows_of(A["w_o_2"][layer], 2 * i, 2, 0, D))
                gate_w = A["w_gate_2"][layer].rearrange("e (k p) (h n) -> e h p k n", p=P, h=2)
                up_w = A["w_up_2"][layer].rearrange("e (k p) (h n) -> e h p k n", p=P, h=2)
                down_w = A["w_down_2"][layer].rearrange("e (h k p) n -> e h p k n", p=P, h=2)
                with sp.Fori(0, EXPERTS) as e:
                    for i, w in enumerate((gate_w[e, 0], up_w[e, 0], gate_w[e, 1], up_w[e, 1],
                                           down_w[e, 0], down_w[e, 1])):
                        load(b + L_MOE + i, w, e, PER_EXPERT)
            sp.wait_ge(S["ln_done"], 2 * HALVES * LAYERS)
            for i in range(HALVES):
                sp.dma_start(out[0, i * P:(i + 1) * P, :], x[:, i, :]).then_inc(S["out_stored"], 16)
            sp.wait_ge(S["out_stored"], 16 * HALVES)

        @block.gpsimd
        def _(pool):
            w = Waits(pool, S)
            nc.gpsimd.memset(power[:], -0.5).then_inc(S["fills_set"], 1)
            nc.gpsimd.memset(zeros[:], 0.0).then_inc(S["fills_set"], 1)
            nc.gpsimd.memset(k_t[:], 0.0).then_inc(S["fills_set"], 1)
            w.next("fills_set", 3)

            def root(n):
                w.next("mean_square")
                nc.gpsimd.tensor_tensor(stat[:, 2, 0:n], stat[:, 1, 0:n], power[:, 0:n], ALU.pow)\
                    .then_inc(S["rstd_ready"], 1)

            def load_ln(gain, shift):
                pool.dma_start(ln_gb[:, 0, :], gain.partition_broadcast(P)).then_inc(S["ln_in"], 16)
                pool.dma_start(ln_gb[:, 1, :], shift.partition_broadcast(P)).then_inc(S["ln_in"], 16)

            root(HALVES)
            root(HALVES * 2 * HEADS)
            root(HALVES)
            for layer in range(LAYERS):
                root(2 * HALVES)
                if layer == 0:
                    pool.wait_ge(S["x_updated"], 8)
                else:
                    pool.wait_ge(S["ln_done"], 2 * HALVES * layer)
                nc.gpsimd.memset(q_up[:, :, :, MLA_D:P], 0.0).then_inc(S["pads_zero"], 1)
                nc.gpsimd.memset(k_up[:, :, :, MLA_D:P], 0.0).then_inc(S["pads_zero"], 1)
                w.next("turned_a", 8)
                load_ln(A["ln1_g_2"][layer], A["ln1_b_2"][layer])
                nc.gpsimd.memset(stage, 0.0).then_inc(S["stage_zero"], 1)
                w.next("stage_zero")
                w.next("in_saved0", 3)
                w.next("in_saved1", 5)
                for v in range(2):
                    nc.gpsimd.tensor_copy(stage[:, :, v, HD * v:HD * (v + 1)], proj[:, :, AT_DK:AT_DK + HD])\
                        .then_inc(S["staged"], 1)
                for v in range(4):
                    nc.gpsimd.tensor_copy(stage[:, :, 2 + v, IDX_D * v:IDX_D * (v + 1)],
                                          proj[:, :, AT_IK:AT_IK + IDX_D]).then_inc(S["staged"], 1)
                root(HALVES)
                pool.wait_ge(S["ln_done"], 2 * HALVES * layer + HALVES)
                load_ln(A["ln2_g_2"][layer], A["ln2_b_2"][layer])
                root(HALVES)

        @block.scalar
        def _(act):
            w = Waits(act, S)
            split = [0]

            def split_hi(n, j=None, per=0):
                act.wait_ge(S[f"raw_in{n % RING}"], 16 * count(n // RING + 1, j, per // RING))
                if j is not None or n >= RING:
                    act.wait_ge(S["slab_used"], count(n, j, per) - RING + 1)
                nc.scalar.copy(hi[:, n % RING, :], raw[:, n % RING, :]).then_inc(S["hi_done"], 1)

            def splits_to(n):
                while split[0] <= min(n, S_END - 1):
                    m = split[0]
                    short = (m - S_BLOCK2) % PER_LAYER if m >= S_BLOCK2 else -1
                    size = {L_IN_C: DC * (IN2 - D - 512), L_UK: 1024, L_UV: 1024}.get(short, SLAB)
                    size = 3 * 4 * MLA_D if short in (L_QUP, L_QUP + 1) else size
                    act.wait_ge(S[f"raw_in{m % RING}"], 16 * (m // RING + 1))
                    w.upto("slab_used", m - RING + 1)
                    nc.scalar.copy(hi[:, m % RING, 0:size], raw[:, m % RING, 0:size]).then_inc(S["hi_done"], 1)
                    split[0] += 1

            def params():
                loads = [(const[:], A["constants"]),
                         (rows[V_G1:V_BG, :], A["norm_mix_g"][0].rearrange("(c p) -> c p", p=P)),
                         (rows[V_BG:V_G2, :], A["b_gate"][0].rearrange("(c p) -> c p", p=P)),
                         (rows[V_G2:V_PS, :], A["norm_ffn_g"][0].rearrange("(c p) -> c p", p=P)),
                         (rows[V_PS:V_QA, :], A["pool_scale"][0].rearrange("(c p) -> c p", p=P)),
                         (rows[V_QA:V_KVA, :], A["q_norm_g_2"].rearrange("l (c p) -> (l c) p", p=P)),
                         (rows[V_KVA:V_N, :], A["kv_norm_g_2"].rearrange("l (c p) -> (l c) p", p=P)),
                         (conv_rows[:, 0:TAPS, :], A["conv_w"][0].rearrange("t (c p) -> c t p", p=P)),
                         (conv_rows[:, TAPS, :], A["conv_b"][0].rearrange("(c p) -> c p", p=P)),
                         (head_gain[:, 0, :], A["q_norm_g"][0].partition_broadcast(P)),
                         (head_gain[:, 1, :], A["k_norm_g"][0].partition_broadcast(P)),
                         (w_pool[:], A["w_pool"][0].rearrange("g c d -> c g d")),
                         (router_w[:], A["router_w_2"].rearrange("(k p) e -> p k e", p=P)),
                         (router_b[:], A["router_bias_2"].partition_broadcast(P))]
                for dst, src in loads:
                    act.dma_start(dst, src).then_inc(S["params_in"], 16)

            def squares(sources, scratch, after=None):
                for i, src in enumerate(sources):
                    if after:
                        after(i)
                    nc.scalar.activation(scratch(i), src, ACT.Square, accum_out=stat[:, 0, i:i + 1])\
                        .then_inc(S["squares_summed"], 1)

            fm = [0]

            def feature_major(chunks, gain=None):
                for b in range(0, chunks, 2):
                    k = min(2, chunks - b)
                    w.next("fm_turned")
                    src = bank[6 + fm[0] % 2][:, 0:k * SEQ].rearrange("p (c t) -> p c t", c=k)
                    if gain is None:
                        nc.scalar.copy(xs[:, b:b + k, 0:SEQ], src).then_inc(S["fm_hi"], 1)
                    else:
                        for c in range(k):
                            nc.scalar.activation(xs[:, b + c, 0:SEQ], src[:, c, :], ACT.Copy,
                                                 scale=vec[:, gain(b + c):gain(b + c) + 1]).then_inc(S["fm_hi"], 1)
                    fm[0] += 1

            units = [0]

            def attention(scale_out=None):
                base = units[0]

                def exps(i):
                    act.wait_ge(S["logits"], base + i + 1)
                    w.upto("flipped", base + i - 1)
                    keys = P * (i // HEADS + 1)
                    nc.scalar.activation(prob[:, i % 2, 0:keys], logit[:, i % 2, 0:keys], ACT.Exp,
                                         bias=row_min[:, i:i + 1], scale=-1.0,
                                         accum_out=row_sum[:, i:i + 1]).then_inc(S["probs"], 1)

                def turned(i):
                    act.wait_ge(S["flipped"], base + i + 1)
                    w.upto("weighted", base + i - 1)
                    nk = i // HEADS + 1
                    nc.scalar.copy(prob_t[:, i % 2, 0:nk, :],
                                   bank[2 + i % 2][:, 0:nk * P].rearrange("p (k q) -> p k q", k=nk))\
                        .then_inc(S["probs_turned"], 1)

                for i in range(2 * HEADS):
                    exps(i)
                    if i:
                        turned(i - 1)
                turned(2 * HEADS - 1)
                units[0] += 2 * HEADS

            def save_half(n, name, saves):
                act.wait_ge(S["slab_used"], n + 1)
                for dst, src in saves:
                    nc.scalar.copy(dst, src).then_inc(S[name], 1)

            params()
            act.wait_ge(S["x_in"], 16 * HALVES)
            squares([x[:, i, :] for i in range(HALVES)], lambda i: xn[:, i, :])
            w.next("turned_params")
            nc.scalar.copy(vec[:], bank[0][:, 0:V_N]).then_inc(S["params_copied"], 1)
            nc.scalar.copy(conv[:].rearrange("p t c -> p (t c)"), bank[1][:, 0:(TAPS + 1) * 2 * FFC])\
                .then_inc(S["params_copied"], 1)
            w.next("params_copied", 2)
            feature_major(DC, lambda c: V_G1 + c)
            splits_to(S_QK + 5)
            save_half(S_QK + 3, "qk_saved0", [(qk[:, 0, 512 * i:512 * (i + 1)], bank[i][:]) for i in range(2)])
            splits_to(S_VU + 5)
            save_half(S_VU + 3, "vu_saved0", [(vu[:, 0, 512 * i:512 * (i + 1)], bank[4 + i][:]) for i in range(2)])
            for i in range(8):
                splits_to(S_GATE + i + 2)
                act.wait_ge(S["slab_used"], S_GATE + i + 1)
                for c in range(2):
                    nc.scalar.activation(gates[:, 2 * i + c, :], bank[i % 4][:, c * SEQ:(c + 1) * SEQ], ACT.Sigmoid,
                                         bias=vec[:, V_BG + 2 * i + c:V_BG + 2 * i + c + 1])\
                        .then_inc(S["gates_saved"], 1)
            w.next("pooled_summed")
            for i in range(2):
                nc.scalar.copy(pooled[:, 2 * i:2 * i + 2, :],
                               bank[4 + i][:].rearrange("p (g t) -> p g t", g=2)).then_inc(S["pooled_copied"], 1)
            w.next("mixed_summed")
            for g in range(GROUPS):
                nc.scalar.activation(xs[:, 4 + g, 0:SEQ], bank[6 + g // 2][:, (g % 2) * SEQ:(g % 2 + 1) * SEQ],
                                     ACT.Copy, scale=vec[:, V_PS + g:V_PS + g + 1]).then_inc(S["mixed_hi"], 1)
            act.wait_ge(S["fills_set"], 3)
            for b in range(4):
                w.next("pairs_turned")
                src = bank[b % 2][:].rearrange("p (c t) -> p c t", c=2)
                if b < 2:
                    nc.scalar.copy(q_t[:, 2 * b:2 * b + 2, :], src).then_inc(S["pairs_copied"], 1)
                else:
                    for odd in range(2):
                        part = slice(HD * odd, HD * (odd + 1))
                        first = 4 * (b - 2) + odd
                        nc.scalar.copy(k_t[part, first:first + 3:2, :], src[part]).then_inc(S["pairs_copied"], 1)
            splits_to(S_BA + 2)
            attention()
            feature_major(4)
            splits_to(S_BP + 1)
            w.next("ab_summed")
            nc.scalar.copy(xs[:, :, 0:SEQ], mix).then_inc(S["mixed_hi"], 1)
            splits_to(S_OUT + 3)
            w.next("x_updated", 4)
            squares([x[:, i, :] for i in range(HALVES)], lambda i: xn[:, i, :])
            splits_to(S_FFN)
            feature_major(DC, lambda c: V_G2 + c)

            def ffn_step(n, par, j, jj=None):
                first = jj is None
                split_hi(n + 1, jj, 6)
                if not first:
                    split_hi(n + 2, jj, 6)
                for side, name in ((0, "tap2_g"), (1, "tap2_v")):
                    if side and not first:
                        split_hi(n + 3, jj, 6)
                    act.wait_ge(S["slab_used"], count(n + side + 1, jj, 6))
                    if not first:
                        act.wait_ge(S["act_lo"], j)
                    for c in range(2):
                        at = j * 2 + side * FFC + c
                        nc.scalar.activation(y[:, side, c, :], bank[side][:, c * SEQ:(c + 1) * SEQ], ACT.Identity,
                                             bias=conv[:, TAPS, bass.ds(at, 1)],
                                             scale=conv[:, 2, bass.ds(at, 1)]).then_inc(S[name], 1)
                act.wait_ge(S["taps_g"], j * 2 + 2)
                nc.scalar.activation(y[:, 0, :, :], y[:, 0, :, :], ACT.Silu).then_inc(S["silu_done"], 1)
                act.wait_ge(S["act_ready"], j + 1)
                nc.scalar.copy(act_s[:, par, :, 0:SEQ], y[:, 1, :, :]).then_inc(S["act_hi"], 1)

            ffn_step(S_FFN, 0, 0)
            split_hi(S_FFN_LOOP)
            with act.Fori(0, (N_FF - 1) // 2) as jj:
                for s in range(2):
                    ffn_step(S_FFN_LOOP + 3 * s, (1 + s) % 2, jj * 2 + (1 + s), jj)
            split[0] = S_BLOCK2

            for layer in range(LAYERS):
                b = layer_base(layer)
                feature_major(DC)
                splits_to(b + L_IN + 5)
                save_half(b + L_IN + 3, "in_saved0",
                          [(proj[:, 0, 512 * i:512 * (i + 1)], bank[i][:]) for i in range(2)])
                splits_to(b + L_IN_C + 1)
                save_half(b + L_IN_B + 1, "in_saved0", [(proj[:, 0, D:D + 512], bank[4][:])])
                w.next("in_saved0", 3)
                parts = [(i, at, n) for at, n in ((0, Q_LORA), (AT_KVA, KV_LORA)) for i in range(HALVES)]
                squares([proj[:, i, at:at + n] for i, at, n in parts],
                        lambda k: xn[:, parts[k][0], parts[k][1]:parts[k][1] + parts[k][2]],
                        after=lambda k: w.next("in_saved1", 5) if k == 1 else None)
                feature_major(QC + KVC, lambda c: V_QA + QC * layer + c if c < QC else V_KVA + KVC * layer + c - QC)
                splits_to(b + L_UV)
                w.next("pads_zero", 2)
                for i in range(2):
                    save_half(b + L_QUP + i, "qup_saved0",
                              [(q_up[:, 0, 4 * i:4 * i + 4, 0:MLA_D],
                                bank[2 * i][:, 0:4 * MLA_D].rearrange("p (h d) -> p h d", h=4))])
                save_half(b + L_UK, "uk_saved0",
                          [(k_up[:, 0, :, 0:HD], bank[4][:].rearrange("p (h d) -> p h d", h=HEADS))])
                save_half(b + L_UV, "uv_saved0", [(value[:, 0, :], bank[6][:])])
                splits_to(b + L_O + 2)
                for i in range(4):
                    w.next("turned_a")
                    nc.scalar.copy(q_t[:, 2 * i:2 * i + 2, :], bank[6][:].rearrange("p (c t) -> p c t", c=2))\
                        .then_inc(S["copied_q"], 1)
                    w.skip("turned_a")
                attention()
                for i in range(3):
                    w.next("turned_b")
                    nc.scalar.copy(sparse_t[:, 4 * i:4 * i + 2, :],
                                   bank[6][:].rearrange("p (c t) -> p c t", c=2)).then_inc(S["copied_even"], 1)
                    w.skip("turned_b")
                n_idx = HALVES * IDX_HEADS
                for i in range(n_idx):
                    keys = P * (i // IDX_HEADS + 1)
                    w.next("idx_scores")
                    w.upto("idx_added", n_idx * layer + i - 1)
                    nc.scalar.activation(logit[:, i % 2, 0:keys], bank[i % 2][:, 0:keys], ACT.Relu,
                                         scale=IDX_D ** -0.5).then_inc(S["idx_relu"], 1)
                attention()
                feature_major(DC)
                splits_to(b + L_O + 3)
                w.next("ln_centred", HALVES)
                squares([x[:, i, :] for i in range(HALVES)], lambda i: xn[:, i, :])
                feature_major(DC)
                w.next("router_logits")
                for i in range(HALVES):
                    nc.scalar.activation(route[:, 0, EXPERTS * i:EXPERTS * (i + 1)], bank[i][:, 0:EXPERTS], ACT.Exp,
                                         scale=-1.0).then_inc(S["router_exp"], 1)
                for i in range(EXPERTS // 4):
                    w.next("gates_spread")
                    nc.scalar.copy(gates[:, 4 * i:4 * i + 2, :], bank[3][:].rearrange("p (c t) -> p c t", c=2))\
                        .then_inc(S["gates_kept0"], 1)
                    w.skip("gates_spread")
                base = b + L_MOE
                steps = N_FF + layer * 2 * EXPERTS
                with act.Fori(0, EXPERTS) as e:
                    for i in range(3):
                        split_hi(base + i, e, PER_EXPERT)
                    for h in range(2):
                        done = steps + h + 1
                        act.wait_ge(S["slab_used"], count(base + 2 * h + 1, e, PER_EXPERT))
                        act.wait_ge(S["act_ready"], count(done - 1, e, 2))
                        nc.scalar.activation(y[:, 0, :, :], bank[2 * h][:].rearrange("p (c t) -> p c t", c=2),
                                             ACT.Silu).then_inc(S["silu_done"], 1)
                        split_hi(base + 3 + 2 * h, e, PER_EXPERT)
                        act.wait_ge(S["act_ready"], count(done, e, 2))
                        nc.scalar.copy(act_s[:, h, :, 0:SEQ], y[:, 1, :, :]).then_inc(S["act_hi"], 1)
                        if h == 0:
                            split_hi(base + 4, e, PER_EXPERT)
                split[0] = b + PER_LAYER
                w.next("ln_centred", HALVES)
                squares([x[:, i, :] for i in range(HALVES)], lambda i: xn[:, i, :])

        @block.vector
        def _(dve):
            w = Waits(dve, S)
            split = [0]
            tt = nc.vector.tensor_tensor

            def split_lo(n, j=None, per=0, size=SLAB):
                dve.wait_ge(S["hi_done"], count(n + 1, j, per))
                tt(lo[:, n % RING, 0:size], raw[:, n % RING, 0:size], hi[:, n % RING, 0:size].bitcast(F32),
                   ALU.subtract).then_inc(S["lo_done"], 1)

            def splits_to(n):
                while split[0] <= min(n, S_END - 1):
                    m = split[0]
                    short = (m - S_BLOCK2) % PER_LAYER if m >= S_BLOCK2 else -1
                    size = {L_IN_C: DC * (IN2 - D - 512), L_UK: 1024, L_UV: 1024}.get(short, SLAB)
                    size = 3 * 4 * MLA_D if short in (L_QUP, L_QUP + 1) else size
                    split_lo(m, size=size)
                    split[0] += 1

            def mean_square(parts, eps, signals):
                if signals:
                    w.next("squares_summed", signals)
                for i, (at, k, n) in enumerate(parts):
                    ins = nc.vector.tensor_scalar(stat[:, 1, at:at + k], stat[:, 0, at:at + k], 1.0 / n, eps,
                                                  ALU.mult, ALU.add)
                    if i == len(parts) - 1:
                        ins.then_inc(S["mean_square"], 1)

            fm = [0]

            def feature_major(chunks, gain=None):
                for b in range(0, chunks, 2):
                    k = min(2, chunks - b)
                    w.next("fm_hi", 1 if gain is None else k)
                    src = bank[6 + fm[0] % 2][:, 0:k * SEQ].rearrange("p (c t) -> p c t", c=k)
                    if gain is None:
                        tt(xs[:, b:b + k, SEQ:2 * SEQ], src, xs[:, b:b + k, 0:SEQ].bitcast(F32), ALU.subtract)\
                            .then_inc(S["fm_lo"], 1)
                    else:
                        for c in range(k):
                            ins = nc.vector.scalar_tensor_tensor(
                                out=xs[:, b + c, SEQ:2 * SEQ], in0=src[:, c, :],
                                scalar=vec[:, gain(b + c):gain(b + c) + 1],
                                in1=xs[:, b + c, 0:SEQ].bitcast(F32), op0=ALU.mult, op1=ALU.subtract)
                        ins.then_inc(S["fm_lo"], 1)
                    fm[0] += 1

            def rotate(x1, x2, c, s, tmp, shape, step="rope"):
                c, s = (t.unsqueeze(2).broadcast_to(shape) for t in (c, s))
                for dst, a, t in ((0, x1, c), (1, x2, s), (2, x2, c), (3, x1, s)):
                    tt(tmp(dst), a, t, ALU.mult).then_inc(S["rope_products"], 1)
                w.next("rope_products", 4)
                tt(x1, tmp(0), tmp(1), ALU.subtract).then_inc(S["rope_summed"], 1)
                tt(x2, tmp(2), tmp(3), ALU.add).then_inc(S["rope_summed"], 1)

            units = [0]

            def attention(scale, col, sparse=False):
                base = units[0]

                def logits(i):
                    half, h = divmod(i, HEADS)
                    keys = P * (half + 1)
                    m = mask[:, half, 0:keys]
                    if sparse:
                        w.upto("logits", base + i - 1)
                        nc.vector.scalar_tensor_tensor(out=prob_bias(i, keys), in0=dist[:, half, 0:keys],
                                                       scalar=SLOPES[h] / scale, in1=sel_score[:, half, 0:keys],
                                                       op0=ALU.mult, op1=ALU.add).then_inc(S["bias_ready"], 1)
                        w.next("bias_ready")
                        m = prob_bias(i, keys)
                    dve.wait_ge(S["scores"], base + i + 1)
                    w.upto("probs", base + i - 1)
                    nc.vector.tensor_tensor_reduce(logit[:, i % 2, 0:keys], bank[i % 2][:, 0:keys], m, -scale, 3e38,
                                                   ALU.add, ALU.min, row_min[:, i:i + 1]).then_inc(S["logits"], 1)

                def save(half):
                    at = slice(HEADS * half, HEADS * (half + 1))
                    dve.wait_ge(S["probs"], base + HEADS * (half + 1))
                    nc.vector.reciprocal(row_inv[:, at], row_sum[:, at]).then_inc(S["sums_inverted"], 1)
                    w.next("sums_inverted")
                    dve.wait_ge(S["weighted"], base + HEADS * (half + 1))
                    tt(xn[:, half, col:col + WIDTH].rearrange("p (h d) -> p h d", h=HEADS),
                       bank[4 + half][:].rearrange("p (h d) -> p h d", h=HEADS),
                       row_inv[:, at].unsqueeze(2).broadcast_to([P, HEADS, HD]), ALU.mult)\
                        .then_inc(S["heads_saved"], 1)

                for i in range(2 * HEADS):
                    logits(i)
                    if i == HEADS + 1:
                        save(0)
                save(1)
                units[0] += 2 * HEADS

            def prob_bias(i, keys):
                return spare[:, (i % 2) * SEQ:(i % 2) * SEQ + keys]

            def save_half(n, name, saves):
                dve.wait_ge(S["slab_used"], n + 1)
                for dst, src in saves:
                    nc.vector.tensor_copy(dst, src).then_inc(S[name], 1)

            def router():
                def step(ins):
                    ins.then_inc(S["router_step"], 1)
                    w.next("router_step")

                r = [route[:, i, :] for i in range(8)]
                n_groups = HALVES * EGROUPS

                def by_group(t):
                    return t.rearrange("p (g e) -> p g e", e=EPG)

                def against(t, n):
                    shape = [P, n, EPG, EPG]
                    return t.unsqueeze(3).broadcast_to(shape), t.unsqueeze(2).broadcast_to(shape)

                pairs = [route4[:, i, :].rearrange("p (g e j) -> p g e j", e=EPG, j=EPG) for i in range(2)]

                def tri_of(n):
                    return tri.unsqueeze(1).broadcast_to([P, n, EPG, EPG])

                w.next("router_exp", HALVES)
                step(nc.vector.tensor_scalar(r[1], r[0], 1.0, None, ALU.add))
                step(nc.vector.reciprocal(r[2], r[1]))
                affinity, biased, sel = r[2], r[3], r[4]
                step(tt(biased.rearrange("p (a e) -> p a e", a=HALVES),
                        affinity.rearrange("p (a e) -> p a e", a=HALVES),
                        router_b[:].unsqueeze(1).broadcast_to([P, HALVES, EXPERTS]), ALU.add))
                own, other = against(by_group(biased), n_groups)
                nc.vector.tensor_tensor(pairs[0], other, own, ALU.is_gt)
                step(tt(pairs[1], other, own, ALU.is_equal))
                step(tt(pairs[1], pairs[1], tri_of(n_groups), ALU.mult))
                step(tt(pairs[0], pairs[0], pairs[1], ALU.add))
                step(nc.vector.tensor_reduce(by_group(r[5]), pairs[0], AX.X, ALU.add))
                step(nc.vector.tensor_scalar(sel, r[5], TOP_E - 0.5, None, ALU.is_lt))
                step(tt(r[5], sel, biased, ALU.mult))
                step(nc.vector.tensor_reduce(r[6][:, 0:n_groups], by_group(r[5]), AX.X, ALU.add))
                score = r[6][:, 0:n_groups].rearrange("p (a g) -> p a g", a=HALVES)
                top = r[6][:, n_groups:n_groups + HALVES]
                step(nc.vector.tensor_reduce(top, score, AX.X, ALU.max))
                is_top = r[7][:, 0:n_groups].rearrange("p (a g) -> p a g", a=HALVES)
                step(tt(is_top, score, top.unsqueeze(2).broadcast_to([P, HALVES, EGROUPS]), ALU.is_equal))
                few = pairs[0][:, 0:HALVES]
                step(tt(few, against(is_top, HALVES)[1], tri_of(HALVES), ALU.mult))
                earlier = r[7][:, n_groups:2 * n_groups].rearrange("p (a g) -> p a g", a=HALVES)
                step(nc.vector.tensor_reduce(earlier, few, AX.X, ALU.add))
                step(nc.vector.tensor_scalar(earlier, earlier, 0.5, None, ALU.is_lt))
                step(tt(is_top, is_top, earlier, ALU.mult))
                step(tt(by_group(sel), by_group(sel),
                        r[7][:, 0:n_groups].unsqueeze(2).broadcast_to([P, n_groups, EPG]), ALU.mult))
                step(tt(r[5], sel, affinity, ALU.mult))
                total = r[6][:, n_groups:n_groups + HALVES]
                halves = r[5].rearrange("p (a e) -> p a e", a=HALVES)
                step(nc.vector.tensor_reduce(total, halves, AX.X, ALU.add))
                step(nc.vector.reciprocal(r[6][:, 0:HALVES], total))
                tt(r[0].rearrange("p (a e) -> p a e", a=HALVES), halves,
                   r[6][:, 0:HALVES].unsqueeze(2).broadcast_to([P, HALVES, EXPERTS]), ALU.mult)\
                    .then_inc(S["routed"], 1)

            def experts(b, layer):
                base = b + L_MOE
                steps = N_FF + layer * 2 * EXPERTS
                with dve.Fori(0, EXPERTS) as e:
                    for i in range(3):
                        split_lo(base + i, e, PER_EXPERT)
                    for h in range(2):
                        done = steps + h + 1
                        split_lo(base + 3 + 2 * h if h == 0 else base + 4, e, PER_EXPERT)
                        dve.wait_ge(S["slab_used"], count(base + 2 * h + 2, e, PER_EXPERT))
                        dve.wait_ge(S["act_lo"], count(done - 1, e, 2))
                        gate = gates[:, bass.ds(e, 1), :].broadcast_to([P, 2, SEQ])
                        tt(y[:, 1, :, :], bank[2 * h + 1][:].rearrange("p (c t) -> p c t", c=2), gate, ALU.mult)\
                            .then_inc(S["up_gated"], 1)
                        dve.wait_ge(S["up_gated"], count(layer * 2 * EXPERTS + h + 1, e, 2))
                        dve.wait_ge(S["silu_done"], count(done, e, 2))
                        tt(y[:, 1, :, :], y[:, 0, :, :], y[:, 1, :, :], ALU.mult).then_inc(S["act_ready"], 1)
                        if h:
                            split_lo(base + 5, e, PER_EXPERT)
                        dve.wait_ge(S["act_hi"], count(done, e, 2))
                        tt(act_s[:, h, :, SEQ:2 * SEQ], y[:, 1, :, :], act_s[:, h, :, 0:SEQ].bitcast(F32),
                           ALU.subtract).then_inc(S["act_lo"], 1)

            dve.wait_ge(S["x_in"], 16 * HALVES)
            mean_square([(0, HALVES, D)], EPS_RMS, HALVES)
            w.next("rstd_ready")
            for i in range(HALVES):
                nc.vector.tensor_scalar(xn[:, i, :], x[:, i, :], stat[:, 2, i:i + 1], None, ALU.mult)\
                    .then_inc(S["normed"], 1)
            w.next("params_copied", 2)
            feature_major(DC, lambda c: V_G1 + c)
            splits_to(S_QK + 5)
            save_half(S_QK + 3, "qk_saved1", [(qk[:, 1, 512 * i:512 * (i + 1)], bank[2 + i][:]) for i in range(2)])
            w.next("qk_saved0", 2)
            w.next("qk_saved1", 2)
            qk_heads = qk.rearrange("p a (h d) -> p (a h) d", d=HD)
            sq = xn[:].rearrange("p a (h d) -> p (a h) d", d=HD)
            n_rows = HALVES * 2 * HEADS
            tt(sq, qk_heads, qk_heads, ALU.mult).then_inc(S["qk_squared"], 1)
            splits_to(S_VU + 2)
            w.next("qk_squared")
            nc.vector.tensor_reduce(stat[:, 0, 0:n_rows], sq, AX.X, ALU.add).then_inc(S["qk_summed"], 1)
            w.next("qk_summed")
            mean_square([(0, n_rows, HD)], EPS_RMS, 0)
            splits_to(S_VU + 5)
            save_half(S_VU + 3, "vu_saved1", [(vu[:, 1, 512 * i:512 * (i + 1)], bank[6 + i][:]) for i in range(2)])
            splits_to(S_GATE + 2)
            w.next("rstd_ready")
            tt(qk_heads, qk_heads, stat[:, 2, 0:n_rows].unsqueeze(2).broadcast_to([P, n_rows, HD]), ALU.mult)\
                .then_inc(S["qk_scaled"], 1)
            splits_to(S_GATE + 3)
            w.next("qk_scaled")
            for i in range(2):
                part = qk[:, :, WIDTH * i:WIDTH * (i + 1)].rearrange("p a (h d) -> p a h d", d=HD)
                gain = head_gain[:, i, :].unsqueeze(1).unsqueeze(1).broadcast_to([P, HALVES, HEADS, HD])
                tt(part, part, gain, ALU.mult).then_inc(S["qk_gained"], 1)
            splits_to(S_GATE + 4)
            w.next("qk_gained", 2)
            four = qk.rearrange("p a (h d) -> p a h d", d=HD)
            shape = [P, HALVES, 2 * HEADS, ROPE1]

            def tmp1(i):
                n = HALVES * 2 * HEADS * ROPE1
                flat = xn[:].rearrange("p a n -> p (a n)")[:, i * n:(i + 1) * n]
                return flat.rearrange("p (a h d) -> p a h d", a=HALVES, d=ROPE1)

            rotate(four[:, :, :, 0:ROPE1], four[:, :, :, ROPE1:2 * ROPE1], cos1, sin1, tmp1, shape)
            splits_to(S_GATE + 9)
            w.next("mixed_hi", GROUPS)
            for g in range(GROUPS):
                nc.vector.scalar_tensor_tensor(
                    out=xs[:, 4 + g, SEQ:2 * SEQ], in0=bank[6 + g // 2][:, (g % 2) * SEQ:(g % 2 + 1) * SEQ],
                    scalar=vec[:, V_PS + g:V_PS + g + 1], in1=xs[:, 4 + g, 0:SEQ].bitcast(F32),
                    op0=ALU.mult, op1=ALU.subtract).then_inc(S["mixed_lo"], 1)
            splits_to(S_BA + 2)
            attention(SC1, 0)
            feature_major(4)
            splits_to(S_BP + 1)
            dve.wait_ge(S["gates_saved"], 2 * 8)
            for i in range(4):
                dve.wait_ge(S["slab_used"], S_BA + i // 2 + 1)
                tt(mix[:, 2 * i:2 * i + 2, :], bank[i][:].rearrange("p (c t) -> p c t", c=2),
                   gates[:, 2 * i:2 * i + 2, :], ALU.mult).then_inc(S["a_gated"], 1)
            for i in range(4):
                dve.wait_ge(S["slab_used"], S_BP + i // 2 + 1)
                part = gates[:, DC + 2 * i:DC + 2 * i + 2, :]
                tt(part, bank[4 + i][:].rearrange("p (c t) -> p c t", c=2), part, ALU.mult)\
                    .then_inc(S["b_gated"], 1)
            w.next("a_gated", 4)
            w.next("b_gated", 4)
            tt(mix, mix, gates[:, DC:2 * DC, :], ALU.add).then_inc(S["ab_summed"], 1)
            w.next("mixed_hi")
            tt(xs[:, :, SEQ:2 * SEQ], mix, xs[:, :, 0:SEQ].bitcast(F32), ALU.subtract).then_inc(S["mixed_lo"], 1)
            splits_to(S_OUT + 3)

            def add_to_x(first):
                for i in range(4):
                    part = x[:, i // 2, 512 * (i % 2):512 * (i % 2 + 1)]
                    tt(part, part, bank[first + i][:], ALU.add).then_inc(S["x_updated"], 1)
                w.next("x_updated", 4)

            dve.wait_ge(S["slab_used"], S_OUT + 4)
            add_to_x(0)
            mean_square([(0, HALVES, D)], EPS_RMS, HALVES)
            w.next("rstd_ready")
            for i in range(HALVES):
                nc.vector.tensor_scalar(xn[:, i, :], x[:, i, :], stat[:, 2, i:i + 1], None, ALU.mult)\
                    .then_inc(S["normed"], 1)
            splits_to(S_FFN)
            feature_major(DC, lambda c: V_G2 + c)

            def ffn_step(n, par, j, jj=None):
                first = jj is None
                split_lo(n + 1, jj, 6)
                if not first:
                    split_lo(n + 2, jj, 6)
                for side, name in ((0, "g"), (1, "v")):
                    if side and not first:
                        split_lo(n + 3, jj, 6)
                    dve.wait_ge(S["tap2_" + name], j * 2 + 2)
                    for t, done in ((1, "tap1_"), (0, "taps_")):
                        back = 2 - t
                        if t == 0:
                            dve.wait_ge(S["tap1_" + name], j * 2 + 2)
                        for c in range(2):
                            dst = y[:, side, c, back:SEQ]
                            nc.vector.scalar_tensor_tensor(
                                out=dst, in0=bank[side][:, c * SEQ:(c + 1) * SEQ - back],
                                scalar=conv[:, t, bass.ds(j * 2 + side * FFC + c, 1)], in1=dst,
                                op0=ALU.mult, op1=ALU.add).then_inc(S[done + name], 1)
                dve.wait_ge(S["silu_done"], j + 1)
                dve.wait_ge(S["taps_v"], j * 2 + 2)
                tt(y[:, 1, :, :], y[:, 0, :, :], y[:, 1, :, :], ALU.mult).then_inc(S["act_ready"], 1)
                dve.wait_ge(S["act_hi"], j + 1)
                tt(act_s[:, par, :, SEQ:2 * SEQ], y[:, 1, :, :], act_s[:, par, :, 0:SEQ].bitcast(F32), ALU.subtract)\
                    .then_inc(S["act_lo"], 1)

            ffn_step(S_FFN, 0, 0)
            split_lo(S_FFN_LOOP)
            with dve.Fori(0, (N_FF - 1) // 2) as jj:
                for s in range(2):
                    ffn_step(S_FFN_LOOP + 3 * s, (1 + s) % 2, jj * 2 + (1 + s), jj)
            split[0] = S_BLOCK2
            w.next("acc_closed")
            add_to_x(4)

            for layer in range(LAYERS):
                b = layer_base(layer)
                feature_major(DC)
                splits_to(b + L_IN + 5)
                save_half(b + L_IN + 3, "in_saved1", [(proj[:, 1, 512 * i:512 * (i + 1)], bank[2 + i][:]) for i in range(2)])
                splits_to(b + L_IN_C + 1)
                save_half(b + L_IN_C, "in_saved1", [(proj[:, 1, D:D + 512], bank[5][:])])
                for i in range(HALVES):
                    nc.vector.tensor_copy(proj[:, i, D + 512:IN2], bank[6 + i][:, 0:IN2 - D - 512])\
                        .then_inc(S["in_saved1"], 1)
                w.next("in_saved1", 5)
                w.next("in_saved0", 3)
                mean_square([(0, 2, Q_LORA), (2, 2, KV_LORA)], EPS_RMS, 2 * HALVES)
                kr = proj[:, :, AT_KR:AT_KR + KR]
                spare4 = spare.rearrange("p (i n) -> p i n", i=4)

                def tmp_k(i):
                    return spare4[:, i, 0:HALVES * ROPE2].rearrange("p (a h d) -> p a h d", a=HALVES, h=1)

                kr4 = kr.unsqueeze(2)
                rotate(kr4[:, :, :, 0:ROPE2], kr4[:, :, :, ROPE2:KR], cos2, sin2, tmp_k, [P, HALVES, 1, ROPE2])
                nc.vector.tensor_scalar(idx_w[:], proj[:, :, AT_IW:IN2], IDX_HEADS ** -0.5, None, ALU.mult)\
                    .then_inc(S["idx_weights"], 1)
                w.next("rstd_ready")
                for p_, (at, n) in enumerate(((0, Q_LORA), (AT_KVA, KV_LORA))):
                    for i in range(HALVES):
                        nc.vector.tensor_scalar(xn[:, i, at:at + n], proj[:, i, at:at + n],
                                                stat[:, 2, 2 * p_ + i:2 * p_ + i + 1], None, ALU.mult)\
                            .then_inc(S["normed"], 1)
                feature_major(QC + KVC, lambda c: V_QA + QC * layer + c if c < QC else V_KVA + KVC * layer + c - QC)
                splits_to(b + L_UV)
                w.next("pads_zero", 2)
                w.next("rope_summed", 2 if layer else 4)
                nc.vector.tensor_copy(k_up[:, :, :, HD:MLA_D], kr.unsqueeze(2).broadcast_to([P, HALVES, HEADS, KR]))\
                    .then_inc(S["kr_spread"], 1)
                for i in range(2):
                    save_half(b + L_QUP + i, "qup_saved1",
                              [(q_up[:, 1, 4 * i:4 * i + 4, 0:MLA_D],
                                bank[2 * i + 1][:, 0:4 * MLA_D].rearrange("p (h d) -> p h d", h=4))])
                w.next("qup_saved0", 2)
                w.next("qup_saved1", 2)

                def tmp_q(i):
                    return spare4[:, i, :].rearrange("p (a h d) -> p a h d", a=HALVES, h=HEADS)

                rotate(q_up[:, :, :, HD:HD + ROPE2], q_up[:, :, :, HD + ROPE2:MLA_D], cos2, sin2, tmp_q,
                       [P, HALVES, HEADS, ROPE2])
                w.skip("rope_summed", 2)
                save_half(b + L_UK, "uk_saved1",
                          [(k_up[:, 1, :, 0:HD], bank[5][:].rearrange("p (h d) -> p h d", h=HEADS))])
                save_half(b + L_UV, "uv_saved1", [(value[:, 1, :], bank[7][:])])
                splits_to(b + L_O + 2)
                for i in range(4):
                    w.next("turned_a", 2)
                    nc.vector.tensor_copy(k_t[:, 2 * i:2 * i + 2, :], bank[7][:].rearrange("p (c t) -> p c t", c=2))\
                        .then_inc(S["copied_k"], 1)
                attention(SC_MLA, 0)
                for i in range(3):
                    w.next("turned_b", 2)
                    nc.vector.tensor_copy(sparse_t[:, 4 * i + 2:4 * i + 4, :], bank[7][:].rearrange("p (c t) -> p c t", c=2))\
                        .then_inc(S["copied_odd"], 1)

                w.next("idx_weights")
                score = sel_score
                for i in range(HALVES * IDX_HEADS):
                    half, h = divmod(i, IDX_HEADS)
                    keys = P * (half + 1)
                    dst = score[:, half, 0:keys]
                    w.next("idx_relu")
                    weight = idx_w[:, half, h:h + 1]
                    if h == 0:
                        nc.vector.tensor_scalar(dst, logit[:, i % 2, 0:keys], weight, None, ALU.mult)\
                            .then_inc(S["idx_added"], 1)
                    else:
                        nc.vector.scalar_tensor_tensor(out=dst, in0=logit[:, i % 2, 0:keys], scalar=weight, in1=dst,
                                                       op0=ALU.mult, op1=ALU.add).then_inc(S["idx_added"], 1)
                    w.next("idx_added")
                for half in range(HALVES):
                    keys = P * (half + 1)
                    dst = score[:, half, 0:keys]
                    tt(dst, dst, mask[:, half, 0:keys], ALU.add).then_inc(S["idx_masked"], 1)
                    w.next("idx_masked")
                    for _ in range(KEEP // 8):
                        nc.vector.max(best[:], dst).then_inc(S["topk_step"], 1)
                        w.next("topk_step")
                        nc.vector.match_replace(dst, best[:], dst, TAKEN).then_inc(S["topk_step"], 1)
                        w.next("topk_step")
                    nc.vector.tensor_scalar(dst, dst, TAKEN * 0.5, -NEG, ALU.is_le, ALU.mult).then_inc(S["sel_step"], 1)
                    w.next("sel_step")
                    nc.vector.scalar_tensor_tensor(out=dst, in0=dst, scalar=NEG, in1=mask[:, half, 0:keys],
                                                   op0=ALU.add, op1=ALU.add).then_inc(S["sel_step"], 1)
                    w.next("sel_step")
                attention(SC_DSA, WIDTH, sparse=True)
                feature_major(DC)
                splits_to(b + L_O + 3)
                dve.wait_ge(S["slab_used"], b + L_O + 4)
                for norm in range(2):
                    if norm:
                        feature_major(DC)
                        router()
                        for i in range(EXPERTS // 4):
                            w.next("gates_spread", 2)
                            nc.vector.tensor_copy(gates[:, 4 * i + 2:4 * i + 4, :],
                                                  bank[0][:].rearrange("p (c t) -> p c t", c=2))\
                                .then_inc(S["gates_kept1"], 1)
                        dve.wait_ge(S["gates_kept0"], EXPERTS // 4 * (layer + 1))
                        dve.wait_ge(S["gates_kept1"], EXPERTS // 4 * (layer + 1))
                        experts(b, layer)
                        w.next("acc_closed")
                    for i in range(4):
                        part = x[:, i // 2, 512 * (i % 2):512 * (i % 2 + 1)]
                        nc.vector.scalar_tensor_tensor(out=part, in0=part, scalar=ALPHA,
                                                       in1=bank[4 * norm + i][:], op0=ALU.mult, op1=ALU.add,
                                                       accum_out=stat[:, 0, i:i + 1]).then_inc(S["ln_added"], 1)
                    w.next("ln_added", 4)
                    tt(stat[:, 1, 0:2], stat[:, 0, 0:4:2], stat[:, 0, 1:4:2], ALU.add).then_inc(S["ln_mean_step"], 1)
                    w.next("ln_mean_step")
                    nc.vector.tensor_scalar(stat[:, 2, 0:2], stat[:, 1, 0:2], 1.0 / D, None, ALU.mult)\
                        .then_inc(S["ln_mean_step"], 1)
                    w.next("ln_mean_step")
                    for i in range(HALVES):
                        nc.vector.tensor_scalar(x[:, i, :], x[:, i, :], stat[:, 2, i:i + 1], None, ALU.subtract)\
                            .then_inc(S["ln_centred"], 1)
                    mean_square([(0, HALVES, D)], EPS_LN, HALVES)
                    w.next("rstd_ready")
                    w.next("ln_centred", HALVES)
                    w.next("ln_in", 32)
                    for i in range(HALVES):
                        nc.vector.scalar_tensor_tensor(out=x[:, i, :], in0=x[:, i, :], scalar=stat[:, 2, i:i + 1],
                                                       in1=ln_gb[:, 0, :], op0=ALU.mult, op1=ALU.mult)\
                            .then_inc(S["ln_scaled"], 1)
                    w.next("ln_scaled", HALVES)
                    for i in range(HALVES):
                        tt(x[:, i, :], x[:, i, :], ln_gb[:, 1, :], ALU.add).then_inc(S["ln_done"], 1)
                    w.next("ln_done", HALVES)
                split[0] = b + PER_LAYER
        @block.tensor
        def _(pe):
            w = Waits(pe, S)
            mm = nc.tensor.matmul

            def turn(dst, src):
                return nc.tensor.transpose(dst, src, ident[0:src.shape[0], 0:src.shape[0]])

            fm = [0]

            def feature_major(chunks, src):
                for b in range(0, chunks, 2):
                    w.upto("fm_lo", fm[0] - 1)
                    for c in range(b, min(b + 2, chunks)):
                        for half in range(HALVES):
                            at = (c - b) * SEQ + half * P
                            ins = turn(bank[6 + fm[0] % 2][:, at:at + P], src(c, half))
                    ins.then_inc(S["fm_turned"], 1)
                    fm[0] += 1

            def fm_ready():
                w.upto("fm_lo", fm[0])

            def products(out_, lhs_hi, lhs_lo, rhs_hi, rhs_lo, first, last):
                mm(out_, lhs_hi, rhs_hi, start=first, stop=False)
                mm(out_, lhs_lo, rhs_hi, start=False, stop=False)
                return mm(out_, lhs_hi, rhs_lo, start=False, stop=last)

            def token_major(n, slabs, k_per, widths, banks, chunk=0, lhs=xs, j=None, per=0, open_=True, close=True,
                            ready=None):
                for s in range(slabs):
                    pe.wait_ge(S["lo_done"], count(n + s + 1, j, per))
                    wh, wl = (slab_of(t, n + s, k_per)(sum(widths)) for t in (hi, lo))
                    for k in range(k_per):
                        kk = s * k_per + k
                        first, last = open_ and kk == 0, close and kk == slabs * k_per - 1
                        for half in range(HALVES):
                            at = half * P
                            a_hi = lhs[:, chunk + kk, at:at + P]
                            a_lo = lhs[:, chunk + kk, SEQ + at:SEQ + at + P]
                            for i, width in enumerate(widths):
                                c0 = sum(widths[:i])
                                ins = products(banks[half][i][:, 0:width], a_hi, a_lo, wh[:, k, c0:c0 + width],
                                               wl[:, k, c0:c0 + width], first, last)
                    ins.then_inc(S["slab_used"], 1)

            def feature_slab(n, k_chunks, columns, banks, chunk=0, j=None, per=0):
                pe.wait_ge(S["lo_done"], count(n + 1, j, per))
                wh, wl = (slab_of(t, n, k_chunks)(columns) for t in (hi, lo))
                for c in range(columns // P):
                    dst = banks[c // 2][:, (c % 2) * SEQ:(c % 2 + 1) * SEQ]
                    for k in range(k_chunks):
                        x_hi, x_lo = xs[:, chunk + k, 0:SEQ], xs[:, chunk + k, SEQ:2 * SEQ]
                        col = slice(c * P, (c + 1) * P)
                        mm(dst, wh[:, k, col], x_hi, start=k == 0, stop=False)
                        mm(dst, wh[:, k, col], x_lo, start=False, stop=False)
                        ins = mm(dst, wl[:, k, col], x_hi, start=False, stop=k == k_chunks - 1)
                ins.then_inc(S["slab_used"], 1)

            units = [0]

            def attention(q, k, v):
                base, n = units[0], 2 * HEADS

                def score(i):
                    half, h = divmod(i, HEADS)
                    if i >= 2:
                        pe.wait_ge(S["logits"], base + i - 1)
                    keys = P * (half + 1)
                    mm(bank[i % 2][:, 0:keys], q(h, half), k(h)[:, 0:keys], start=True, stop=True)\
                        .then_inc(S["scores"], 1)

                def flip(i):
                    pe.wait_ge(S["probs"], base + i + 1)
                    if i >= 2:
                        pe.wait_ge(S["probs_turned"], base + i - 1)
                    for c in range(i // HEADS + 1):
                        ins = turn(bank[2 + i % 2][:, c * P:(c + 1) * P], prob[:, i % 2, c * P:(c + 1) * P])
                    ins.then_inc(S["flipped"], 1)

                def weigh(i):
                    half, h = divmod(i, HEADS)
                    pe.wait_ge(S["probs_turned"], base + i + 1)
                    for c in range(half + 1):
                        ins = mm(bank[4 + half][:, h * HD:(h + 1) * HD], prob_t[:, i % 2, c, :], v(h, c),
                                 start=c == 0, stop=c == half)
                    ins.then_inc(S["weighted"], 1)

                for i in range(n + 2):
                    if i < n:
                        score(i)
                    if 1 <= i <= n:
                        flip(i - 1)
                    if i >= 2:
                        weigh(i - 2)
                units[0] += n

            halves4 = [[bank[0], bank[1]], [bank[2], bank[3]]]
            acc = [[bank[4], bank[5]], [bank[6], bank[7]]]

            def open_acc():
                for half in range(HALVES):
                    for i in range(2):
                        mm(acc[half][i][:], zeros[:, 0:P], zeros[:], start=True, stop=False)

            def close_acc():
                for half in range(HALVES):
                    for i in range(2):
                        ins = mm(acc[half][i][:], zeros[:, 0:P], zeros[:], start=False, stop=True)
                ins.then_inc(S["acc_closed"], 1)

            w.next("params_in", 16 * N_PARAMS)
            turn(bank[0][:, 0:V_N], rows)
            for t in range(TAPS + 1):
                ins = turn(bank[1][:, t * 2 * FFC:(t + 1) * 2 * FFC], conv_rows[:, t, :])
            ins.then_inc(S["turned_params"], 1)
            w.next("normed", HALVES)
            feature_major(DC, lambda c, half: xn[:, half, c * P:(c + 1) * P])
            fm_ready()
            w.next("params_copied", 2)
            token_major(S_QK, 4, 2, [512, 512], halves4)
            token_major(S_VU, 4, 2, [512, 512], acc)
            for i in range(8):
                if i == 0:
                    w.next("qk_saved0", 2)
                    w.next("qk_saved1", 2)
                if i >= 4:
                    pe.wait_ge(S["gates_saved"], 2 * (i - 3))
                feature_slab(S_GATE + i, DC, 256, [bank[i % 4]])
            w.next("vu_saved0", 2)
            w.next("vu_saved1", 2)
            for g in range(GROUPS):
                dst = bank[4 + g // 2][:, (g % 2) * SEQ:(g % 2 + 1) * SEQ]
                for half in range(HALVES):
                    ins = mm(dst, vu[:, half, WIDTH + g * P:WIDTH + (g + 1) * P], band[:, g, half, :],
                             start=half == 0, stop=half == HALVES - 1)
            ins.then_inc(S["pooled_summed"], 1)
            w.next("pooled_copied", 2)
            for g in range(GROUPS):
                ins = mm(bank[6 + g // 2][:, (g % 2) * SEQ:(g % 2 + 1) * SEQ], w_pool[:, g, :], pooled[:, g, :],
                         start=True, stop=True)
            ins.then_inc(S["mixed_summed"], 1)
            w.next("rope_summed", 2)
            w.next("gates_saved", 2 * 8)
            for b in range(4):
                w.upto("pairs_copied", (0, 0, 1, 2)[b])
                for c in range(2):
                    for half in range(HALVES):
                        at = c * SEQ + half * P
                        col = (2 * b + c) * P
                        ins = turn(bank[b % 2][:, at:at + P], qk[:, half, col:col + P])
                ins.then_inc(S["pairs_turned"], 1)
            w.next("pairs_copied", 6)
            attention(lambda h, half: q_t[:, h // 2, half * P:(half + 1) * P],
                      lambda h: k_t[:, h, :],
                      lambda h, c: vu[:, c, h * HD:(h + 1) * HD])
            w.next("mixed_lo", GROUPS)
            w.next("heads_saved", 2)
            feature_major(4, lambda c, half: xn[:, half, c * P:(c + 1) * P])
            fm_ready()
            for i in range(2):
                feature_slab(S_BA + i, 4, 512, bank[2 * i:2 * i + 2])
            for i in range(2):
                feature_slab(S_BP + i, 4, 512, bank[4 + 2 * i:6 + 2 * i], chunk=4)
            w.next("mixed_lo")
            token_major(S_OUT, 4, 2, [512, 512], halves4)
            w.next("normed", HALVES)
            feature_major(DC, lambda c, half: xn[:, half, c * P:(c + 1) * P])
            fm_ready()
            pe.wait_ge(S["fills_set"], 3)
            open_acc()

            def down(n, par, j, jj=None):
                pe.wait_ge(S["act_lo"], j)
                token_major(n, 1, 2, [512, 512], acc, lhs=act_s[:, par], j=jj, per=6, open_=False, close=False)

            feature_slab(S_FFN, DC, 256, [bank[0]])
            feature_slab(S_FFN + 1, DC, 256, [bank[1]])
            with pe.Fori(0, (N_FF - 1) // 2) as jj:
                for s in range(2):
                    n, j = S_FFN_LOOP + 3 * s, jj * 2 + (1 + s)
                    pe.wait_ge(S["taps_g"], j * 2)
                    feature_slab(n, DC, 256, [bank[0]], j=jj, per=6)
                    pe.wait_ge(S["taps_v"], j * 2)
                    feature_slab(n + 1, DC, 256, [bank[1]], j=jj, per=6)
                    down(n + 2, s, j, jj)
            down(S_BLOCK2 - 1, 0, N_FF)
            close_acc()
            w.next("x_updated", 8)

            for layer in range(LAYERS):
                b = layer_base(layer)
                feature_major(DC, lambda c, half: x[:, half, c * P:(c + 1) * P])
                fm_ready()
                token_major(b + L_IN, 4, 2, [512, 512], halves4)
                token_major(b + L_IN_B, 2, 4, [512], [[bank[4]], [bank[5]]])
                token_major(b + L_IN_C, 1, DC, [IN2 - D - 512], [[bank[6]], [bank[7]]])
                w.next("normed", 2 * HALVES)
                feature_major(QC + KVC, lambda c, half: xn[:, half, c * P:(c + 1) * P])
                fm_ready()
                for i in range(2):
                    token_major(b + L_QUP + i, 1, QC, [4 * MLA_D], [[bank[2 * i]], [bank[2 * i + 1]]])
                token_major(b + L_UK, 1, KVC, [WIDTH], [[bank[4]], [bank[5]]], chunk=QC)
                token_major(b + L_UV, 1, KVC, [WIDTH], [[bank[6]], [bank[7]]], chunk=QC)
                pe.wait_ge(S["rope_summed"], 2 + 4 * (layer + 1))
                w.next("kr_spread")
                for name in ("uk_saved0", "uk_saved1", "uv_saved0", "uv_saved1"):
                    w.next(name)
                w.next("pads_zero", 2)
                for i in range(4):
                    for src, to, copied in ((q_up, bank[6], "copied_q"), (k_up, bank[7], "copied_k")):
                        w.upto(copied, 4 * layer + i)
                        for c in range(2):
                            for half in range(HALVES):
                                at = c * SEQ + half * P
                                ins = turn(to[:, at:at + P], src[:, half, 2 * i + c, :])
                        ins.then_inc(S["turned_a"], 1)
                w.next("copied_q", 4)
                w.next("copied_k", 4)
                attention(lambda h, half: q_t[:, h, half * P:(half + 1) * P],
                          lambda h: k_t[:, h, :],
                          lambda h, c: value[:, c, h * HD:(h + 1) * HD])

                def sparse_src(c, half):
                    if c < T_DK:
                        return proj[:, half, AT_DQ + c * P:AT_DQ + (c + 1) * P]
                    if c < T_IQ:
                        return stage[:, half, c - T_DK, :]
                    return proj[:, half, AT_IQ + (c - T_IQ) * P:AT_IQ + (c - T_IQ + 1) * P]

                w.next("staged", 6)
                for i in range(6):
                    w.upto(("copied_even", "copied_odd")[i % 2], 3 * layer + i // 2)
                    for c in range(2):
                        for half in range(HALVES):
                            at = c * SEQ + half * P
                            ins = turn(bank[6 + i % 2][:, at:at + P], sparse_src(2 * i + c, half))
                    ins.then_inc(S["turned_b"], 1)
                w.next("copied_even", 3)
                w.next("copied_odd", 3)
                n_idx = HALVES * IDX_HEADS
                for i in range(n_idx):
                    half, h = divmod(i, IDX_HEADS)
                    keys = P * (half + 1)
                    if i >= 2:
                        pe.wait_ge(S["idx_relu"], n_idx * layer + i - 1)
                    mm(bank[i % 2][:, 0:keys], sparse_t[:, T_IQ + h // 4, half * P:(half + 1) * P],
                       sparse_t[:, T_IK + h % 4, 0:keys], start=True, stop=True).then_inc(S["idx_scores"], 1)
                w.next("idx_relu", n_idx)
                w.next("heads_saved", 2)
                attention(lambda h, half: sparse_t[:, T_DQ + h // 2, half * P:(half + 1) * P],
                          lambda h: sparse_t[:, T_DK + h % 2, :],
                          lambda h, c: proj[:, c, AT_DV:AT_DV + HD])
                w.next("heads_saved", 2)
                feature_major(DC, lambda c, half: xn[:, half, c * P:(c + 1) * P])
                fm_ready()
                token_major(b + L_O, 4, 2, [512, 512], halves4)
                pe.wait_ge(S["ln_done"], 2 * HALVES * layer + HALVES)
                feature_major(DC, lambda c, half: x[:, half, c * P:(c + 1) * P])
                fm_ready()
                for half in range(HALVES):
                    for k in range(DC):
                        for part in range(2):
                            at = part * SEQ + half * P
                            ins = mm(bank[half][:, 0:EXPERTS], xs[:, k, at:at + P].bitcast(F32), router_w[:, k, :],
                                     start=k == 0 and part == 0, stop=k == DC - 1 and part == 1)
                ins.then_inc(S["router_logits"], 1)
                w.next("routed")
                for i in range(EXPERTS // 2):
                    w.upto(("gates_kept0", "gates_kept1")[i % 2], EXPERTS // 4 * layer + i // 2)
                    for c in range(2):
                        for half in range(HALVES):
                            at = c * SEQ + half * P
                            col = EXPERTS * half + 2 * i + c
                            ins = mm(bank[(3, 0)[i % 2]][:, at:at + P],
                                     route[:, 0, col:col + 1].broadcast_to([P, P]), ident, start=True, stop=True)
                    ins.then_inc(S["gates_spread"], 1)
                w.next("gates_kept0", EXPERTS // 4)
                w.next("gates_kept1", EXPERTS // 4)
                open_acc()
                base = b + L_MOE
                steps = N_FF + layer * 2 * EXPERTS
                with pe.Fori(0, EXPERTS) as e:
                    for h in range(2):
                        pe.wait_ge(S["silu_done"], count(steps + h - 1, e, 2))
                        feature_slab(base + 2 * h, DC, 256, [bank[2 * h]], j=e, per=PER_EXPERT)
                        pe.wait_ge(S["act_ready"], count(steps + h - 1, e, 2))
                        feature_slab(base + 2 * h + 1, DC, 256, [bank[2 * h + 1]], j=e, per=PER_EXPERT)
                    for h in range(2):
                        pe.wait_ge(S["act_lo"], count(steps + h + 1, e, 2))
                        token_major(base + 4 + h, 1, 2, [512, 512], acc, lhs=act_s[:, h], j=e, per=PER_EXPERT,
                                    open_=False, close=False)
                close_acc()
                pe.wait_ge(S["ln_done"], 2 * HALVES * (layer + 1))


def kernel(**inputs):
    import numpy as _np
    import concourse.bacc as _bacc
    from concourse import mybir as _mybir
    from concourse.bass_utils import run_bass_kernel_spmd as _run

    nc = _bacc.Bacc("TRN2", target_bir_lowering=False, num_devices=1)
    arrays = {name: _np.ascontiguousarray(value) for name, value in inputs.items()}
    arrays["constants"] = constants()
    aps = {name: nc.dram_tensor(f"in_{name}", a.shape, _mybir.dt.from_np(a.dtype), kind="ExternalInput").ap()
           for name, a in arrays.items()}
    out = nc.dram_tensor("out", (1, SEQ, D), F32, kind="ExternalOutput").ap()
    build(nc, aps, out)
    r = _run(nc, [{f"in_{name}": a for name, a in arrays.items()}], core_ids=[0])
    return r.results[0]["out"]
```

```python
from contextlib import ExitStack

import numpy as np

import concourse.bass as bass
from concourse import mybir

F32 = mybir.dt.float32
F32R = mybir.dt.float32r
BF16 = mybir.dt.bfloat16
ACT = mybir.ActivationFunctionType
ALU = mybir.AluOpType
AX = mybir.AxisListType

P = 128
SEQ, D = 256, 1024
HALVES = SEQ // P
DC = D // P
HEADS, HD = 8, 64
WIDTH = HEADS * HD
EPS_RMS, EPS_LN = 1e-6, 1e-5
NEG = -1e30

POOL_WINDOWS = (2, 4, 8, 16)
GROUPS = len(POOL_WINDOWS)
ROPE1 = HD // 4 // 2
FF = 2816
FFC = FF // P
TAPS = 3

LAYERS = 2
Q_LORA, KV_LORA, KR = 384, 256, 32
QC, KVC = Q_LORA // P, KV_LORA // P
ROPE2 = KR // 2
MLA_D = HD + KR
IDX_HEADS, IDX_D = 8, 32
KEEP = SEQ // 4
AT_KVA = Q_LORA
AT_KR = AT_KVA + KV_LORA
AT_DQ = AT_KR + KR
AT_DK = AT_DQ + WIDTH
AT_DV = AT_DK + HD
AT_IQ = AT_DV + HD
AT_IK = AT_IQ + IDX_HEADS * IDX_D
AT_IW = AT_IK + IDX_D
IN2 = AT_IW + IDX_HEADS
EXPERTS, EGROUPS, EPG, TOP_E = 16, 4, 4, 2
SLOTS = 64
ELSEWHERE = 4096.0
FFE = 512
ALPHA = (2.0 * LAYERS) ** 0.25
SLOPES = [2.0 ** (-8.0 * h / HEADS) for h in range(1, HEADS + 1)]
SC1 = HD ** -0.5
SC_MLA = MLA_D ** -0.5
SC_DSA = HD ** -0.5
N_PARAMS = 15
TAKEN = -3e38

RING = 3
SLAB = 2048

S_QK, S_VU, S_GATE, S_BA, S_BP, S_OUT = 0, 4, 8, 16, 18, 20
S_FFN = 24
S_FFN_LOOP = S_FFN + 2
N_FF = FFC // 2
S_BLOCK2 = S_FFN + 3 * N_FF
L_IN, L_IN_B, L_IN_C, L_QUP, L_UK, L_UV, L_O, L_MOE = 0, 4, 6, 7, 9, 10, 11, 15
PER_EXPERT = 6
PER_ROUND = PER_EXPERT * EXPERTS
PER_LAYER = L_MOE + PER_ROUND
S_SECOND = S_BLOCK2 + PER_LAYER
S_END = S_BLOCK2 + LAYERS * PER_LAYER

C_ID = 0
C_MASK = C_ID + P
C_DIST = C_MASK + HALVES * SEQ
C_COS1 = C_DIST + HALVES * SEQ
C_SIN1 = C_COS1 + HALVES * ROPE1
C_COS2 = C_SIN1 + HALVES * ROPE1
C_SIN2 = C_COS2 + HALVES * ROPE2
C_TRI = C_SIN2 + HALVES * ROPE2
C_BEFORE = C_TRI + EPG * EPG
C_ONE = C_BEFORE + P
C_IOTA = C_ONE + 1
C_FULL = C_IOTA + SLOTS
C_KEPT = C_FULL + SEQ // SLOTS - 1
C_BAND = C_KEPT
C_N = C_BAND + GROUPS * HALVES * SEQ

V_G1 = 0
V_BG = V_G1 + DC
V_G2 = V_BG + 2 * DC
V_PS = V_G2 + DC
V_QA = V_PS + GROUPS
V_KVA = V_QA + LAYERS * QC
V_N = V_KVA + LAYERS * KVC

SEMAPHORES = """x_in params_in ln_in out_stored
 raw_in0 raw_in1 raw_in2 hi_done lo_done slab_used
 raw_in0_b raw_in1_b raw_in2_b hi_done_b lo_done_b slab_used_b
 fills_set turned_params params_copied
 squares_summed mean_square rstd_ready normed
 fm_turned fm_hi fm_lo
 qk_saved0 qk_saved1 vu_saved0 vu_saved1 gates_saved
 qk_squared qk_summed qk_scaled qk_gained rope_products rope_summed
 pairs_turned pairs_copied pooled_summed pooled_copied mixed_summed mixed_hi mixed_lo
 a_gated b_gated ab_summed x_updated
 scores logits bias_ready probs flipped probs_turned weighted sums_inverted heads_saved
 acc_closed tap2_g tap2_v tap1_g tap1_v taps_g taps_v silu_done act_ready act_hi act_lo
 in_saved0 in_saved1 qup_saved0 qup_saved1 uk_saved0 uk_saved1 uv_saved0 uv_saved1 pads_zero
 kr_spread turned_a copied_q copied_k stage_zero staged turned_b copied_even copied_odd
 idx_scores idx_relu idx_weights idx_added idx_masked topk_step sel_step
 ln_added ln_mean_step ln_centred ln_scaled ln_done
 router_logits router_exp router_step routed counted places_step rounds_known rows_hi rows_lo""".split()
SEMAPHORES += [f"{name}_{layer}" for layer in range(LAYERS) for name in """
 one_hot places_moved gathered xg_hi xg_lo gate_low gate_added silu_done up_low up_added act_gated
 act_turned act_hi act_lo dispatched dispatch_copied expert_out_a expert_out_v scattered""".split()]


def constants():
    c = np.zeros((P, C_N), np.float32)
    c[:, C_ID:C_ID + P] = np.eye(P)
    t = np.arange(SEQ)
    for half in range(HALVES):
        q = half * P + np.arange(P)
        at = half * SEQ
        c[:, C_MASK + at:C_MASK + at + SEQ] = np.where(t[None, :] <= q[:, None], 0.0, NEG)
        c[:, C_DIST + at:C_DIST + at + SEQ] = t[None, :] - q[:, None]
        for g, w in enumerate(POOL_WINDOWS):
            s = q
            inside = (s[:, None] <= t[None, :]) & (s[:, None] > t[None, :] - w)
            band = inside / np.minimum(t + 1.0, w)[None, :] - (s[:, None] == t[None, :])
            at = C_BAND + (g * HALVES + half) * SEQ
            c[:, at:at + SEQ] = band
        for n, theta, ccos, csin in ((ROPE1, 500000.0, C_COS1, C_SIN1), (ROPE2, 10000.0, C_COS2, C_SIN2)):
            inv = (np.float32(theta) ** (-np.arange(n, dtype=np.float32) / np.float32(n))).astype(np.float32)
            ang = q.astype(np.float32)[:, None] * inv[None, :]
            c[:, ccos + half * n:ccos + (half + 1) * n] = np.cos(ang)
            c[:, csin + half * n:csin + (half + 1) * n] = np.sin(ang)
    for e in range(EPG):
        for j in range(e):
            c[:, C_TRI + e * EPG + j] = 1.0
    c[:, C_BEFORE:C_ONE] = np.arange(P)[:, None] < np.arange(P)[None, :]
    c[:, C_ONE] = 1.0
    c[:, C_IOTA:C_FULL] = np.arange(SLOTS)
    c[:, C_FULL:C_KEPT] = SLOTS * np.arange(1, SEQ // SLOTS)
    return c


class Waits:

    def __init__(self, eng, sems):
        self.eng, self.sems, self.count = eng, sems, {}

    def next(self, name, k=1):
        self.count[name] = self.count.get(name, 0) + k
        self.eng.wait_ge(self.sems[name], self.count[name])

    def skip(self, name, k=1):
        self.count[name] = self.count.get(name, 0) + k

    def upto(self, name, n):
        if n > 0:
            self.eng.wait_ge(self.sems[name], n)


def build(nc, A, out):
    ctx = ExitStack()
    with ctx:
        def sb(name, shape, dt=F32):
            return ctx.enter_context(nc.sbuf_tensor(name, shape, dt))

        S = {name: ctx.enter_context(nc.semaphore(name)) for name in SEMAPHORES}
        bank = [ctx.enter_context(nc.psum_tensor(f"bank{i}", [P, 512], F32)) for i in range(8)]

        const = sb("const", [P, C_KEPT])
        vec = sb("vec", [P, V_N])
        conv = sb("conv", [P, TAPS + 1, 2 * FFC])
        router_w = sb("router_w", [P, DC, EXPERTS])
        router_b = sb("router_b", [P, EXPERTS])
        power = sb("power", [P, HALVES * 2 * HEADS])
        zeros = sb("zeros", [P, P], BF16)

        x = sb("x", [P, HALVES, D])
        xn = sb("xn", [P, HALVES, D])
        xs = sb("xs", [P, DC, 2 * SEQ], F32R)
        raw = sb("raw", [P, RING, SLAB])
        hi = sb("hi", [P, RING, SLAB], F32R)
        lo = sb("lo", [P, RING, SLAB], F32R)
        proj = sb("proj", [P, HALVES, IN2])
        gates = sb("gates", [P, 2 * DC, SEQ])
        wide_a = sb("wide_a", [P, HALVES * D])
        wide_b = sb("wide_b", [P, HALVES * D])
        value = sb("value", [P, HALVES, WIDTH])
        q_t = sb("q_t", [P, HEADS, SEQ])
        k_t = sb("k_t", [P, HEADS, SEQ])
        xg = sb("xg", [P, EPG, DC, 2 * SLOTS], F32R)
        act_t = sb("act_t", [P, FFE // P, 2 * SLOTS], F32R)
        one_hot = sb("one_hot", [P, HALVES, EPG, 2 * SLOTS], F32R)
        slot_gate = sb("slot_gate", [P, 2])
        rounds = sb("rounds", [P, 1], mybir.dt.int32)
        logit = sb("logit", [P, 2, SEQ])
        prob = sb("prob", [P, 2, SEQ])
        prob_t = sb("prob_t", [P, 2, HALVES, P])
        bias_h = sb("bias_h", [P, 2, SEQ])
        row_min = sb("row_min", [P, 2 * HEADS])
        row_sum = sb("row_sum", [P, 2 * HEADS])
        row_inv = sb("row_inv", [P, 2 * HEADS])
        stat = sb("stat", [P, 3, HALVES * 2 * HEADS])
        best = sb("best", [P, 8])
        idx_w = sb("idx_w", [P, HALVES, IDX_HEADS])
        route = sb("route", [P, 8, HALVES * EXPERTS])

        ident = const[:, C_ID:C_ID + P]
        mask = const[:, C_MASK:C_DIST].rearrange("p (a t) -> p a t", a=HALVES)
        dist = const[:, C_DIST:C_COS1].rearrange("p (a t) -> p a t", a=HALVES)
        one = const[:, C_ONE:C_ONE + 1]
        before = const[:, C_BEFORE:C_BEFORE + P]

        def table(at, n):
            return const[:, at:at + HALVES * n].rearrange("p (a n) -> p a n", a=HALVES)

        cos1, sin1 = table(C_COS1, ROPE1), table(C_SIN1, ROPE1)
        cos2, sin2 = table(C_COS2, ROPE2), table(C_SIN2, ROPE2)
        tri = const[:, C_TRI:C_BEFORE].rearrange("p (e j) -> p e j", e=EPG)

        rows = gates[0:V_N, 0, 0:P]
        conv_rows = gates[0:2 * FFC, 2:4, :].rearrange("c a (b p) -> c (a b) p", p=P)
        qk = proj[:].rearrange("p a n -> p (a n)")[:, 0:HALVES * D].rearrange("p (a n) -> p a n", a=HALVES)
        band = wide_b[:].rearrange("p (g a t) -> p g a t", g=GROUPS, a=HALVES)
        head_gain = prob_t[:, 0, 0, :].rearrange("p (i d) -> p i d", i=2)
        w_pool = q_t[:, 0:2, :].rearrange("p a (b d) -> p (a b) d", d=P)
        act_s = xg[:].rearrange("p e c s -> p (e c s)")[:, 0:8 * SEQ]\
            .rearrange("p (b c s) -> p b c s", b=2, c=2)
        vu = wide_a[:].rearrange("p (a n) -> p a n", a=HALVES)
        mix = wide_b[:].rearrange("p (c t) -> p c t", c=DC)
        pooled = value[:].rearrange("p a n -> p (a n)").rearrange("p (g t) -> p g t", g=GROUPS)
        q_up = wide_a[:].rearrange("p (a h d) -> p a h d", a=HALVES, h=HEADS)
        k_up = wide_b[:].rearrange("p (a h d) -> p a h d", a=HALVES, h=HEADS)
        ln_gb = wide_a[:].rearrange("p (g n) -> p g n", g=2)
        stage = wide_b[:, 0:HALVES * 6 * P].rearrange("p (a v n) -> p a v n", a=HALVES, v=6)
        T_DQ, T_DK, T_IK, T_IQ = 0, 4, 6, 10
        sparse_t = gates[:, 0:12, :]
        spare = gates[:, 12:16, :].rearrange("p a n -> p (a n)")
        sel_score = bias_h
        y = proj[:].rearrange("p a n -> p (a n)")[:, 0:4 * SEQ].rearrange("p (s c t) -> p s c t", s=2, c=2)

        x_rows = xs[:].rearrange("p c s -> p (c s)").rearrange("p (v a n) -> p v a n", v=2, a=HALVES)
        flat = proj[:].rearrange("p a n -> p (a n)")
        low_g, low_u, hg, hu, act_e = (flat[0:SLOTS, FFE * i:FFE * (i + 1)] for i in range(5))
        expert_out = gates[:, 0:4, :].rearrange("p a n -> p (a n)").rearrange("p (b n) -> p b n", b=2)
        slot_to_token = gates[:, 4:6, :]
        place = route[:, 3, :]
        route4 = value[:, 0, :].rearrange("p (i n) -> p i n", i=2)[:, :, 0:HALVES * EGROUPS * EPG * EPG]

        def slab_of(tile, n, k):
            return lambda width: tile[:, n % RING, 0:k * width].rearrange("p (k n) -> p k n", k=k)

        def count(n, j=None, per=0):
            return n if j is None else j * per + n

        def layer_base(layer):
            return S_BLOCK2 + layer * PER_LAYER

        def ring(name, n):
            return (S[name + "_b"], n - S_SECOND) if n >= S_SECOND else (S[name], n)

        def wait_slab(eng, name, n, j=None, per=0):
            sem, local = ring(name, n)
            eng.wait_ge(sem, count(local + 1, j, per))

        def wait_raw(eng, n, j=None, per=0):
            sem, local = ring(f"raw_in{n % RING}", n)
            eng.wait_ge(sem, 16 * count(local // RING + 1, j, per // RING))

        def wait_slot(eng, name, n, j=None, per=0, more=None):
            sem, local = ring(name, n)
            if j is not None or local >= RING:
                eng.wait_ge(sem, count(local - RING + 1, j, per))
            elif n >= S_SECOND:
                eng.wait_ge(S[name], more * PER_ROUND + (n - RING + 1))

        def further_rounds(eng, layer):
            eng.wait_ge(S["rounds_known"], layer + 1)
            return eng.value_load(rounds[0:1, 0:1], min_val=0, max_val=SEQ // SLOTS - 1)

        class Visits:

            def __init__(self, eng, layer):
                self.eng, self.layer = eng, layer

            def sem(self, name):
                return S[f"{name}_{self.layer}"]

            def upto(self, name, v, j, k=1):
                n = k * (v + 1)
                if j is None and n > 0:
                    self.eng.wait_ge(self.sem(name), n)
                elif j is not None:
                    self.eng.wait_ge(self.sem(name), j * (EPG * k) + n)

            def groups(self, name, j, n, k):
                if j is not None or n > 0:
                    self.eng.wait_ge(self.sem(name), n if j is None else j * k + n)

        def over_experts(eng, layer, start, group, finish):
            def one_round(j0):
                start(j0)
                group(0, j0, True)
                with eng.Fori(1, EGROUPS) as g:
                    group(g, g if j0 is None else j0 + g, False)
                finish(EGROUPS - 1 if j0 is None else j0 + (EGROUPS - 1), j0)

            one_round(None)
            more = further_rounds(eng, layer)
            with eng.If(more > 0):
                with eng.Fori(0, more) as rr:
                    one_round(rr * EGROUPS + EGROUPS)
            return more

        def first_slab(i, first):
            return 0 if first and i == 0 else PER_EXPERT * i - 2

        GROUP_SLABS = EPG * PER_EXPERT

        block = ctx.enter_context(nc.Block())

        @block.sync
        def _(sp):
            more = None

            def load(n, src, j=None, per=0):
                k, width = src.shape[1], src.shape[2]
                wait_slot(sp, "lo_done", n, j, per, more)
                sp.dma_start(slab_of(raw, n, k)(width), src).then_inc(ring(f"raw_in{n % RING}", n)[0], 16)

            def rows_of(w, k0, k, c0, width):
                return w[k0 * P:(k0 + k) * P, c0:c0 + width].rearrange("(k p) n -> p k n", p=P)

            w_in, w_up, w_down = A["w_in"][0], A["w_up"][0], A["w_down"][0]
            for i in range(HALVES):
                sp.dma_start(x[:, i, :], A["x"][0, i * P:(i + 1) * P, :]).then_inc(S["x_in"], 16)
            for g in range(2):
                for i in range(4):
                    load(S_QK + 4 * g + i, rows_of(w_in, 2 * i, 2, D * g, D))
            for i in range(8):
                load(S_GATE + i, rows_of(w_in, 0, DC, 2 * D + 256 * i, 256))
            for i in range(2):
                load(S_BA + i, rows_of(A["w_branch_attn"][0], 0, 4, 512 * i, 512))
            for i in range(2):
                load(S_BP + i, rows_of(A["w_branch_pool"][0], 0, 4, 512 * i, 512))
            for i in range(4):
                load(S_OUT + i, rows_of(A["w_out"][0], 2 * i, 2, 0, D))

            up_steps = w_up.rearrange("(k p) (s j n) -> s j p k n", p=P, s=2, j=N_FF)
            down_steps = w_down.rearrange("(j k p) n -> j p k n", p=P, k=2)
            load(S_FFN, up_steps[0, 0])
            load(S_FFN + 1, up_steps[1, 0])
            with sp.Fori(0, (N_FF - 1) // 2) as jj:
                for s in range(2):
                    n = S_FFN_LOOP + 3 * s
                    j = jj * 2 + (1 + s)
                    load(n, up_steps[0, j], jj, 6)
                    load(n + 1, up_steps[1, j], jj, 6)
                    load(n + 2, down_steps[jj * 2 + s], jj, 6)
            load(S_BLOCK2 - 1, down_steps[N_FF - 1])

            for layer in range(LAYERS):
                b = layer_base(layer)
                w = A["w_in_2"][layer]
                for i in range(4):
                    load(b + L_IN + i, rows_of(w, 2 * i, 2, 0, D))
                for i in range(2):
                    load(b + L_IN_B + i, rows_of(w, 4 * i, 4, D, 512))
                load(b + L_IN_C, rows_of(w, 0, DC, D + 512, IN2 - D - 512))
                for i in range(2):
                    load(b + L_QUP + i, rows_of(A["w_q_up_2"][layer], 0, QC, 4 * MLA_D * i, 4 * MLA_D))
                load(b + L_UK, rows_of(A["w_uk_2"][layer], 0, KVC, 0, WIDTH))
                load(b + L_UV, rows_of(A["w_uv_2"][layer], 0, KVC, 0, WIDTH))
                for i in range(4):
                    load(b + L_O + i, rows_of(A["w_o_2"][layer], 2 * i, 2, 0, D))
                gate_w = A["w_gate_2"][layer].rearrange("e (h k p) n -> e h p k n", p=P, h=2)
                up_w = A["w_up_2"][layer].rearrange("e (h k p) n -> e h p k n", p=P, h=2)
                down_w = A["w_down_2"][layer].rearrange("e (h k p) n -> e h p k n", p=P, h=2)
                base = b + L_MOE

                def start(j):
                    pass

                def group(g, j, first):
                    for i in range(EPG):
                        n = base + first_slab(i, first)
                        slabs = [(gate_w, 0), (up_w, 0)] + ([] if first and i == 0 else [(down_w, -1)])
                        for at, (w, back) in enumerate(slabs):
                            for h in range(2):
                                load(n + 2 * at + h, w[g * EPG + (i + back), h], j, GROUP_SLABS)

                def finish(j, j0):
                    n = base + PER_ROUND - 2
                    for h in range(2):
                        load(n + h, down_w[EXPERTS - 1, h], j0, GROUP_SLABS)

                more = over_experts(sp, layer, start, group, finish)
            sp.wait_ge(S["ln_done"], 2 * HALVES * LAYERS)
            for i in range(HALVES):
                sp.dma_start(out[0, i * P:(i + 1) * P, :], x[:, i, :]).then_inc(S["out_stored"], 16)
            sp.wait_ge(S["out_stored"], 16 * HALVES)

        @block.gpsimd
        def _(pool):
            w = Waits(pool, S)
            nc.gpsimd.memset(power[:], -0.5).then_inc(S["fills_set"], 1)
            nc.gpsimd.memset(zeros[:], 0.0).then_inc(S["fills_set"], 1)
            nc.gpsimd.memset(k_t[:], 0.0).then_inc(S["fills_set"], 1)
            w.next("fills_set", 3)

            def root(n):
                w.next("mean_square")
                nc.gpsimd.tensor_tensor(stat[:, 2, 0:n], stat[:, 1, 0:n], power[:, 0:n], ALU.pow)\
                    .then_inc(S["rstd_ready"], 1)

            def load_ln(gain, shift):
                pool.dma_start(ln_gb[:, 0, :], gain.partition_broadcast(P)).then_inc(S["ln_in"], 16)
                pool.dma_start(ln_gb[:, 1, :], shift.partition_broadcast(P)).then_inc(S["ln_in"], 16)

            root(HALVES)
            root(HALVES * 2 * HEADS)
            root(HALVES)
            for layer in range(LAYERS):
                root(2 * HALVES)
                if layer == 0:
                    pool.wait_ge(S["x_updated"], 8)
                else:
                    pool.wait_ge(S["ln_done"], 2 * HALVES * layer)
                nc.gpsimd.memset(q_up[:, :, :, MLA_D:P], 0.0).then_inc(S["pads_zero"], 1)
                nc.gpsimd.memset(k_up[:, :, :, MLA_D:P], 0.0).then_inc(S["pads_zero"], 1)
                w.next("turned_a", 8)
                load_ln(A["ln1_g_2"][layer], A["ln1_b_2"][layer])
                nc.gpsimd.memset(stage, 0.0).then_inc(S["stage_zero"], 1)
                w.next("stage_zero")
                w.next("in_saved0", 3)
                w.next("in_saved1", 5)
                for v in range(2):
                    nc.gpsimd.tensor_copy(stage[:, :, v, HD * v:HD * (v + 1)], proj[:, :, AT_DK:AT_DK + HD])\
                        .then_inc(S["staged"], 1)
                for v in range(4):
                    nc.gpsimd.tensor_copy(stage[:, :, 2 + v, IDX_D * v:IDX_D * (v + 1)],
                                          proj[:, :, AT_IK:AT_IK + IDX_D]).then_inc(S["staged"], 1)
                root(HALVES)
                pool.wait_ge(S["ln_done"], 2 * HALVES * layer + HALVES)
                load_ln(A["ln2_g_2"][layer], A["ln2_b_2"][layer])
                root(HALVES)

        @block.scalar
        def _(act):
            w = Waits(act, S)
            split = [0]

            more = None

            def split_hi(n, j=None, per=0, size=SLAB):
                wait_raw(act, n, j, per)
                wait_slot(act, "slab_used", n, j, per, more)
                nc.scalar.copy(hi[:, n % RING, 0:size], raw[:, n % RING, 0:size])\
                    .then_inc(ring("hi_done", n)[0], 1)

            def splits_to(n):
                while split[0] <= min(n, S_END - 1):
                    m = split[0]
                    short = (m - S_BLOCK2) % PER_LAYER if m >= S_BLOCK2 else -1
                    size = {L_IN_C: DC * (IN2 - D - 512), L_UK: 1024, L_UV: 1024}.get(short, SLAB)
                    size = 3 * 4 * MLA_D if short in (L_QUP, L_QUP + 1) else size
                    split_hi(m, size=size)
                    split[0] += 1

            def params():
                loads = [(const[:], A["constants"][:, 0:C_KEPT]),
                         (wide_b[:], A["constants"][:, C_BAND:C_N]),
                         (rows[V_G1:V_BG, :], A["norm_mix_g"][0].rearrange("(c p) -> c p", p=P)),
                         (rows[V_BG:V_G2, :], A["b_gate"][0].rearrange("(c p) -> c p", p=P)),
                         (rows[V_G2:V_PS, :], A["norm_ffn_g"][0].rearrange("(c p) -> c p", p=P)),
                         (rows[V_PS:V_QA, :], A["pool_scale"][0].rearrange("(c p) -> c p", p=P)),
                         (rows[V_QA:V_KVA, :], A["q_norm_g_2"].rearrange("l (c p) -> (l c) p", p=P)),
                         (rows[V_KVA:V_N, :], A["kv_norm_g_2"].rearrange("l (c p) -> (l c) p", p=P)),
                         (conv_rows[:, 0:TAPS, :], A["conv_w"][0].rearrange("t (c p) -> c t p", p=P)),
                         (conv_rows[:, TAPS, :], A["conv_b"][0].rearrange("(c p) -> c p", p=P)),
                         (head_gain[:, 0, :], A["q_norm_g"][0].partition_broadcast(P)),
                         (head_gain[:, 1, :], A["k_norm_g"][0].partition_broadcast(P)),
                         (w_pool, A["w_pool"][0].rearrange("g c d -> c g d")),
                         (router_w[:], A["router_w_2"].rearrange("(k p) e -> p k e", p=P)),
                         (router_b[:], A["router_bias_2"].partition_broadcast(P))]
                for dst, src in loads:
                    act.dma_start(dst, src).then_inc(S["params_in"], 16)

            def squares(sources, scratch, after=None):
                for i, src in enumerate(sources):
                    if after:
                        after(i)
                    nc.scalar.activation(scratch(i), src, ACT.Square, accum_out=stat[:, 0, i:i + 1])\
                        .then_inc(S["squares_summed"], 1)

            fm = [0]

            def feature_major(chunks, gain=None):
                for b in range(0, chunks, 2):
                    k = min(2, chunks - b)
                    w.next("fm_turned")
                    src = bank[6 + fm[0] % 2][:, 0:k * SEQ].rearrange("p (c t) -> p c t", c=k)
                    if gain is None:
                        nc.scalar.copy(xs[:, b:b + k, 0:SEQ], src).then_inc(S["fm_hi"], 1)
                    else:
                        for c in range(k):
                            nc.scalar.activation(xs[:, b + c, 0:SEQ], src[:, c, :], ACT.Copy,
                                                 scale=vec[:, gain(b + c):gain(b + c) + 1]).then_inc(S["fm_hi"], 1)
                    fm[0] += 1

            units = [0]

            def attention(scale_out=None):
                base = units[0]

                def exps(i):
                    act.wait_ge(S["logits"], base + i + 1)
                    w.upto("flipped", base + i - 1)
                    keys = P * (i // HEADS + 1)
                    nc.scalar.activation(prob[:, i % 2, 0:keys], logit[:, i % 2, 0:keys], ACT.Exp,
                                         bias=row_min[:, i:i + 1], scale=-1.0,
                                         accum_out=row_sum[:, i:i + 1]).then_inc(S["probs"], 1)

                def turned(i):
                    act.wait_ge(S["flipped"], base + i + 1)
                    w.upto("weighted", base + i - 1)
                    nk = i // HEADS + 1
                    nc.scalar.copy(prob_t[:, i % 2, 0:nk, :],
                                   bank[2 + i % 2][:, 0:nk * P].rearrange("p (k q) -> p k q", k=nk))\
                        .then_inc(S["probs_turned"], 1)

                for i in range(2 * HEADS):
                    exps(i)
                    if i:
                        turned(i - 1)
                turned(2 * HEADS - 1)
                units[0] += 2 * HEADS

            def save_half(n, name, saves):
                wait_slab(act, "slab_used", n)
                for dst, src in saves:
                    nc.scalar.copy(dst, src).then_inc(S[name], 1)

            params()
            act.wait_ge(S["x_in"], 16 * HALVES)
            squares([x[:, i, :] for i in range(HALVES)], lambda i: xn[:, i, :])
            w.next("turned_params")
            nc.scalar.copy(vec[:], bank[0][:, 0:V_N]).then_inc(S["params_copied"], 1)
            nc.scalar.copy(conv[:].rearrange("p t c -> p (t c)"), bank[1][:, 0:(TAPS + 1) * 2 * FFC])\
                .then_inc(S["params_copied"], 1)
            w.next("params_copied", 2)
            feature_major(DC, lambda c: V_G1 + c)
            splits_to(S_QK + 5)
            save_half(S_QK + 3, "qk_saved0", [(qk[:, 0, 512 * i:512 * (i + 1)], bank[i][:]) for i in range(2)])
            splits_to(S_VU + 5)
            save_half(S_VU + 3, "vu_saved0", [(vu[:, 0, 512 * i:512 * (i + 1)], bank[4 + i][:]) for i in range(2)])
            for i in range(8):
                splits_to(S_GATE + i + 2)
                act.wait_ge(S["slab_used"], S_GATE + i + 1)
                for c in range(2):
                    nc.scalar.activation(gates[:, 2 * i + c, :], bank[i % 4][:, c * SEQ:(c + 1) * SEQ], ACT.Sigmoid,
                                         bias=vec[:, V_BG + 2 * i + c:V_BG + 2 * i + c + 1])\
                        .then_inc(S["gates_saved"], 1)
            w.next("pooled_summed")
            for i in range(2):
                nc.scalar.copy(pooled[:, 2 * i:2 * i + 2, :],
                               bank[4 + i][:].rearrange("p (g t) -> p g t", g=2)).then_inc(S["pooled_copied"], 1)
            w.next("mixed_summed")
            for g in range(GROUPS):
                nc.scalar.activation(xs[:, 4 + g, 0:SEQ], bank[6 + g // 2][:, (g % 2) * SEQ:(g % 2 + 1) * SEQ],
                                     ACT.Copy, scale=vec[:, V_PS + g:V_PS + g + 1]).then_inc(S["mixed_hi"], 1)
            act.wait_ge(S["fills_set"], 3)
            for b in range(4):
                w.next("pairs_turned")
                src = bank[b % 2][:].rearrange("p (c t) -> p c t", c=2)
                if b < 2:
                    nc.scalar.copy(q_t[:, 2 * b:2 * b + 2, :], src).then_inc(S["pairs_copied"], 1)
                else:
                    for odd in range(2):
                        part = slice(HD * odd, HD * (odd + 1))
                        first = 4 * (b - 2) + odd
                        nc.scalar.copy(k_t[part, first:first + 3:2, :], src[part]).then_inc(S["pairs_copied"], 1)
            splits_to(S_BA + 2)
            attention()
            feature_major(4)
            splits_to(S_BP + 1)
            w.next("ab_summed")
            nc.scalar.copy(xs[:, :, 0:SEQ], mix).then_inc(S["mixed_hi"], 1)
            splits_to(S_OUT + 3)
            w.next("x_updated", 4)
            squares([x[:, i, :] for i in range(HALVES)], lambda i: xn[:, i, :])
            splits_to(S_FFN)
            feature_major(DC, lambda c: V_G2 + c)

            def ffn_step(n, par, j, jj=None):
                first = jj is None
                split_hi(n + 1, jj, 6)
                if not first:
                    split_hi(n + 2, jj, 6)
                for side, name in ((0, "tap2_g"), (1, "tap2_v")):
                    if side and not first:
                        split_hi(n + 3, jj, 6)
                    act.wait_ge(S["slab_used"], count(n + side + 1, jj, 6))
                    if not first:
                        act.wait_ge(S["act_lo"], j)
                    for c in range(2):
                        at = j * 2 + side * FFC + c
                        nc.scalar.activation(y[:, side, c, :], bank[side][:, c * SEQ:(c + 1) * SEQ], ACT.Identity,
                                             bias=conv[:, TAPS, bass.ds(at, 1)],
                                             scale=conv[:, 2, bass.ds(at, 1)]).then_inc(S[name], 1)
                act.wait_ge(S["taps_g"], j * 2 + 2)
                nc.scalar.activation(y[:, 0, :, :], y[:, 0, :, :], ACT.Silu).then_inc(S["silu_done"], 1)
                act.wait_ge(S["act_ready"], j + 1)
                nc.scalar.copy(act_s[:, par, :, 0:SEQ], y[:, 1, :, :]).then_inc(S["act_hi"], 1)

            ffn_step(S_FFN, 0, 0)
            split_hi(S_FFN_LOOP)
            with act.Fori(0, (N_FF - 1) // 2) as jj:
                for s in range(2):
                    ffn_step(S_FFN_LOOP + 3 * s, (1 + s) % 2, jj * 2 + (1 + s), jj)
            split[0] = S_BLOCK2

            for layer in range(LAYERS):
                b = layer_base(layer)
                feature_major(DC)
                splits_to(b + L_IN + 5)
                save_half(b + L_IN + 3, "in_saved0",
                          [(proj[:, 0, 512 * i:512 * (i + 1)], bank[i][:]) for i in range(2)])
                splits_to(b + L_IN_C + 1)
                save_half(b + L_IN_B + 1, "in_saved0", [(proj[:, 0, D:D + 512], bank[4][:])])
                w.next("in_saved0", 3)
                parts = [(i, at, n) for at, n in ((0, Q_LORA), (AT_KVA, KV_LORA)) for i in range(HALVES)]
                squares([proj[:, i, at:at + n] for i, at, n in parts],
                        lambda k: xn[:, parts[k][0], parts[k][1]:parts[k][1] + parts[k][2]],
                        after=lambda k: w.next("in_saved1", 5) if k == 1 else None)
                feature_major(QC + KVC, lambda c: V_QA + QC * layer + c if c < QC else V_KVA + KVC * layer + c - QC)
                splits_to(b + L_UV)
                w.next("pads_zero", 2)
                for i in range(2):
                    save_half(b + L_QUP + i, "qup_saved0",
                              [(q_up[:, 0, 4 * i:4 * i + 4, 0:MLA_D],
                                bank[2 * i][:, 0:4 * MLA_D].rearrange("p (h d) -> p h d", h=4))])
                save_half(b + L_UK, "uk_saved0",
                          [(k_up[:, 0, :, 0:HD], bank[4][:].rearrange("p (h d) -> p h d", h=HEADS))])
                save_half(b + L_UV, "uv_saved0", [(value[:, 0, :], bank[6][:])])
                splits_to(b + L_O + 2)
                for i in range(4):
                    w.next("turned_a")
                    nc.scalar.copy(q_t[:, 2 * i:2 * i + 2, :], bank[6][:].rearrange("p (c t) -> p c t", c=2))\
                        .then_inc(S["copied_q"], 1)
                    w.skip("turned_a")
                attention()
                for i in range(3):
                    w.next("turned_b")
                    nc.scalar.copy(sparse_t[:, 4 * i:4 * i + 2, :],
                                   bank[6][:].rearrange("p (c t) -> p c t", c=2)).then_inc(S["copied_even"], 1)
                    w.skip("turned_b")
                n_idx = HALVES * IDX_HEADS
                for i in range(n_idx):
                    keys = P * (i // IDX_HEADS + 1)
                    w.next("idx_scores")
                    w.upto("idx_added", n_idx * layer + i - 1)
                    nc.scalar.activation(logit[:, i % 2, 0:keys], bank[i % 2][:, 0:keys], ACT.Relu,
                                         scale=IDX_D ** -0.5).then_inc(S["idx_relu"], 1)
                attention()
                feature_major(DC)
                splits_to(b + L_O + 3)
                w.next("ln_centred", HALVES)
                squares([x[:, i, :] for i in range(HALVES)], lambda i: xn[:, i, :])
                feature_major(DC)
                w.next("router_logits")
                for i in range(HALVES):
                    nc.scalar.activation(route[:, 0, EXPERTS * i:EXPERTS * (i + 1)], bank[i][:, 0:EXPERTS], ACT.Exp,
                                         scale=-1.0).then_inc(S["router_exp"], 1)
                nc.scalar.copy(x_rows[:, 0], x[:]).then_inc(S["rows_hi"], 1)
                base = b + L_MOE
                V = Visits(act, layer)

                def low_rows(dst, src, name):
                    nc.scalar.copy(dst, src[SLOTS:2 * SLOTS, :]).then_inc(V.sem(name), 1)

                def turned_hi(v, j):
                    V.upto("act_turned", v, j)
                    nc.scalar.copy(act_t[:, :, 0:SLOTS], bank[2][:, 0:4 * SLOTS].rearrange("p (c s) -> p c s", c=4))\
                        .then_inc(V.sem("act_hi"), 1)

                def out_copied(last_slab, j):
                    wait_slab(act, "slab_used", last_slab, j, GROUP_SLABS)
                    nc.scalar.copy(expert_out[:, 0, :], bank[2][:]).then_inc(V.sem("expert_out_a"), 1)

                def start(j):
                    for i in range(2):
                        split_hi(base + i, j, GROUP_SLABS)

                def group(g, j, first):
                    for f in range(4):
                        V.groups("gathered", j, f + 1, 4)
                        nc.scalar.copy(xg[:, :, 2 * f:2 * f + 2, 0:SLOTS],
                                       bank[f % 2][:].rearrange("p (c e s) -> p e c s", c=2, e=EPG))\
                            .then_inc(V.sem("xg_hi"), 1)
                    for i in range(EPG):
                        n = base + first_slab(i, first)
                        after = n + (4 if first and i == 0 else 6)
                        split_hi(n + 2, j, GROUP_SLABS)
                        wait_slab(act, "slab_used", n + 1, j, GROUP_SLABS)
                        V.upto("gate_added", i - 1, j)
                        low_rows(low_g, bank[0], "gate_low")
                        split_hi(n + 3, j, GROUP_SLABS)
                        V.upto("gate_added", i, j)
                        nc.scalar.activation(hg, hg, ACT.Silu).then_inc(V.sem("silu_done"), 1)
                        if after == n + 6:
                            turned_hi(i - 1, j)
                        V.upto("dispatched", i, j)
                        nc.scalar.copy(slot_to_token[:, i % 2, :], bank[3][:, 0:SEQ])\
                            .then_inc(V.sem("dispatch_copied"), 1)
                        nc.scalar.copy(slot_gate[:, i % 2:i % 2 + 1], bank[3][:, bass.ds(g * EPG + (SEQ + i), 1)])\
                            .then_inc(V.sem("dispatch_copied"), 1)
                        for m in range(n + 4, after):
                            split_hi(m, j, GROUP_SLABS)
                        wait_slab(act, "slab_used", n + 3, j, GROUP_SLABS)
                        low_rows(low_u, bank[1], "up_low")
                        split_hi(after, j, GROUP_SLABS)
                        if after == n + 6:
                            out_copied(n + 5, j)
                        split_hi(after + 1, j, GROUP_SLABS)

                def finish(j, j0):
                    turned_hi(EPG - 1, j)
                    out_copied(base + PER_ROUND - 1, j0)

                more = over_experts(act, layer, start, group, finish)
                split[0] = b + PER_LAYER
                w.next("ln_centred", HALVES)
                squares([x[:, i, :] for i in range(HALVES)], lambda i: xn[:, i, :])

        @block.vector
        def _(dve):
            w = Waits(dve, S)
            split = [0]
            tt = nc.vector.tensor_tensor

            def split_lo(n, j=None, per=0, size=SLAB):
                wait_slab(dve, "hi_done", n, j, per)
                tt(lo[:, n % RING, 0:size], raw[:, n % RING, 0:size], hi[:, n % RING, 0:size].bitcast(F32),
                   ALU.subtract).then_inc(ring("lo_done", n)[0], 1)

            def splits_to(n):
                while split[0] <= min(n, S_END - 1):
                    m = split[0]
                    short = (m - S_BLOCK2) % PER_LAYER if m >= S_BLOCK2 else -1
                    size = {L_IN_C: DC * (IN2 - D - 512), L_UK: 1024, L_UV: 1024}.get(short, SLAB)
                    size = 3 * 4 * MLA_D if short in (L_QUP, L_QUP + 1) else size
                    split_lo(m, size=size)
                    split[0] += 1

            def mean_square(parts, eps, signals):
                if signals:
                    w.next("squares_summed", signals)
                for i, (at, k, n) in enumerate(parts):
                    ins = nc.vector.tensor_scalar(stat[:, 1, at:at + k], stat[:, 0, at:at + k], 1.0 / n, eps,
                                                  ALU.mult, ALU.add)
                    if i == len(parts) - 1:
                        ins.then_inc(S["mean_square"], 1)

            fm = [0]

            def feature_major(chunks, gain=None):
                for b in range(0, chunks, 2):
                    k = min(2, chunks - b)
                    w.next("fm_hi", 1 if gain is None else k)
                    src = bank[6 + fm[0] % 2][:, 0:k * SEQ].rearrange("p (c t) -> p c t", c=k)
                    if gain is None:
                        tt(xs[:, b:b + k, SEQ:2 * SEQ], src, xs[:, b:b + k, 0:SEQ].bitcast(F32), ALU.subtract)\
                            .then_inc(S["fm_lo"], 1)
                    else:
                        for c in range(k):
                            ins = nc.vector.scalar_tensor_tensor(
                                out=xs[:, b + c, SEQ:2 * SEQ], in0=src[:, c, :],
                                scalar=vec[:, gain(b + c):gain(b + c) + 1],
                                in1=xs[:, b + c, 0:SEQ].bitcast(F32), op0=ALU.mult, op1=ALU.subtract)
                        ins.then_inc(S["fm_lo"], 1)
                    fm[0] += 1

            def rotate(x1, x2, c, s, tmp, shape, step="rope"):
                c, s = (t.unsqueeze(2).broadcast_to(shape) for t in (c, s))
                for dst, a, t in ((0, x1, c), (1, x2, s), (2, x2, c), (3, x1, s)):
                    tt(tmp(dst), a, t, ALU.mult).then_inc(S["rope_products"], 1)
                w.next("rope_products", 4)
                tt(x1, tmp(0), tmp(1), ALU.subtract).then_inc(S["rope_summed"], 1)
                tt(x2, tmp(2), tmp(3), ALU.add).then_inc(S["rope_summed"], 1)

            units = [0]

            def attention(scale, col, sparse=False):
                base = units[0]

                def logits(i):
                    half, h = divmod(i, HEADS)
                    keys = P * (half + 1)
                    m = mask[:, half, 0:keys]
                    if sparse:
                        w.upto("logits", base + i - 1)
                        nc.vector.scalar_tensor_tensor(out=prob_bias(i, keys), in0=dist[:, half, 0:keys],
                                                       scalar=SLOPES[h] / scale, in1=sel_score[:, half, 0:keys],
                                                       op0=ALU.mult, op1=ALU.add).then_inc(S["bias_ready"], 1)
                        w.next("bias_ready")
                        m = prob_bias(i, keys)
                    dve.wait_ge(S["scores"], base + i + 1)
                    w.upto("probs", base + i - 1)
                    nc.vector.tensor_tensor_reduce(logit[:, i % 2, 0:keys], bank[i % 2][:, 0:keys], m, -scale, 3e38,
                                                   ALU.add, ALU.min, row_min[:, i:i + 1]).then_inc(S["logits"], 1)

                def save(half):
                    at = slice(HEADS * half, HEADS * (half + 1))
                    dve.wait_ge(S["probs"], base + HEADS * (half + 1))
                    nc.vector.reciprocal(row_inv[:, at], row_sum[:, at]).then_inc(S["sums_inverted"], 1)
                    w.next("sums_inverted")
                    dve.wait_ge(S["weighted"], base + HEADS * (half + 1))
                    tt(xn[:, half, col:col + WIDTH].rearrange("p (h d) -> p h d", h=HEADS),
                       bank[4 + half][:].rearrange("p (h d) -> p h d", h=HEADS),
                       row_inv[:, at].unsqueeze(2).broadcast_to([P, HEADS, HD]), ALU.mult)\
                        .then_inc(S["heads_saved"], 1)

                for i in range(2 * HEADS):
                    logits(i)
                    if i == HEADS + 1:
                        save(0)
                save(1)
                units[0] += 2 * HEADS

            def prob_bias(i, keys):
                return spare[:, (i % 2) * SEQ:(i % 2) * SEQ + keys]

            def save_half(n, name, saves):
                wait_slab(dve, "slab_used", n)
                for dst, src in saves:
                    nc.vector.tensor_copy(dst, src).then_inc(S[name], 1)

            def router():
                def step(ins):
                    ins.then_inc(S["router_step"], 1)
                    w.next("router_step")

                r = [route[:, i, :] for i in range(8)]
                n_groups = HALVES * EGROUPS

                def by_group(t):
                    return t.rearrange("p (g e) -> p g e", e=EPG)

                def against(t, n):
                    shape = [P, n, EPG, EPG]
                    return t.unsqueeze(3).broadcast_to(shape), t.unsqueeze(2).broadcast_to(shape)

                pairs = [route4[:, i, :].rearrange("p (g e j) -> p g e j", e=EPG, j=EPG) for i in range(2)]

                def tri_of(n):
                    return tri.unsqueeze(1).broadcast_to([P, n, EPG, EPG])

                w.next("router_exp", HALVES)
                step(nc.vector.tensor_scalar(r[1], r[0], 1.0, None, ALU.add))
                step(nc.vector.reciprocal(r[2], r[1]))
                affinity, biased, sel = r[2], r[3], r[4]
                step(tt(biased.rearrange("p (a e) -> p a e", a=HALVES),
                        affinity.rearrange("p (a e) -> p a e", a=HALVES),
                        router_b[:].unsqueeze(1).broadcast_to([P, HALVES, EXPERTS]), ALU.add))
                own, other = against(by_group(biased), n_groups)
                nc.vector.tensor_tensor(pairs[0], other, own, ALU.is_gt)
                step(tt(pairs[1], other, own, ALU.is_equal))
                step(tt(pairs[1], pairs[1], tri_of(n_groups), ALU.mult))
                step(tt(pairs[0], pairs[0], pairs[1], ALU.add))
                step(nc.vector.tensor_reduce(by_group(r[5]), pairs[0], AX.X, ALU.add))
                step(nc.vector.tensor_scalar(sel, r[5], TOP_E - 0.5, None, ALU.is_lt))
                step(tt(r[5], sel, biased, ALU.mult))
                step(nc.vector.tensor_reduce(r[6][:, 0:n_groups], by_group(r[5]), AX.X, ALU.add))
                score = r[6][:, 0:n_groups].rearrange("p (a g) -> p a g", a=HALVES)
                top = r[6][:, n_groups:n_groups + HALVES]
                step(nc.vector.tensor_reduce(top, score, AX.X, ALU.max))
                is_top = r[7][:, 0:n_groups].rearrange("p (a g) -> p a g", a=HALVES)
                step(tt(is_top, score, top.unsqueeze(2).broadcast_to([P, HALVES, EGROUPS]), ALU.is_equal))
                few = pairs[0][:, 0:HALVES]
                step(tt(few, against(is_top, HALVES)[1], tri_of(HALVES), ALU.mult))
                earlier = r[7][:, n_groups:2 * n_groups].rearrange("p (a g) -> p a g", a=HALVES)
                step(nc.vector.tensor_reduce(earlier, few, AX.X, ALU.add))
                step(nc.vector.tensor_scalar(earlier, earlier, 0.5, None, ALU.is_lt))
                step(tt(is_top, is_top, earlier, ALU.mult))
                step(tt(by_group(sel), by_group(sel),
                        r[7][:, 0:n_groups].unsqueeze(2).broadcast_to([P, n_groups, EPG]), ALU.mult))
                step(tt(r[5], sel, affinity, ALU.mult))
                total = r[6][:, n_groups:n_groups + HALVES]
                halves = r[5].rearrange("p (a e) -> p a e", a=HALVES)
                step(nc.vector.tensor_reduce(total, halves, AX.X, ALU.add))
                step(nc.vector.reciprocal(r[6][:, 0:HALVES], total))
                tt(r[0].rearrange("p (a e) -> p a e", a=HALVES), halves,
                   r[6][:, 0:HALVES].unsqueeze(2).broadcast_to([P, HALVES, EXPERTS]), ALU.mult)\
                    .then_inc(S["routed"], 1)

            def places():
                def step(ins):
                    ins.then_inc(S["places_step"], 1)
                    w.next("places_step")

                n = HALVES * EXPERTS
                w.next("counted")
                step(nc.vector.tensor_scalar(route[:, 1, :], route[:, 4, :], -ELSEWHERE, ELSEWHERE,
                                             ALU.mult, ALU.add))
                step(tt(place, route[:, 1, :], bank[3][:, 0:n], ALU.add))
                step(nc.vector.tensor_reduce(route[:, 1, 0:1], bank[3][:, n:n + EXPERTS], AX.X, ALU.max))
                n_full = SEQ // SLOTS - 1
                step(tt(route[:, 1, 1:1 + n_full], route[:, 1, 0:1].broadcast_to([P, n_full]),
                        const[:, C_FULL:C_KEPT], ALU.is_gt))
                step(nc.vector.tensor_reduce(route[:, 1, 0:1], route[:, 1, 1:1 + n_full], AX.X, ALU.add))
                nc.vector.tensor_copy(rounds[:], route[:, 1, 0:1]).then_inc(S["rounds_known"], 1)

            def experts(b, layer):
                base = b + L_MOE
                V = Visits(dve, layer)

                def turned_lo(v, j):
                    V.upto("act_hi", v, j)
                    tt(act_t[:, :, SLOTS:2 * SLOTS], bank[2][:, 0:4 * SLOTS].rearrange("p (c s) -> p c s", c=4),
                       act_t[:, :, 0:SLOTS].bitcast(F32), ALU.subtract).then_inc(V.sem("act_lo"), 1)

                def out_copied(last_slab, j):
                    wait_slab(dve, "slab_used", last_slab, j, GROUP_SLABS)
                    nc.vector.tensor_copy(expert_out[:, 1, :], bank[3][:]).then_inc(V.sem("expert_out_v"), 1)

                def start(j):
                    for i in range(2):
                        split_lo(base + i, j, GROUP_SLABS)
                    if j is not None:
                        V.groups("one_hot", j, 0, HALVES)
                        tt(place, place, const[:, C_FULL:C_FULL + 1].broadcast_to([P, HALVES * EXPERTS]),
                           ALU.subtract).then_inc(V.sem("places_moved"), EGROUPS)

                def group(g, j, first):
                    V.upto("dispatched", -1, j)
                    if first:
                        V.groups("places_moved", j, 0, 1)
                    for half in range(HALVES):
                        own = place[:, bass.ds(g * EPG + EXPERTS * half, EPG)]
                        shape = [P, EPG, 2, SLOTS]
                        tt(one_hot[:, half].rearrange("p e (v s) -> p e v s", v=2),
                           const[:, C_IOTA:C_IOTA + SLOTS].unsqueeze(1).unsqueeze(1).broadcast_to(shape),
                           own.unsqueeze(2).unsqueeze(2).broadcast_to(shape), ALU.is_equal).then_inc(V.sem("one_hot"), 1)
                    for f in range(4):
                        V.groups("xg_hi", j, f + 1, 4)
                        tt(xg[:, :, 2 * f:2 * f + 2, SLOTS:2 * SLOTS],
                           bank[f % 2][:].rearrange("p (c e s) -> p e c s", c=2, e=EPG),
                           xg[:, :, 2 * f:2 * f + 2, 0:SLOTS].bitcast(F32), ALU.subtract)\
                            .then_inc(V.sem("xg_lo"), 1)
                    for i in range(EPG):
                        n = base + first_slab(i, first)
                        after = n + (4 if first and i == 0 else 6)
                        split_lo(n + 2, j, GROUP_SLABS)
                        V.upto("gate_low", i, j)
                        V.upto("act_gated", i - 1, j)
                        tt(hg, bank[0][0:SLOTS, :], low_g, ALU.add).then_inc(V.sem("gate_added"), 1)
                        split_lo(n + 3, j, GROUP_SLABS)
                        if after == n + 6:
                            turned_lo(i - 1, j)
                        for m in range(n + 4, after):
                            split_lo(m, j, GROUP_SLABS)
                        V.upto("up_low", i, j)
                        tt(hu, bank[1][0:SLOTS, :], low_u, ALU.add).then_inc(V.sem("up_added"), 1)
                        V.upto("up_added", i, j)
                        V.upto("dispatch_copied", i, j, k=2)
                        V.upto("silu_done", i, j)
                        nc.vector.scalar_tensor_tensor(out=act_e, in0=hu, scalar=slot_gate[0:SLOTS, i % 2:i % 2 + 1],
                                                       in1=hg, op0=ALU.mult, op1=ALU.mult)\
                            .then_inc(V.sem("act_gated"), 1)
                        split_lo(after, j, GROUP_SLABS)
                        if after == n + 6:
                            out_copied(n + 5, j)
                        split_lo(after + 1, j, GROUP_SLABS)

                def finish(j, j0):
                    turned_lo(EPG - 1, j)
                    out_copied(base + PER_ROUND - 1, j0)

                return over_experts(dve, layer, start, group, finish)

            dve.wait_ge(S["x_in"], 16 * HALVES)
            mean_square([(0, HALVES, D)], EPS_RMS, HALVES)
            w.next("rstd_ready")
            for i in range(HALVES):
                nc.vector.tensor_scalar(xn[:, i, :], x[:, i, :], stat[:, 2, i:i + 1], None, ALU.mult)\
                    .then_inc(S["normed"], 1)
            w.next("params_copied", 2)
            feature_major(DC, lambda c: V_G1 + c)
            splits_to(S_QK + 5)
            save_half(S_QK + 3, "qk_saved1", [(qk[:, 1, 512 * i:512 * (i + 1)], bank[2 + i][:]) for i in range(2)])
            w.next("qk_saved0", 2)
            w.next("qk_saved1", 2)
            qk_heads = qk.rearrange("p a (h d) -> p (a h) d", d=HD)
            sq = xn[:].rearrange("p a (h d) -> p (a h) d", d=HD)
            n_rows = HALVES * 2 * HEADS
            tt(sq, qk_heads, qk_heads, ALU.mult).then_inc(S["qk_squared"], 1)
            splits_to(S_VU + 2)
            w.next("qk_squared")
            nc.vector.tensor_reduce(stat[:, 0, 0:n_rows], sq, AX.X, ALU.add).then_inc(S["qk_summed"], 1)
            w.next("qk_summed")
            mean_square([(0, n_rows, HD)], EPS_RMS, 0)
            splits_to(S_VU + 5)
            save_half(S_VU + 3, "vu_saved1", [(vu[:, 1, 512 * i:512 * (i + 1)], bank[6 + i][:]) for i in range(2)])
            splits_to(S_GATE + 2)
            w.next("rstd_ready")
            tt(qk_heads, qk_heads, stat[:, 2, 0:n_rows].unsqueeze(2).broadcast_to([P, n_rows, HD]), ALU.mult)\
                .then_inc(S["qk_scaled"], 1)
            splits_to(S_GATE + 3)
            w.next("qk_scaled")
            for i in range(2):
                part = qk[:, :, WIDTH * i:WIDTH * (i + 1)].rearrange("p a (h d) -> p a h d", d=HD)
                gain = head_gain[:, i, :].unsqueeze(1).unsqueeze(1).broadcast_to([P, HALVES, HEADS, HD])
                tt(part, part, gain, ALU.mult).then_inc(S["qk_gained"], 1)
            splits_to(S_GATE + 4)
            w.next("qk_gained", 2)
            four = qk.rearrange("p a (h d) -> p a h d", d=HD)
            shape = [P, HALVES, 2 * HEADS, ROPE1]

            def tmp1(i):
                n = HALVES * 2 * HEADS * ROPE1
                flat = xn[:].rearrange("p a n -> p (a n)")[:, i * n:(i + 1) * n]
                return flat.rearrange("p (a h d) -> p a h d", a=HALVES, d=ROPE1)

            rotate(four[:, :, :, 0:ROPE1], four[:, :, :, ROPE1:2 * ROPE1], cos1, sin1, tmp1, shape)
            splits_to(S_GATE + 9)
            w.next("mixed_hi", GROUPS)
            for g in range(GROUPS):
                nc.vector.scalar_tensor_tensor(
                    out=xs[:, 4 + g, SEQ:2 * SEQ], in0=bank[6 + g // 2][:, (g % 2) * SEQ:(g % 2 + 1) * SEQ],
                    scalar=vec[:, V_PS + g:V_PS + g + 1], in1=xs[:, 4 + g, 0:SEQ].bitcast(F32),
                    op0=ALU.mult, op1=ALU.subtract).then_inc(S["mixed_lo"], 1)
            splits_to(S_BA + 2)
            attention(SC1, 0)
            feature_major(4)
            splits_to(S_BP + 1)
            dve.wait_ge(S["gates_saved"], 2 * 8)
            for i in range(4):
                dve.wait_ge(S["slab_used"], S_BA + i // 2 + 1)
                tt(mix[:, 2 * i:2 * i + 2, :], bank[i][:].rearrange("p (c t) -> p c t", c=2),
                   gates[:, 2 * i:2 * i + 2, :], ALU.mult).then_inc(S["a_gated"], 1)
            for i in range(4):
                dve.wait_ge(S["slab_used"], S_BP + i // 2 + 1)
                part = gates[:, DC + 2 * i:DC + 2 * i + 2, :]
                tt(part, bank[4 + i][:].rearrange("p (c t) -> p c t", c=2), part, ALU.mult)\
                    .then_inc(S["b_gated"], 1)
            w.next("a_gated", 4)
            w.next("b_gated", 4)
            tt(mix, mix, gates[:, DC:2 * DC, :], ALU.add).then_inc(S["ab_summed"], 1)
            w.next("mixed_hi")
            tt(xs[:, :, SEQ:2 * SEQ], mix, xs[:, :, 0:SEQ].bitcast(F32), ALU.subtract).then_inc(S["mixed_lo"], 1)
            splits_to(S_OUT + 3)

            def add_to_x(first):
                for i in range(4):
                    part = x[:, i // 2, 512 * (i % 2):512 * (i % 2 + 1)]
                    tt(part, part, bank[first + i][:], ALU.add).then_inc(S["x_updated"], 1)
                w.next("x_updated", 4)

            dve.wait_ge(S["slab_used"], S_OUT + 4)
            add_to_x(0)
            mean_square([(0, HALVES, D)], EPS_RMS, HALVES)
            w.next("rstd_ready")
            for i in range(HALVES):
                nc.vector.tensor_scalar(xn[:, i, :], x[:, i, :], stat[:, 2, i:i + 1], None, ALU.mult)\
                    .then_inc(S["normed"], 1)
            splits_to(S_FFN)
            feature_major(DC, lambda c: V_G2 + c)

            def ffn_step(n, par, j, jj=None):
                first = jj is None
                split_lo(n + 1, jj, 6)
                if not first:
                    split_lo(n + 2, jj, 6)
                for side, name in ((0, "g"), (1, "v")):
                    if side and not first:
                        split_lo(n + 3, jj, 6)
                    dve.wait_ge(S["tap2_" + name], j * 2 + 2)
                    for t, done in ((1, "tap1_"), (0, "taps_")):
                        back = 2 - t
                        if t == 0:
                            dve.wait_ge(S["tap1_" + name], j * 2 + 2)
                        for c in range(2):
                            dst = y[:, side, c, back:SEQ]
                            nc.vector.scalar_tensor_tensor(
                                out=dst, in0=bank[side][:, c * SEQ:(c + 1) * SEQ - back],
                                scalar=conv[:, t, bass.ds(j * 2 + side * FFC + c, 1)], in1=dst,
                                op0=ALU.mult, op1=ALU.add).then_inc(S[done + name], 1)
                dve.wait_ge(S["silu_done"], j + 1)
                dve.wait_ge(S["taps_v"], j * 2 + 2)
                tt(y[:, 1, :, :], y[:, 0, :, :], y[:, 1, :, :], ALU.mult).then_inc(S["act_ready"], 1)
                dve.wait_ge(S["act_hi"], j + 1)
                tt(act_s[:, par, :, SEQ:2 * SEQ], y[:, 1, :, :], act_s[:, par, :, 0:SEQ].bitcast(F32), ALU.subtract)\
                    .then_inc(S["act_lo"], 1)

            ffn_step(S_FFN, 0, 0)
            split_lo(S_FFN_LOOP)
            with dve.Fori(0, (N_FF - 1) // 2) as jj:
                for s in range(2):
                    ffn_step(S_FFN_LOOP + 3 * s, (1 + s) % 2, jj * 2 + (1 + s), jj)
            split[0] = S_BLOCK2
            w.next("acc_closed")
            add_to_x(4)

            for layer in range(LAYERS):
                b = layer_base(layer)
                feature_major(DC)
                splits_to(b + L_IN + 5)
                save_half(b + L_IN + 3, "in_saved1", [(proj[:, 1, 512 * i:512 * (i + 1)], bank[2 + i][:]) for i in range(2)])
                splits_to(b + L_IN_C + 1)
                save_half(b + L_IN_C, "in_saved1", [(proj[:, 1, D:D + 512], bank[5][:])])
                for i in range(HALVES):
                    nc.vector.tensor_copy(proj[:, i, D + 512:IN2], bank[6 + i][:, 0:IN2 - D - 512])\
                        .then_inc(S["in_saved1"], 1)
                w.next("in_saved1", 5)
                w.next("in_saved0", 3)
                mean_square([(0, 2, Q_LORA), (2, 2, KV_LORA)], EPS_RMS, 2 * HALVES)
                kr = proj[:, :, AT_KR:AT_KR + KR]
                spare4 = spare.rearrange("p (i n) -> p i n", i=4)

                def tmp_k(i):
                    return spare4[:, i, 0:HALVES * ROPE2].rearrange("p (a h d) -> p a h d", a=HALVES, h=1)

                kr4 = kr.unsqueeze(2)
                rotate(kr4[:, :, :, 0:ROPE2], kr4[:, :, :, ROPE2:KR], cos2, sin2, tmp_k, [P, HALVES, 1, ROPE2])
                nc.vector.tensor_scalar(idx_w[:], proj[:, :, AT_IW:IN2], IDX_HEADS ** -0.5, None, ALU.mult)\
                    .then_inc(S["idx_weights"], 1)
                w.next("rstd_ready")
                for p_, (at, n) in enumerate(((0, Q_LORA), (AT_KVA, KV_LORA))):
                    for i in range(HALVES):
                        nc.vector.tensor_scalar(xn[:, i, at:at + n], proj[:, i, at:at + n],
                                                stat[:, 2, 2 * p_ + i:2 * p_ + i + 1], None, ALU.mult)\
                            .then_inc(S["normed"], 1)
                feature_major(QC + KVC, lambda c: V_QA + QC * layer + c if c < QC else V_KVA + KVC * layer + c - QC)
                splits_to(b + L_UV)
                w.next("pads_zero", 2)
                w.next("rope_summed", 2 if layer else 4)
                nc.vector.tensor_copy(k_up[:, :, :, HD:MLA_D], kr.unsqueeze(2).broadcast_to([P, HALVES, HEADS, KR]))\
                    .then_inc(S["kr_spread"], 1)
                for i in range(2):
                    save_half(b + L_QUP + i, "qup_saved1",
                              [(q_up[:, 1, 4 * i:4 * i + 4, 0:MLA_D],
                                bank[2 * i + 1][:, 0:4 * MLA_D].rearrange("p (h d) -> p h d", h=4))])
                w.next("qup_saved0", 2)
                w.next("qup_saved1", 2)

                def tmp_q(i):
                    return spare4[:, i, :].rearrange("p (a h d) -> p a h d", a=HALVES, h=HEADS)

                rotate(q_up[:, :, :, HD:HD + ROPE2], q_up[:, :, :, HD + ROPE2:MLA_D], cos2, sin2, tmp_q,
                       [P, HALVES, HEADS, ROPE2])
                w.skip("rope_summed", 2)
                save_half(b + L_UK, "uk_saved1",
                          [(k_up[:, 1, :, 0:HD], bank[5][:].rearrange("p (h d) -> p h d", h=HEADS))])
                save_half(b + L_UV, "uv_saved1", [(value[:, 1, :], bank[7][:])])
                splits_to(b + L_O + 2)
                for i in range(4):
                    w.next("turned_a", 2)
                    nc.vector.tensor_copy(k_t[:, 2 * i:2 * i + 2, :], bank[7][:].rearrange("p (c t) -> p c t", c=2))\
                        .then_inc(S["copied_k"], 1)
                attention(SC_MLA, 0)
                for i in range(3):
                    w.next("turned_b", 2)
                    nc.vector.tensor_copy(sparse_t[:, 4 * i + 2:4 * i + 4, :], bank[7][:].rearrange("p (c t) -> p c t", c=2))\
                        .then_inc(S["copied_odd"], 1)

                w.next("idx_weights")
                score = sel_score
                for i in range(HALVES * IDX_HEADS):
                    half, h = divmod(i, IDX_HEADS)
                    keys = P * (half + 1)
                    dst = score[:, half, 0:keys]
                    w.next("idx_relu")
                    weight = idx_w[:, half, h:h + 1]
                    if h == 0:
                        nc.vector.tensor_scalar(dst, logit[:, i % 2, 0:keys], weight, None, ALU.mult)\
                            .then_inc(S["idx_added"], 1)
                    else:
                        nc.vector.scalar_tensor_tensor(out=dst, in0=logit[:, i % 2, 0:keys], scalar=weight, in1=dst,
                                                       op0=ALU.mult, op1=ALU.add).then_inc(S["idx_added"], 1)
                    w.next("idx_added")
                for half in range(HALVES):
                    keys = P * (half + 1)
                    dst = score[:, half, 0:keys]
                    tt(dst, dst, mask[:, half, 0:keys], ALU.add).then_inc(S["idx_masked"], 1)
                    w.next("idx_masked")
                    for _ in range(KEEP // 8):
                        nc.vector.max(best[:], dst).then_inc(S["topk_step"], 1)
                        w.next("topk_step")
                        nc.vector.match_replace(dst, best[:], dst, TAKEN).then_inc(S["topk_step"], 1)
                        w.next("topk_step")
                    nc.vector.tensor_scalar(dst, dst, TAKEN * 0.5, -NEG, ALU.is_le, ALU.mult).then_inc(S["sel_step"], 1)
                    w.next("sel_step")
                    nc.vector.scalar_tensor_tensor(out=dst, in0=dst, scalar=NEG, in1=mask[:, half, 0:keys],
                                                   op0=ALU.add, op1=ALU.add).then_inc(S["sel_step"], 1)
                    w.next("sel_step")
                attention(SC_DSA, WIDTH, sparse=True)
                feature_major(DC)
                splits_to(b + L_O + 3)
                wait_slab(dve, "slab_used", b + L_O + 3)
                for norm in range(2):
                    if norm:
                        feature_major(DC)
                        router()
                        w.next("rows_hi")
                        tt(x_rows[:, 1], x[:], x_rows[:, 0].bitcast(F32), ALU.subtract).then_inc(S["rows_lo"], 1)
                        places()
                        experts(b, layer)
                        w.next("acc_closed")
                    for i in range(4):
                        part = x[:, i // 2, 512 * (i % 2):512 * (i % 2 + 1)]
                        nc.vector.scalar_tensor_tensor(out=part, in0=part, scalar=ALPHA,
                                                       in1=bank[4 * norm + i][:], op0=ALU.mult, op1=ALU.add,
                                                       accum_out=stat[:, 0, i:i + 1]).then_inc(S["ln_added"], 1)
                    w.next("ln_added", 4)
                    tt(stat[:, 1, 0:2], stat[:, 0, 0:4:2], stat[:, 0, 1:4:2], ALU.add).then_inc(S["ln_mean_step"], 1)
                    w.next("ln_mean_step")
                    nc.vector.tensor_scalar(stat[:, 2, 0:2], stat[:, 1, 0:2], 1.0 / D, None, ALU.mult)\
                        .then_inc(S["ln_mean_step"], 1)
                    w.next("ln_mean_step")
                    for i in range(HALVES):
                        nc.vector.tensor_scalar(x[:, i, :], x[:, i, :], stat[:, 2, i:i + 1], None, ALU.subtract)\
                            .then_inc(S["ln_centred"], 1)
                    mean_square([(0, HALVES, D)], EPS_LN, HALVES)
                    w.next("rstd_ready")
                    w.next("ln_centred", HALVES)
                    w.next("ln_in", 32)
                    for i in range(HALVES):
                        nc.vector.scalar_tensor_tensor(out=x[:, i, :], in0=x[:, i, :], scalar=stat[:, 2, i:i + 1],
                                                       in1=ln_gb[:, 0, :], op0=ALU.mult, op1=ALU.mult)\
                            .then_inc(S["ln_scaled"], 1)
                    w.next("ln_scaled", HALVES)
                    for i in range(HALVES):
                        tt(x[:, i, :], x[:, i, :], ln_gb[:, 1, :], ALU.add).then_inc(S["ln_done"], 1)
                    w.next("ln_done", HALVES)
                split[0] = b + PER_LAYER
        @block.tensor
        def _(pe):
            w = Waits(pe, S)
            mm = nc.tensor.matmul

            def turn(dst, src):
                return nc.tensor.transpose(dst, src, ident[0:src.shape[0], 0:src.shape[0]])

            fm = [0]

            def feature_major(chunks, src):
                for b in range(0, chunks, 2):
                    w.upto("fm_lo", fm[0] - 1)
                    for c in range(b, min(b + 2, chunks)):
                        for half in range(HALVES):
                            at = (c - b) * SEQ + half * P
                            ins = turn(bank[6 + fm[0] % 2][:, at:at + P], src(c, half))
                    ins.then_inc(S["fm_turned"], 1)
                    fm[0] += 1

            def fm_ready():
                w.upto("fm_lo", fm[0])

            def products(out_, lhs_hi, lhs_lo, rhs_hi, rhs_lo, first, last):
                mm(out_, lhs_hi, rhs_hi, start=first, stop=False)
                mm(out_, lhs_lo, rhs_hi, start=False, stop=False)
                return mm(out_, lhs_hi, rhs_lo, start=False, stop=last)

            def token_major(n, slabs, k_per, widths, banks, chunk=0, lhs=xs, j=None, per=0, open_=True, close=True,
                            ready=None):
                for s in range(slabs):
                    wait_slab(pe, "lo_done", n + s, j, per)
                    wh, wl = (slab_of(t, n + s, k_per)(sum(widths)) for t in (hi, lo))
                    for k in range(k_per):
                        kk = s * k_per + k
                        first, last = open_ and kk == 0, close and kk == slabs * k_per - 1
                        for half in range(HALVES):
                            at = half * P
                            a_hi = lhs[:, chunk + kk, at:at + P]
                            a_lo = lhs[:, chunk + kk, SEQ + at:SEQ + at + P]
                            for i, width in enumerate(widths):
                                c0 = sum(widths[:i])
                                ins = products(banks[half][i][:, 0:width], a_hi, a_lo, wh[:, k, c0:c0 + width],
                                               wl[:, k, c0:c0 + width], first, last)
                    ins.then_inc(ring("slab_used", n + s)[0], 1)

            def feature_slab(n, k_chunks, columns, banks, chunk=0, j=None, per=0):
                wait_slab(pe, "lo_done", n, j, per)
                wh, wl = (slab_of(t, n, k_chunks)(columns) for t in (hi, lo))
                for c in range(columns // P):
                    dst = banks[c // 2][:, (c % 2) * SEQ:(c % 2 + 1) * SEQ]
                    for k in range(k_chunks):
                        x_hi, x_lo = xs[:, chunk + k, 0:SEQ], xs[:, chunk + k, SEQ:2 * SEQ]
                        col = slice(c * P, (c + 1) * P)
                        mm(dst, wh[:, k, col], x_hi, start=k == 0, stop=False)
                        mm(dst, wh[:, k, col], x_lo, start=False, stop=False)
                        ins = mm(dst, wl[:, k, col], x_hi, start=False, stop=k == k_chunks - 1)
                ins.then_inc(ring("slab_used", n)[0], 1)

            units = [0]

            def attention(q, k, v):
                base, n = units[0], 2 * HEADS

                def score(i):
                    half, h = divmod(i, HEADS)
                    if i >= 2:
                        pe.wait_ge(S["logits"], base + i - 1)
                    keys = P * (half + 1)
                    mm(bank[i % 2][:, 0:keys], q(h, half), k(h)[:, 0:keys], start=True, stop=True)\
                        .then_inc(S["scores"], 1)

                def flip(i):
                    pe.wait_ge(S["probs"], base + i + 1)
                    if i >= 2:
                        pe.wait_ge(S["probs_turned"], base + i - 1)
                    for c in range(i // HEADS + 1):
                        ins = turn(bank[2 + i % 2][:, c * P:(c + 1) * P], prob[:, i % 2, c * P:(c + 1) * P])
                    ins.then_inc(S["flipped"], 1)

                def weigh(i):
                    half, h = divmod(i, HEADS)
                    pe.wait_ge(S["probs_turned"], base + i + 1)
                    for c in range(half + 1):
                        ins = mm(bank[4 + half][:, h * HD:(h + 1) * HD], prob_t[:, i % 2, c, :], v(h, c),
                                 start=c == 0, stop=c == half)
                    ins.then_inc(S["weighted"], 1)

                for i in range(n + 2):
                    if i < n:
                        score(i)
                    if 1 <= i <= n:
                        flip(i - 1)
                    if i >= 2:
                        weigh(i - 2)
                units[0] += n

            halves4 = [[bank[0], bank[1]], [bank[2], bank[3]]]
            acc = [[bank[4], bank[5]], [bank[6], bank[7]]]

            def open_acc():
                for half in range(HALVES):
                    for i in range(2):
                        mm(acc[half][i][:], zeros[:], zeros[:, 0:1].broadcast_to([P, 512]), start=True, stop=False)

            def close_acc():
                for half in range(HALVES):
                    for i in range(2):
                        ins = mm(acc[half][i][:], zeros[:], zeros[:, 0:1].broadcast_to([P, 512]), start=False, stop=True)
                ins.then_inc(S["acc_closed"], 1)

            w.next("params_in", 16 * N_PARAMS)
            turn(bank[0][:, 0:V_N], rows)
            for t in range(TAPS + 1):
                ins = turn(bank[1][:, t * 2 * FFC:(t + 1) * 2 * FFC], conv_rows[:, t, :])
            ins.then_inc(S["turned_params"], 1)
            w.next("normed", HALVES)
            feature_major(DC, lambda c, half: xn[:, half, c * P:(c + 1) * P])
            fm_ready()
            w.next("params_copied", 2)
            token_major(S_QK, 4, 2, [512, 512], halves4)
            token_major(S_VU, 4, 2, [512, 512], acc)
            for i in range(8):
                if i == 0:
                    w.next("qk_saved0", 2)
                    w.next("qk_saved1", 2)
                if i >= 4:
                    pe.wait_ge(S["gates_saved"], 2 * (i - 3))
                feature_slab(S_GATE + i, DC, 256, [bank[i % 4]])
            w.next("vu_saved0", 2)
            w.next("vu_saved1", 2)
            for g in range(GROUPS):
                dst = bank[4 + g // 2][:, (g % 2) * SEQ:(g % 2 + 1) * SEQ]
                for half in range(HALVES):
                    ins = mm(dst, vu[:, half, WIDTH + g * P:WIDTH + (g + 1) * P], band[:, g, half, :],
                             start=half == 0, stop=half == HALVES - 1)
            ins.then_inc(S["pooled_summed"], 1)
            w.next("pooled_copied", 2)
            for g in range(GROUPS):
                ins = mm(bank[6 + g // 2][:, (g % 2) * SEQ:(g % 2 + 1) * SEQ], w_pool[:, g, :], pooled[:, g, :],
                         start=True, stop=True)
            ins.then_inc(S["mixed_summed"], 1)
            w.next("rope_summed", 2)
            w.next("gates_saved", 2 * 8)
            for b in range(4):
                w.upto("pairs_copied", (0, 0, 1, 2)[b])
                for c in range(2):
                    for half in range(HALVES):
                        at = c * SEQ + half * P
                        col = (2 * b + c) * P
                        ins = turn(bank[b % 2][:, at:at + P], qk[:, half, col:col + P])
                ins.then_inc(S["pairs_turned"], 1)
            w.next("pairs_copied", 6)
            attention(lambda h, half: q_t[:, h // 2, half * P:(half + 1) * P],
                      lambda h: k_t[:, h, :],
                      lambda h, c: vu[:, c, h * HD:(h + 1) * HD])
            w.next("mixed_lo", GROUPS)
            w.next("heads_saved", 2)
            feature_major(4, lambda c, half: xn[:, half, c * P:(c + 1) * P])
            fm_ready()
            for i in range(2):
                feature_slab(S_BA + i, 4, 512, bank[2 * i:2 * i + 2])
            for i in range(2):
                feature_slab(S_BP + i, 4, 512, bank[4 + 2 * i:6 + 2 * i], chunk=4)
            w.next("mixed_lo")
            token_major(S_OUT, 4, 2, [512, 512], halves4)
            w.next("normed", HALVES)
            feature_major(DC, lambda c, half: xn[:, half, c * P:(c + 1) * P])
            fm_ready()
            pe.wait_ge(S["fills_set"], 3)
            open_acc()

            def down(n, par, j, jj=None):
                pe.wait_ge(S["act_lo"], j)
                token_major(n, 1, 2, [512, 512], acc, lhs=act_s[:, par], j=jj, per=6, open_=False, close=False)

            feature_slab(S_FFN, DC, 256, [bank[0]])
            feature_slab(S_FFN + 1, DC, 256, [bank[1]])
            with pe.Fori(0, (N_FF - 1) // 2) as jj:
                for s in range(2):
                    n, j = S_FFN_LOOP + 3 * s, jj * 2 + (1 + s)
                    pe.wait_ge(S["taps_g"], j * 2)
                    feature_slab(n, DC, 256, [bank[0]], j=jj, per=6)
                    pe.wait_ge(S["taps_v"], j * 2)
                    feature_slab(n + 1, DC, 256, [bank[1]], j=jj, per=6)
                    down(n + 2, s, j, jj)
            down(S_BLOCK2 - 1, 0, N_FF)
            close_acc()
            w.next("x_updated", 8)

            for layer in range(LAYERS):
                b = layer_base(layer)
                feature_major(DC, lambda c, half: x[:, half, c * P:(c + 1) * P])
                fm_ready()
                token_major(b + L_IN, 4, 2, [512, 512], halves4)
                token_major(b + L_IN_B, 2, 4, [512], [[bank[4]], [bank[5]]])
                token_major(b + L_IN_C, 1, DC, [IN2 - D - 512], [[bank[6]], [bank[7]]])
                w.next("normed", 2 * HALVES)
                feature_major(QC + KVC, lambda c, half: xn[:, half, c * P:(c + 1) * P])
                fm_ready()
                for i in range(2):
                    token_major(b + L_QUP + i, 1, QC, [4 * MLA_D], [[bank[2 * i]], [bank[2 * i + 1]]])
                token_major(b + L_UK, 1, KVC, [WIDTH], [[bank[4]], [bank[5]]], chunk=QC)
                token_major(b + L_UV, 1, KVC, [WIDTH], [[bank[6]], [bank[7]]], chunk=QC)
                pe.wait_ge(S["rope_summed"], 2 + 4 * (layer + 1))
                w.next("kr_spread")
                for name in ("uk_saved0", "uk_saved1", "uv_saved0", "uv_saved1"):
                    w.next(name)
                w.next("pads_zero", 2)
                for i in range(4):
                    for src, to, copied in ((q_up, bank[6], "copied_q"), (k_up, bank[7], "copied_k")):
                        w.upto(copied, 4 * layer + i)
                        for c in range(2):
                            for half in range(HALVES):
                                at = c * SEQ + half * P
                                ins = turn(to[:, at:at + P], src[:, half, 2 * i + c, :])
                        ins.then_inc(S["turned_a"], 1)
                w.next("copied_q", 4)
                w.next("copied_k", 4)
                attention(lambda h, half: q_t[:, h, half * P:(half + 1) * P],
                          lambda h: k_t[:, h, :],
                          lambda h, c: value[:, c, h * HD:(h + 1) * HD])

                def sparse_src(c, half):
                    if c < T_DK:
                        return proj[:, half, AT_DQ + c * P:AT_DQ + (c + 1) * P]
                    if c < T_IQ:
                        return stage[:, half, c - T_DK, :]
                    return proj[:, half, AT_IQ + (c - T_IQ) * P:AT_IQ + (c - T_IQ + 1) * P]

                w.next("staged", 6)
                for i in range(6):
                    w.upto(("copied_even", "copied_odd")[i % 2], 3 * layer + i // 2)
                    for c in range(2):
                        for half in range(HALVES):
                            at = c * SEQ + half * P
                            ins = turn(bank[6 + i % 2][:, at:at + P], sparse_src(2 * i + c, half))
                    ins.then_inc(S["turned_b"], 1)
                w.next("copied_even", 3)
                w.next("copied_odd", 3)
                n_idx = HALVES * IDX_HEADS
                for i in range(n_idx):
                    half, h = divmod(i, IDX_HEADS)
                    keys = P * (half + 1)
                    if i >= 2:
                        pe.wait_ge(S["idx_relu"], n_idx * layer + i - 1)
                    mm(bank[i % 2][:, 0:keys], sparse_t[:, T_IQ + h // 4, half * P:(half + 1) * P],
                       sparse_t[:, T_IK + h % 4, 0:keys], start=True, stop=True).then_inc(S["idx_scores"], 1)
                w.next("idx_relu", n_idx)
                w.next("heads_saved", 2)
                attention(lambda h, half: sparse_t[:, T_DQ + h // 2, half * P:(half + 1) * P],
                          lambda h: sparse_t[:, T_DK + h % 2, :],
                          lambda h, c: proj[:, c, AT_DV:AT_DV + HD])
                w.next("heads_saved", 2)
                feature_major(DC, lambda c, half: xn[:, half, c * P:(c + 1) * P])
                fm_ready()
                token_major(b + L_O, 4, 2, [512, 512], halves4)
                pe.wait_ge(S["ln_done"], 2 * HALVES * layer + HALVES)
                feature_major(DC, lambda c, half: x[:, half, c * P:(c + 1) * P])
                fm_ready()
                for half in range(HALVES):
                    for k in range(DC):
                        for part in range(2):
                            at = part * SEQ + half * P
                            ins = mm(bank[half][:, 0:EXPERTS], xs[:, k, at:at + P].bitcast(F32), router_w[:, k, :],
                                     start=k == 0 and part == 0, stop=k == DC - 1 and part == 1)
                ins.then_inc(S["router_logits"], 1)
                w.next("routed")
                picked = route[:, 4, :].rearrange("p (a e) -> p a e", a=HALVES)
                all_ones = one.broadcast_to([P, P])
                mm(bank[3][:, 0:EXPERTS], before, picked[:, 0, :], start=True, stop=True)
                mm(bank[3][:, EXPERTS:2 * EXPERTS], all_ones, picked[:, 0, :], start=True, stop=False)
                mm(bank[3][:, EXPERTS:2 * EXPERTS], before, picked[:, 1, :], start=False, stop=True)
                for half in range(HALVES):
                    ins = mm(bank[3][:, 2 * EXPERTS:3 * EXPERTS], all_ones, picked[:, half, :], start=half == 0,
                             stop=half == HALVES - 1)
                ins.then_inc(S["counted"], 1)
                open_acc()
                w.next("rows_lo")
                base = b + L_MOE
                V = Visits(pe, layer)

                def wide_product(n, j, lhs, k_per, to):
                    for s in range(2):
                        wait_slab(pe, "lo_done", n + s, j, GROUP_SLABS)
                        wh, wl = (slab_of(t, n + s, k_per)(512 * len(to)) for t in (hi, lo))
                        for k in range(k_per):
                            kk = s * k_per + k
                            for c, dst in enumerate(to):
                                col = slice(512 * c, 512 * (c + 1))
                                mm(dst[:], lhs(kk), wh[:, k, col], start=kk == 0, stop=False)
                                ins = mm(dst[:], lhs(kk), wl[:, k, col], start=False, stop=kk == 2 * k_per - 1)
                        ins.then_inc(ring("slab_used", n + s)[0], 1)

                def scatter(v, j):
                    V.upto("expert_out_a", v, j)
                    V.upto("expert_out_v", v, j)
                    for half in range(HALVES):
                        for c in range(2):
                            ins = mm(acc[half][c][:], slot_to_token[:, v % 2, half * P:(half + 1) * P],
                                     expert_out[:, c, :], start=False, stop=False)
                    ins.then_inc(V.sem("scattered"), 1)

                def act_there(v, j):
                    V.upto("act_gated", v, j)
                    V.upto("expert_out_a", v - 1, j)

                def turn_act(v, j):
                    for c in range(4):
                        ins = turn(bank[2][:, c * SLOTS:(c + 1) * SLOTS], act_e[:, c * P:(c + 1) * P])
                    ins.then_inc(V.sem("act_turned"), 1)

                def down(v, n, j, jn):
                    V.upto("act_lo", v, j)
                    wide_product(n, jn, lambda k: act_t[:, k, :], 2, [bank[2], bank[3]])

                def start(j):
                    pass

                def group(g, j, first):
                    V.groups("one_hot", j, 2, 2)
                    V.upto("gate_added", -1, j)
                    V.upto("up_added", -1, j)
                    for f in range(4):
                        if f >= 2:
                            V.groups("xg_lo", j, f - 1, 4)
                        for c in range(2):
                            chunk = slice((2 * f + c) * P, (2 * f + c + 1) * P)
                            for half in range(HALVES):
                                for part in range(2):
                                    ins = mm(bank[f % 2][:, c * 256:(c + 1) * 256], x_rows[:, part, half, chunk],
                                             one_hot[:, half, :, 0:SLOTS], start=half == 0 and part == 0,
                                             stop=half == 1 and part == 1)
                        ins.then_inc(V.sem("gathered"), 1)
                    V.groups("xg_lo", j, 4, 4)
                    for i in range(EPG):
                        n = base + first_slab(i, first)
                        second = not (first and i == 0)
                        V.upto("gate_added", i - 1, j)
                        wide_product(n, j, lambda k: xg[:, i, k, :], 4, [bank[0]])
                        if not (first and i <= 1):
                            scatter(i - 2, j)
                        if second:
                            act_there(i - 1, j)
                        V.upto("expert_out_v", i - 2, j)
                        if first and i == 1:
                            V.upto("dispatch_copied", 0, j, k=2)
                        hot = [one_hot[:, half, i, :].bitcast(F32) for half in range(HALVES)]
                        for half in range(HALVES):
                            mm(bank[3][:, half * P:(half + 1) * P], hot[half], ident, start=True, stop=True)
                        for half in range(HALVES):
                            ins = mm(bank[3][:, SEQ:SEQ + EXPERTS], hot[half],
                                     route[:, 0, EXPERTS * half:EXPERTS * (half + 1)], start=half == 0, stop=half == 1)
                        ins.then_inc(V.sem("dispatched"), 1)
                        if second:
                            turn_act(i - 1, j)
                        V.upto("up_added", i - 1, j)
                        wide_product(n + 2, j, lambda k: xg[:, i, k, :], 4, [bank[1]])
                        if second:
                            V.upto("dispatch_copied", i, j, k=2)
                            down(i - 1, n + 4, j, j)

                def finish(j, j0):
                    act_there(EPG - 1, j)
                    scatter(EPG - 2, j)
                    turn_act(EPG - 1, j)
                    down(EPG - 1, base + PER_ROUND - 2, j, j0)
                    scatter(EPG - 1, j)

                over_experts(pe, layer, start, group, finish)
                close_acc()
                pe.wait_ge(S["ln_done"], 2 * HALVES * (layer + 1))


def kernel(**inputs):
    import numpy as _np
    import concourse.bacc as _bacc
    from concourse import mybir as _mybir
    from concourse.bass_utils import run_bass_kernel_spmd as _run

    nc = _bacc.Bacc("TRN2", target_bir_lowering=False, num_devices=1)
    arrays = {name: _np.ascontiguousarray(value) for name, value in inputs.items()}
    arrays["constants"] = constants()
    aps = {name: nc.dram_tensor(f"in_{name}", a.shape, _mybir.dt.from_np(a.dtype), kind="ExternalInput").ap()
           for name, a in arrays.items()}
    out = nc.dram_tensor("out", (1, SEQ, D), F32, kind="ExternalOutput").ap()
    build(nc, aps, out)
    r = _run(nc, [{f"in_{name}": a for name, a in arrays.items()}], core_ids=[0])
    return r.results[0]["out"]
```

```python
from contextlib import ExitStack

import numpy as np

import concourse.bass as bass
from concourse import mybir

F32 = mybir.dt.float32
F32R = mybir.dt.float32r
BF16 = mybir.dt.bfloat16
ACT = mybir.ActivationFunctionType
ALU = mybir.AluOpType
AX = mybir.AxisListType

P = 128
SEQ, D = 256, 1024
HALVES = SEQ // P
DC = D // P
HEADS, HD = 8, 64
WIDTH = HEADS * HD
EPS_RMS, EPS_LN = 1e-6, 1e-5
NEG = -1e30

POOL_WINDOWS = (2, 4, 8, 16)
GROUPS = len(POOL_WINDOWS)
ROPE1 = HD // 4 // 2
FF = 2816
FFC = FF // P
TAPS = 3

LAYERS = 2
Q_LORA, KV_LORA, KR = 384, 256, 32
QC, KVC = Q_LORA // P, KV_LORA // P
ROPE2 = KR // 2
MLA_D = HD + KR
IDX_HEADS, IDX_D = 8, 32
KEEP = SEQ // 4
AT_KVA = Q_LORA
AT_KR = AT_KVA + KV_LORA
AT_DQ = AT_KR + KR
AT_DK = AT_DQ + WIDTH
AT_DV = AT_DK + HD
AT_IQ = AT_DV + HD
AT_IK = AT_IQ + IDX_HEADS * IDX_D
AT_IW = AT_IK + IDX_D
IN2 = AT_IW + IDX_HEADS
EXPERTS, EGROUPS, EPG, TOP_E = 16, 4, 4, 2
SLOTS = 64
ELSEWHERE = 4096.0
FFE = 512
ALPHA = (2.0 * LAYERS) ** 0.25
SLOPES = [2.0 ** (-8.0 * h / HEADS) for h in range(1, HEADS + 1)]
SC1 = HD ** -0.5
SC_MLA = MLA_D ** -0.5
SC_DSA = HD ** -0.5
N_FIRST, N_PARAMS = 7, 8
L_O_AFTER = (15,)
TAKEN = -3e38

RING = 3
SLAB = 2048

S_QK, S_VU, S_GATE, S_BA, S_BP, S_OUT = 0, 4, 8, 16, 18, 20
S_FFN = 24
S_FFN_LOOP = S_FFN + 2
N_FF = FFC // 2
S_BLOCK2 = S_FFN + 3 * N_FF
L_IN, L_IN_B, L_IN_C, L_QUP, L_UK, L_UV, L_O, L_MOE = 0, 4, 6, 7, 9, 10, 11, 15
PER_EXPERT = 6
PER_ROUND = PER_EXPERT * EXPERTS
PER_LAYER = L_MOE + PER_ROUND
S_SECOND = S_BLOCK2 + PER_LAYER
S_END = S_BLOCK2 + LAYERS * PER_LAYER


def in_wide_ring(n):
    return n >= S_BLOCK2 and (n - S_BLOCK2) % PER_LAYER >= L_O


def slot_of(n):
    if in_wide_ring(n):
        return ((n - S_BLOCK2) % PER_LAYER - L_MOE) % (2 * RING)
    return n % RING


def last_in_slot(n):
    first = n - (n - S_BLOCK2) % PER_LAYER + L_O
    if not in_wide_ring(n):
        return n - (2 * RING if n >= S_SECOND and n - S_SECOND < RING else RING) if n >= RING else None
    if n >= first + 4:
        return n - 2 * RING
    return n - RING if slot_of(n) < RING else None


def nth_in_slot(n):
    start = S_SECOND if n >= S_SECOND else 0
    return sum(slot_of(m) == slot_of(n) for m in range(start, n + 1))

C_ID = 0
C_MASK = C_ID + P
C_DIST = C_MASK + HALVES * SEQ
C_COS1 = C_DIST + HALVES * SEQ
C_SIN1 = C_COS1 + HALVES * ROPE1
C_COS2 = C_SIN1 + HALVES * ROPE1
C_SIN2 = C_COS2 + HALVES * ROPE2
C_TRI = C_SIN2 + HALVES * ROPE2
C_BEFORE = C_TRI + EPG * EPG
C_ONE = C_BEFORE + P
C_IOTA = C_ONE + 1
C_FULL = C_IOTA + SLOTS
C_FOLD = C_FULL + SEQ // SLOTS - 1
C_KEPT = C_FOLD + EXPERTS
C_BAND = C_KEPT
C_N = C_BAND + GROUPS * HALVES * SEQ

V_G1 = 0
V_BG = V_G1 + DC
V_G2 = V_BG + 2 * DC
V_PS = V_G2 + DC
V_QA = V_PS + GROUPS
V_KVA = V_QA + LAYERS * QC
V_N = V_KVA + LAYERS * KVC

SEMAPHORES = """x_in first_in params_in ln_in out_stored
 raw_in0 raw_in1 raw_in2 raw_in3 raw_in4 raw_in5 hi_done lo_done slab_used
 raw_in0_b raw_in1_b raw_in2_b raw_in3_b raw_in4_b raw_in5_b hi_done_b lo_done_b slab_used_b
 fills_set turned_params params_copied
 squares_summed mean_square rstd_ready normed
 fm_turned fm_hi fm_lo
 qk_saved0 qk_saved1 vu_saved0 vu_saved1 gates_saved
 qk_squared qk_summed qk_scaled qk_gained rope_products rope_summed
 pairs_turned pairs_copied pooled_summed pooled_copied mixed_summed mixed_hi mixed_lo
 a_gated b_gated ab_summed x_updated
 scores logits bias_ready probs flipped probs_turned weighted sums_inverted heads_saved
 acc_closed tap2_g tap2_v tap1_g tap1_v taps_g taps_v silu_done act_ready act_hi act_lo
 in_saved0 in_saved1 qup_saved0 qup_saved1 uk_saved0 uk_saved1 uv_saved0 uv_saved1 pads_zero
 kr_spread turned_a copied_q copied_k stage_zero staged turned_b copied_even copied_odd
 idx_scores idx_relu idx_weights idx_added idx_masked topk_step sel_step
 ln_added ln_mean_step ln_scaled ln_done
 router_w_hi router_w_lo router_parts parts_copied router_logits router_exp router_step routed counted places_step rounds_known rows_hi rows_lo""".split()
SEMAPHORES += [f"{name}_{layer}" for layer in range(LAYERS) for name in """
 one_hot places_moved gathered xg_hi xg_lo gate_low gate_added silu_done up_low up_added act_gated
 act_turned act_hi act_lo dispatched dispatch_copied expert_out""".split()]


def constants():
    c = np.zeros((P, C_N), np.float32)
    c[:, C_ID:C_ID + P] = np.eye(P)
    t = np.arange(SEQ)
    for half in range(HALVES):
        q = half * P + np.arange(P)
        at = half * SEQ
        c[:, C_MASK + at:C_MASK + at + SEQ] = np.where(t[None, :] <= q[:, None], 0.0, NEG)
        c[:, C_DIST + at:C_DIST + at + SEQ] = t[None, :] - q[:, None]
        for g, w in enumerate(POOL_WINDOWS):
            s = q
            inside = (s[:, None] <= t[None, :]) & (s[:, None] > t[None, :] - w)
            band = inside / np.minimum(t + 1.0, w)[None, :] - (s[:, None] == t[None, :])
            at = C_BAND + (g * HALVES + half) * SEQ
            c[:, at:at + SEQ] = band
        for n, theta, ccos, csin in ((ROPE1, 500000.0, C_COS1, C_SIN1), (ROPE2, 10000.0, C_COS2, C_SIN2)):
            inv = (np.float32(theta) ** (-np.arange(n, dtype=np.float32) / np.float32(n))).astype(np.float32)
            ang = q.astype(np.float32)[:, None] * inv[None, :]
            c[:, ccos + half * n:ccos + (half + 1) * n] = np.cos(ang)
            c[:, csin + half * n:csin + (half + 1) * n] = np.sin(ang)
    for e in range(EPG):
        for j in range(e):
            c[:, C_TRI + e * EPG + j] = 1.0
    c[:, C_BEFORE:C_ONE] = np.arange(P)[:, None] < np.arange(P)[None, :]
    c[:, C_ONE] = 1.0
    c[:, C_IOTA:C_FULL] = np.arange(SLOTS)
    c[:, C_FULL:C_FOLD] = SLOTS * np.arange(1, SEQ // SLOTS)
    for part in range(2):
        c[part * EXPERTS:(part + 1) * EXPERTS, C_FOLD:C_KEPT] = np.eye(EXPERTS)
    return c


class Waits:

    def __init__(self, eng, sems):
        self.eng, self.sems, self.count = eng, sems, {}

    def next(self, name, k=1):
        self.count[name] = self.count.get(name, 0) + k
        self.eng.wait_ge(self.sems[name], self.count[name])

    def skip(self, name, k=1):
        self.count[name] = self.count.get(name, 0) + k

    def upto(self, name, n):
        if n > 0:
            self.eng.wait_ge(self.sems[name], n)


def build(nc, A, out):
    ctx = ExitStack()
    with ctx:
        def sb(name, shape, dt=F32):
            return ctx.enter_context(nc.sbuf_tensor(name, shape, dt))

        S = {name: ctx.enter_context(nc.semaphore(name)) for name in SEMAPHORES}
        bank = [ctx.enter_context(nc.psum_tensor(f"bank{i}", [P, 512], F32)) for i in range(8)]

        const = sb("const", [P, C_KEPT])
        vec = sb("vec", [P, V_N])
        conv = sb("conv", [P, TAPS + 1, 2 * FFC])
        router_w = sb("router_w", [P, DC, EXPERTS])
        router_b = sb("router_b", [P, EXPERTS])
        power = sb("power", [P, HALVES * 2 * HEADS])
        zeros = sb("zeros", [P, P], BF16)

        x = sb("x", [P, HALVES, D])
        xn = sb("xn", [P, HALVES, D])
        xs = sb("xs", [P, DC, 2 * SEQ], F32R)
        raw = sb("raw", [P, RING, SLAB])
        hi = sb("hi", [P, RING, SLAB], F32R)
        lo = sb("lo", [P, RING, SLAB], F32R)
        proj = sb("proj", [P, HALVES, IN2])
        gates = sb("gates", [P, 2 * DC, SEQ])
        wide_a = sb("wide_a", [P, HALVES * D])
        wide_b = sb("wide_b", [P, HALVES * D])
        value = sb("value", [P, HALVES, WIDTH])
        q_t = sb("q_t", [P, HEADS, SEQ])
        k_t = sb("k_t", [P, HEADS, SEQ])
        xg = sb("xg", [P, EPG, DC, 2 * SLOTS], F32R)
        act_t = sb("act_t", [P, FFE // P, 2 * SLOTS], F32R)
        one_hot = sb("one_hot", [P, HALVES, EPG, 2 * SLOTS], F32R)
        slot_gate = sb("slot_gate", [P, 2])
        rounds = sb("rounds", [P, 1], mybir.dt.int32)
        logit = sb("logit", [P, 2, SEQ])
        prob = sb("prob", [P, 2, SEQ])
        prob_t = sb("prob_t", [P, 2, HALVES, P])
        bias_h = sb("bias_h", [P, 2, SEQ])
        row_min = sb("row_min", [P, 2 * HEADS])
        row_sum = sb("row_sum", [P, 2 * HEADS])
        row_inv = sb("row_inv", [P, 2 * HEADS])
        stat = sb("stat", [P, 3, HALVES * 2 * HEADS])
        best = power[:, 8:16]
        idx_w = sb("idx_w", [P, HALVES, IDX_HEADS])
        route = sb("route", [P, 8, HALVES * EXPERTS])

        ident = const[:, C_ID:C_ID + P]
        mask = const[:, C_MASK:C_DIST].rearrange("p (a t) -> p a t", a=HALVES)
        dist = const[:, C_DIST:C_COS1].rearrange("p (a t) -> p a t", a=HALVES)
        one = const[:, C_ONE:C_ONE + 1]
        before = const[:, C_BEFORE:C_BEFORE + P]

        def table(at, n):
            return const[:, at:at + HALVES * n].rearrange("p (a n) -> p a n", a=HALVES)

        cos1, sin1 = table(C_COS1, ROPE1), table(C_SIN1, ROPE1)
        cos2, sin2 = table(C_COS2, ROPE2), table(C_SIN2, ROPE2)
        tri = const[:, C_TRI:C_BEFORE].rearrange("p (e j) -> p e j", e=EPG)

        rows = gates[0:V_N, 0, 0:P]
        conv_rows = gates[0:2 * FFC, 2:4, :].rearrange("c a (b p) -> c (a b) p", p=P)
        qk = proj[:].rearrange("p a n -> p (a n)")[:, 0:HALVES * D].rearrange("p (a n) -> p a n", a=HALVES)
        band = wide_b[:].rearrange("p (g a t) -> p g a t", g=GROUPS, a=HALVES)
        head_gain = prob_t[:, 0, 0, :].rearrange("p (i d) -> p i d", i=2)
        w_pool = q_t[:, 0:2, :].rearrange("p a (b d) -> p (a b) d", d=P)
        act_s = xg[:].rearrange("p e c s -> p (e c s)")[:, 0:8 * SEQ]\
            .rearrange("p (b c s) -> p b c s", b=2, c=2)
        vu = wide_a[:].rearrange("p (a n) -> p a n", a=HALVES)
        mix = wide_b[:].rearrange("p (c t) -> p c t", c=DC)
        pooled = value[:].rearrange("p a n -> p (a n)").rearrange("p (g t) -> p g t", g=GROUPS)
        q_up = wide_a[:].rearrange("p (a h d) -> p a h d", a=HALVES, h=HEADS)
        k_up = wide_b[:].rearrange("p (a h d) -> p a h d", a=HALVES, h=HEADS)
        ln_gb = wide_a[:].rearrange("p (g n) -> p g n", g=2)
        stage = k_t[:].rearrange("p h t -> p (h t)")[:, 0:HALVES * 6 * P]\
            .rearrange("p (a v n) -> p a v n", a=HALVES, v=6)
        T_DQ, T_DK, T_IK, T_IQ = 0, 4, 6, 10
        sparse_t = gates[:, 0:12, :]
        spare = gates[:, 12:16, :].rearrange("p a n -> p (a n)")
        sel_score = bias_h
        y = proj[:].rearrange("p a n -> p (a n)")[:, 0:4 * SEQ].rearrange("p (s c t) -> p s c t", s=2, c=2)

        x_rows = xs[:].rearrange("p c s -> p (c s)").rearrange("p (v a n) -> p v a n", v=2, a=HALVES)
        flat = proj[:].rearrange("p a n -> p (a n)")
        low_g, low_u, hg, hu, act_e = (flat[0:SLOTS, FFE * i:FFE * (i + 1)] for i in range(5))
        expert_out = gates[:, 0:4, :].rearrange("p a n -> p (a n)").rearrange("p (b n) -> p b n", b=2)
        slot_to_token = gates[:, 4:6, :]
        place = route[:, 3, :]
        router_s = xg[:, 0]
        logit_parts = logit[0:2 * EXPERTS, 0, :]
        route4 = value[:, 0, :].rearrange("p (i n) -> p i n", i=2)[:, :, 0:HALVES * EGROUPS * EPG * EPG]

        def slab_of(tile, n, k):
            return lambda width: tile[:, n % RING, 0:k * width].rearrange("p (k n) -> p k n", k=k)

        raw_slots = [raw[:, i, :] for i in range(RING)]
        raw_slots += [q_t[:].rearrange("p h t -> p (h t)"), k_t[:].rearrange("p h t -> p (h t)"), wide_b[:]]

        def count(n, j=None, per=0):
            return n if j is None else j * per + n

        def layer_base(layer):
            return S_BLOCK2 + layer * PER_LAYER

        def ring(name, n):
            return (S[name + "_b"], n - S_SECOND) if n >= S_SECOND else (S[name], n)

        def wait_slab(eng, name, n, j=None, per=0):
            sem, local = ring(name, n)
            eng.wait_ge(sem, count(local + 1, j, per))

        def wait_raw(eng, n, j=None, per=0):
            sem, _ = ring(f"raw_in{slot_of(n)}", n)
            eng.wait_ge(sem, 16 * count(nth_in_slot(n), j, per // (2 * RING if in_wide_ring(n) else RING)))

        def wait_slot(eng, name, n, j=None, per=0, more=None):
            sem, local = ring(name, n)
            if j is not None or local >= RING:
                eng.wait_ge(sem, count(local - RING + 1, j, per))
            elif n >= S_SECOND:
                eng.wait_ge(S[name], more * PER_ROUND + (n - RING + 1))

        def further_rounds(eng, layer):
            eng.wait_ge(S["rounds_known"], layer + 1)
            return eng.value_load(rounds[0:1, 0:1], min_val=0, max_val=SEQ // SLOTS - 1)

        class Visits:

            def __init__(self, eng, layer):
                self.eng, self.layer = eng, layer

            def sem(self, name):
                return S[f"{name}_{self.layer}"]

            def upto(self, name, v, j, k=1):
                n = k * (v + 1)
                if j is None and n > 0:
                    self.eng.wait_ge(self.sem(name), n)
                elif j is not None:
                    self.eng.wait_ge(self.sem(name), j * (EPG * k) + n)

            def groups(self, name, j, n, k):
                if j is not None or n > 0:
                    self.eng.wait_ge(self.sem(name), n if j is None else j * k + n)

        def over_experts(eng, layer, start, group, finish):
            def one_round(j0):
                start(j0)
                group(0, j0, True)
                with eng.Fori(1, EGROUPS) as g:
                    group(g, g if j0 is None else j0 + g, False)
                finish(EGROUPS - 1 if j0 is None else j0 + (EGROUPS - 1), j0)

            one_round(None)
            more = further_rounds(eng, layer)
            with eng.If(more > 0):
                with eng.Fori(0, more) as rr:
                    one_round(rr * EGROUPS + EGROUPS)
            return more

        def first_slab(i, first):
            return 0 if first and i == 0 else PER_EXPERT * i - 2

        GROUP_SLABS = EPG * PER_EXPERT

        block = ctx.enter_context(nc.Block())

        @block.sync
        def _(sp):
            more = None

            def load(n, src, j=None, per=0):
                k, width = src.shape[1], src.shape[2]
                last = last_in_slot(n)
                if j is not None or last is not None and (last >= S_SECOND or n < S_SECOND):
                    sem, local = ring("lo_done", n)
                    last_local = local - (2 * RING if in_wide_ring(n) else RING)
                    if last is not None and j is None:
                        last_local = ring("lo_done", last)[1]
                    sp.wait_ge(sem, count(last_local + 1, j, per))
                elif last is not None:
                    sp.wait_ge(S["lo_done"], more * PER_ROUND + (last + 1))
                dst = raw_slots[slot_of(n)][:, 0:k * width].rearrange("p (k n) -> p k n", k=k)
                sp.dma_start(dst, src).then_inc(ring(f"raw_in{slot_of(n)}", n)[0], 16)

            def rows_of(w, k0, k, c0, width):
                return w[k0 * P:(k0 + k) * P, c0:c0 + width].rearrange("(k p) n -> p k n", p=P)

            w_in, w_up, w_down = A["w_in"][0], A["w_up"][0], A["w_down"][0]
            for i in range(HALVES):
                sp.dma_start(x[:, i, :], A["x"][0, i * P:(i + 1) * P, :]).then_inc(S["x_in"], 16)
            for g in range(2):
                for i in range(4):
                    load(S_QK + 4 * g + i, rows_of(w_in, 2 * i, 2, D * g, D))
            for i in range(8):
                load(S_GATE + i, rows_of(w_in, 0, DC, 2 * D + 256 * i, 256))
            for i in range(2):
                load(S_BA + i, rows_of(A["w_branch_attn"][0], 0, 4, 512 * i, 512))
            for i in range(2):
                load(S_BP + i, rows_of(A["w_branch_pool"][0], 0, 4, 512 * i, 512))
            for i in range(4):
                load(S_OUT + i, rows_of(A["w_out"][0], 2 * i, 2, 0, D))

            up_steps = w_up.rearrange("(k p) (s j n) -> s j p k n", p=P, s=2, j=N_FF)
            down_steps = w_down.rearrange("(j k p) n -> j p k n", p=P, k=2)
            load(S_FFN, up_steps[0, 0])
            load(S_FFN + 1, up_steps[1, 0])
            with sp.Fori(0, (N_FF - 1) // 2) as jj:
                for s in range(2):
                    n = S_FFN_LOOP + 3 * s
                    j = jj * 2 + (1 + s)
                    load(n, up_steps[0, j], jj, 6)
                    load(n + 1, up_steps[1, j], jj, 6)
                    load(n + 2, down_steps[jj * 2 + s], jj, 6)
            load(S_BLOCK2 - 1, down_steps[N_FF - 1])

            for layer in range(LAYERS):
                b = layer_base(layer)
                w = A["w_in_2"][layer]
                for i in range(4):
                    load(b + L_IN + i, rows_of(w, 2 * i, 2, 0, D))
                for i in range(2):
                    load(b + L_IN_B + i, rows_of(w, 4 * i, 4, D, 512))
                load(b + L_IN_C, rows_of(w, 0, DC, D + 512, IN2 - D - 512))
                for i in range(2):
                    load(b + L_QUP + i, rows_of(A["w_q_up_2"][layer], 0, QC, 4 * MLA_D * i, 4 * MLA_D))
                load(b + L_UK, rows_of(A["w_uk_2"][layer], 0, KVC, 0, WIDTH))
                load(b + L_UV, rows_of(A["w_uv_2"][layer], 0, KVC, 0, WIDTH))
                for i in range(4):
                    if i == 1:
                        sp.wait_ge(S["heads_saved"], HALVES * (2 * layer + 2))
                    load(b + L_O + i, rows_of(A["w_o_2"][layer], 2 * i, 2, 0, D))
                gate_w = A["w_gate_2"][layer].rearrange("e (h k p) n -> e h p k n", p=P, h=2)
                up_w = A["w_up_2"][layer].rearrange("e (h k p) n -> e h p k n", p=P, h=2)
                down_w = A["w_down_2"][layer].rearrange("e (h k p) n -> e h p k n", p=P, h=2)
                base = b + L_MOE

                def start(j):
                    pass

                def group(g, j, first):
                    for i in range(EPG):
                        n = base + first_slab(i, first)
                        slabs = [(gate_w, 0), (up_w, 0)] + ([] if first and i == 0 else [(down_w, -1)])
                        for at, (w, back) in enumerate(slabs):
                            for h in range(2):
                                load(n + 2 * at + h, w[g * EPG + (i + back), h], j, GROUP_SLABS)

                def finish(j, j0):
                    n = base + PER_ROUND - 2
                    for h in range(2):
                        load(n + h, down_w[EXPERTS - 1, h], j0, GROUP_SLABS)

                more = over_experts(sp, layer, start, group, finish)
            sp.wait_ge(S["ln_done"], 2 * HALVES * LAYERS)
            for i in range(HALVES):
                sp.dma_start(out[0, i * P:(i + 1) * P, :], x[:, i, :]).then_inc(S["out_stored"], 16)
            sp.wait_ge(S["out_stored"], 16 * HALVES)

        @block.gpsimd
        def _(pool):
            w = Waits(pool, S)
            nc.gpsimd.memset(power[:], -0.5).then_inc(S["fills_set"], 1)
            nc.gpsimd.memset(zeros[:], 0.0).then_inc(S["fills_set"], 1)
            nc.gpsimd.memset(k_t[:], 0.0).then_inc(S["fills_set"], 1)
            w.next("fills_set", 3)

            def root(n):
                w.next("mean_square")
                nc.gpsimd.tensor_tensor(stat[:, 2, 0:n], stat[:, 1, 0:n], power[:, 0:n], ALU.pow)\
                    .then_inc(S["rstd_ready"], 1)

            def load_ln(gain, shift):
                pool.dma_start(ln_gb[:, 0, :], gain.partition_broadcast(P)).then_inc(S["ln_in"], 16)
                pool.dma_start(ln_gb[:, 1, :], shift.partition_broadcast(P)).then_inc(S["ln_in"], 16)

            root(HALVES)
            root(HALVES * 2 * HEADS)
            root(HALVES)
            for layer in range(LAYERS):
                root(2 * HALVES)
                if layer == 0:
                    pool.wait_ge(S["x_updated"], 8)
                else:
                    pool.wait_ge(S["ln_done"], 2 * HALVES * layer)
                nc.gpsimd.memset(q_up[:, :, :, MLA_D:P], 0.0).then_inc(S["pads_zero"], 1)
                nc.gpsimd.memset(k_up[:, :, :, MLA_D:P], 0.0).then_inc(S["pads_zero"], 1)
                nc.gpsimd.memset(stage, 0.0).then_inc(S["stage_zero"], 1)
                w.next("stage_zero")
                w.next("in_saved0", 3)
                w.next("in_saved1", 5)
                for v in range(2):
                    nc.gpsimd.tensor_copy(stage[:, :, v, HD * v:HD * (v + 1)], proj[:, :, AT_DK:AT_DK + HD])\
                        .then_inc(S["staged"], 1)
                for v in range(4):
                    nc.gpsimd.tensor_copy(stage[:, :, 2 + v, IDX_D * v:IDX_D * (v + 1)],
                                          proj[:, :, AT_IK:AT_IK + IDX_D]).then_inc(S["staged"], 1)
                w.next("turned_a", 8)
                load_ln(A["ln1_g_2"][layer], A["ln1_b_2"][layer])
                root(HALVES)
                pool.wait_ge(S["ln_done"], 2 * HALVES * layer + HALVES)
                load_ln(A["ln2_g_2"][layer], A["ln2_b_2"][layer])
                root(HALVES)

        @block.scalar
        def _(act):
            w = Waits(act, S)
            split = [0]

            more = None

            def split_hi(n, j=None, per=0, size=SLAB):
                wait_raw(act, n, j, per)
                wait_slot(act, "slab_used", n, j, per, more)
                nc.scalar.copy(hi[:, n % RING, 0:size], raw_slots[slot_of(n)][:, 0:size])\
                    .then_inc(ring("hi_done", n)[0], 1)

            def splits_to(n):
                while split[0] <= min(n, S_END - 1):
                    m = split[0]
                    short = (m - S_BLOCK2) % PER_LAYER if m >= S_BLOCK2 else -1
                    size = {L_IN_C: DC * (IN2 - D - 512), L_UK: 1024, L_UV: 1024}.get(short, SLAB)
                    size = 3 * 4 * MLA_D if short in (L_QUP, L_QUP + 1) else size
                    split_hi(m, size=size)
                    split[0] += 1

            def params():
                loads = [(const[:], A["constants"][:, 0:C_KEPT]),
                         (rows[V_G1:V_BG, :], A["norm_mix_g"][0].rearrange("(c p) -> c p", p=P)),
                         (rows[V_BG:V_G2, :], A["b_gate"][0].rearrange("(c p) -> c p", p=P)),
                         (rows[V_G2:V_PS, :], A["norm_ffn_g"][0].rearrange("(c p) -> c p", p=P)),
                         (rows[V_PS:V_QA, :], A["pool_scale"][0].rearrange("(c p) -> c p", p=P)),
                         (rows[V_QA:V_KVA, :], A["q_norm_g_2"].rearrange("l (c p) -> (l c) p", p=P)),
                         (rows[V_KVA:V_N, :], A["kv_norm_g_2"].rearrange("l (c p) -> (l c) p", p=P)),
                         (wide_b[:], A["constants"][:, C_BAND:C_N]),
                         (conv_rows[:, 0:TAPS, :], A["conv_w"][0].rearrange("t (c p) -> c t p", p=P)),
                         (conv_rows[:, TAPS, :], A["conv_b"][0].rearrange("(c p) -> c p", p=P)),
                         (head_gain[:, 0, :], A["q_norm_g"][0].partition_broadcast(P)),
                         (head_gain[:, 1, :], A["k_norm_g"][0].partition_broadcast(P)),
                         (w_pool, A["w_pool"][0].rearrange("g c d -> c g d")),
                         (router_w[:], A["router_w_2"].rearrange("(k p) e -> p k e", p=P)),
                         (router_b[:], A["router_bias_2"].partition_broadcast(P))]
                for i, (dst, src) in enumerate(loads):
                    act.dma_start(dst, src).then_inc(S["first_in" if i < N_FIRST else "params_in"], 16)

            def squares(sources, scratch, after=None):
                for i, src in enumerate(sources):
                    if after:
                        after(i)
                    nc.scalar.activation(scratch(i), src, ACT.Square, accum_out=stat[:, 0, i:i + 1])\
                        .then_inc(S["squares_summed"], 1)

            def centred_squares():
                w.next("ln_mean_step", 2)
                for i in range(HALVES):
                    nc.scalar.activation(flat[:, i * D:(i + 1) * D], x[:, i, :], ACT.Square, bias=stat[:, 1, 2 + i:3 + i],
                                         accum_out=stat[:, 0, 4 + i:5 + i]).then_inc(S["squares_summed"], 1)

            fm = [0]

            def feature_major(chunks, gain=None):
                for b in range(0, chunks, 2):
                    k = min(2, chunks - b)
                    w.next("fm_turned")
                    src = bank[6 + fm[0] % 2][:, 0:k * SEQ].rearrange("p (c t) -> p c t", c=k)
                    if gain is None:
                        nc.scalar.copy(xs[:, b:b + k, 0:SEQ], src).then_inc(S["fm_hi"], 1)
                    else:
                        for c in range(k):
                            nc.scalar.activation(xs[:, b + c, 0:SEQ], src[:, c, :], ACT.Copy,
                                                 scale=vec[:, gain(b + c):gain(b + c) + 1]).then_inc(S["fm_hi"], 1)
                    fm[0] += 1

            units = [0]

            def attention(after=None):
                base = units[0]

                def exps(i):
                    act.wait_ge(S["logits"], base + i + 1)
                    w.upto("flipped", base + i - 1)
                    keys = P * (i // HEADS + 1)
                    nc.scalar.activation(prob[:, i % 2, 0:keys], logit[:, i % 2, 0:keys], ACT.Exp,
                                         bias=row_min[:, i:i + 1], scale=-1.0,
                                         accum_out=row_sum[:, i:i + 1]).then_inc(S["probs"], 1)

                def turned(i):
                    act.wait_ge(S["flipped"], base + i + 1)
                    w.upto("weighted", base + i - 1)
                    nk = i // HEADS + 1
                    nc.scalar.copy(prob_t[:, i % 2, 0:nk, :],
                                   bank[2 + i % 2][:, 0:nk * P].rearrange("p (k q) -> p k q", k=nk))\
                        .then_inc(S["probs_turned"], 1)

                for i in range(2 * HEADS + 2):
                    if i < 2 * HEADS:
                        exps(i)
                    if i >= 2:
                        turned(i - 2)
                    if after:
                        after(i)
                units[0] += 2 * HEADS

            def save_half(n, name, saves):
                wait_slab(act, "slab_used", n)
                for dst, src in saves:
                    nc.scalar.copy(dst, src).then_inc(S[name], 1)

            params()
            act.wait_ge(S["x_in"], 16 * HALVES)
            squares([x[:, i, :] for i in range(HALVES)], lambda i: xn[:, i, :])
            w.next("turned_params")
            nc.scalar.copy(vec[:], bank[0][:, 0:V_N]).then_inc(S["params_copied"], 1)
            w.next("params_copied")
            feature_major(DC, lambda c: V_G1 + c)
            w.next("turned_params")
            nc.scalar.copy(conv[:].rearrange("p t c -> p (t c)"), bank[1][:, 0:(TAPS + 1) * 2 * FFC])\
                .then_inc(S["params_copied"], 1)
            splits_to(S_QK + 5)
            save_half(S_QK + 3, "qk_saved0", [(qk[:, 0, 512 * i:512 * (i + 1)], bank[i][:]) for i in range(2)])
            splits_to(S_VU + 5)
            save_half(S_VU + 3, "vu_saved0", [(vu[:, 0, 512 * i:512 * (i + 1)], bank[4 + i][:]) for i in range(2)])
            for i in range(8):
                splits_to(S_GATE + i + 2)
                act.wait_ge(S["slab_used"], S_GATE + i + 1)
                for c in range(2):
                    nc.scalar.activation(gates[:, 2 * i + c, :], bank[i % 4][:, c * SEQ:(c + 1) * SEQ], ACT.Sigmoid,
                                         bias=vec[:, V_BG + 2 * i + c:V_BG + 2 * i + c + 1])\
                        .then_inc(S["gates_saved"], 1)
            w.next("pooled_summed")
            for i in range(2):
                nc.scalar.copy(pooled[:, 2 * i:2 * i + 2, :],
                               bank[4 + i][:].rearrange("p (g t) -> p g t", g=2)).then_inc(S["pooled_copied"], 1)
            w.next("mixed_summed")
            for g in range(GROUPS):
                nc.scalar.activation(xs[:, 4 + g, 0:SEQ], bank[6 + g // 2][:, (g % 2) * SEQ:(g % 2 + 1) * SEQ],
                                     ACT.Copy, scale=vec[:, V_PS + g:V_PS + g + 1]).then_inc(S["mixed_hi"], 1)
            act.wait_ge(S["fills_set"], 3)
            for b in range(4):
                w.next("pairs_turned")
                src = bank[b % 2][:].rearrange("p (c t) -> p c t", c=2)
                if b < 2:
                    nc.scalar.copy(q_t[:, 2 * b:2 * b + 2, :], src).then_inc(S["pairs_copied"], 1)
                else:
                    for odd in range(2):
                        part = slice(HD * odd, HD * (odd + 1))
                        first = 4 * (b - 2) + odd
                        nc.scalar.copy(k_t[part, first:first + 3:2, :], src[part]).then_inc(S["pairs_copied"], 1)
            splits_to(S_BA + 2)
            attention()
            feature_major(4)
            splits_to(S_OUT + 1)
            for i in range(4):
                w.next("ab_summed")
                nc.scalar.copy(xs[:, 2 * i:2 * i + 2, 0:SEQ], mix[:, 2 * i:2 * i + 2, :]).then_inc(S["mixed_hi"], 1)
            splits_to(S_OUT + 3)
            w.next("x_updated", 4)
            squares([x[:, i, :] for i in range(HALVES)], lambda i: xn[:, i, :])
            splits_to(S_FFN)
            feature_major(DC, lambda c: V_G2 + c)

            def ffn_step(n, par, j, jj=None):
                first = jj is None
                split_hi(n + 1, jj, 6)
                split_hi(n + 2, jj, 6)
                for side, name in ((0, "tap2_g"), (1, "tap2_v")):
                    if side and not first:
                        split_hi(n + 3, jj, 6)
                    act.wait_ge(S["slab_used"], count(n + side + 1, jj, 6))
                    if not first:
                        act.wait_ge(S["act_lo"], j)
                    for c in range(2):
                        at = j * 2 + side * FFC + c
                        nc.scalar.activation(y[:, side, c, :], bank[side][:, c * SEQ:(c + 1) * SEQ], ACT.Identity,
                                             bias=conv[:, TAPS, bass.ds(at, 1)],
                                             scale=conv[:, 2, bass.ds(at, 1)]).then_inc(S[name], 1)
                act.wait_ge(S["taps_g"], j * 2 + 2)
                nc.scalar.activation(y[:, 0, :, :], y[:, 0, :, :], ACT.Silu).then_inc(S["silu_done"], 1)
                act.wait_ge(S["act_ready"], j + 1)
                nc.scalar.copy(act_s[:, par, :, 0:SEQ], y[:, 1, :, :]).then_inc(S["act_hi"], 1)

            ffn_step(S_FFN, 0, 0)
            with act.Fori(0, (N_FF - 1) // 2) as jj:
                for s in range(2):
                    ffn_step(S_FFN_LOOP + 3 * s, (1 + s) % 2, jj * 2 + (1 + s), jj)
            split[0] = S_BLOCK2
            splits_to(S_BLOCK2 + L_IN + 1)

            for layer in range(LAYERS):
                b = layer_base(layer)
                feature_major(DC)
                splits_to(b + L_IN + 5)
                save_half(b + L_IN + 3, "in_saved0",
                          [(proj[:, 0, 512 * i:512 * (i + 1)], bank[i][:]) for i in range(2)])
                splits_to(b + L_IN_C + 1)
                save_half(b + L_IN_B + 1, "in_saved0", [(proj[:, 0, D:D + 512], bank[4][:])])
                w.next("in_saved0", 3)
                parts = [(i, at, n) for at, n in ((0, Q_LORA), (AT_KVA, KV_LORA)) for i in range(HALVES)]
                squares([proj[:, i, at:at + n] for i, at, n in parts],
                        lambda k: xn[:, parts[k][0], parts[k][1]:parts[k][1] + parts[k][2]],
                        after=lambda k: w.next("in_saved1", 5) if k == 1 else None)
                feature_major(QC + KVC, lambda c: V_QA + QC * layer + c if c < QC else V_KVA + KVC * layer + c - QC)
                splits_to(b + L_UV)
                w.next("pads_zero", 2)
                for i in range(2):
                    save_half(b + L_QUP + i, "qup_saved0",
                              [(q_up[:, 0, 4 * i:4 * i + 4, 0:MLA_D],
                                bank[2 * i][:, 0:4 * MLA_D].rearrange("p (h d) -> p h d", h=4))])
                save_half(b + L_UK, "uk_saved0",
                          [(k_up[:, 0, :, 0:HD], bank[4][:].rearrange("p (h d) -> p h d", h=HEADS))])
                save_half(b + L_UV, "uv_saved0", [(value[:, 0, :], bank[6][:])])
                for i in range(3):
                    w.next("turned_b")
                    nc.scalar.copy(sparse_t[:, 4 * i:4 * i + 2, :],
                                   bank[6][:].rearrange("p (c t) -> p c t", c=2)).then_inc(S["copied_even"], 1)
                    w.skip("turned_b")
                n_idx = HALVES * IDX_HEADS
                for i in range(n_idx):
                    keys = P * (i // IDX_HEADS + 1)
                    w.next("idx_scores")
                    w.upto("idx_added", n_idx * layer + i - 1)
                    nc.scalar.activation(logit[:, i % 2, 0:keys], bank[i % 2][:, 0:keys], ACT.Relu,
                                         scale=IDX_D ** -0.5).then_inc(S["idx_relu"], 1)
                for i in range(4):
                    w.next("turned_a")
                    nc.scalar.copy(q_t[:, 2 * i:2 * i + 2, :], bank[6][:].rearrange("p (c t) -> p c t", c=2))\
                        .then_inc(S["copied_q"], 1)
                    w.skip("turned_a")
                attention()
                nc.scalar.copy(router_s[:, :, 0:EXPERTS], router_w[:]).then_inc(S["router_w_hi"], 1)
                attention(after=lambda i: splits_to(b + L_O + L_O_AFTER.index(i)) if i in L_O_AFTER else None)
                feature_major(DC)
                splits_to(b + L_O + 3)
                splits_to(b + L_MOE)
                centred_squares()
                feature_major(DC)
                splits_to(b + L_MOE + RING - 1)
                w.next("router_parts")
                nc.scalar.copy(logit_parts, bank[0][0:2 * EXPERTS, 0:SEQ]).then_inc(S["parts_copied"], 1)
                w.next("router_logits")
                nc.scalar.activation(route[:, 0, :], bank[1][:, 0:HALVES * EXPERTS], ACT.Exp, scale=-1.0)\
                    .then_inc(S["router_exp"], 1)
                nc.scalar.copy(x_rows[:, 0], x[:]).then_inc(S["rows_hi"], 1)
                base = b + L_MOE
                V = Visits(act, layer)

                def low_rows(dst, src, name):
                    nc.scalar.copy(dst, src[SLOTS:2 * SLOTS, :]).then_inc(V.sem(name), 1)

                def turned_hi(v, j):
                    V.upto("act_turned", v, j)
                    nc.scalar.copy(act_t[:, :, 0:SLOTS], bank[2][:, 0:4 * SLOTS].rearrange("p (c s) -> p c s", c=4))\
                        .then_inc(V.sem("act_hi"), 1)

                def out_copied(last_slab, j):
                    wait_slab(act, "slab_used", last_slab, j, GROUP_SLABS)
                    for i in range(2):
                        nc.scalar.copy(expert_out[:, i, :], bank[2 + i][:]).then_inc(V.sem("expert_out"), 1)

                def start(j):
                    pass

                def group(g, j, first):
                    if not first:
                        out_copied(base - 3, j)
                    for n in range(base, base if j is None else base + 3 if first else base + 1):
                        split_hi(n, j, GROUP_SLABS)
                    for f in range(4):
                        V.groups("gathered", j, f + 1, 4)
                        nc.scalar.copy(xg[:, :, 2 * f:2 * f + 2, 0:SLOTS],
                                       bank[f % 2][:].rearrange("p (c e s) -> p e c s", c=2, e=EPG))\
                            .then_inc(V.sem("xg_hi"), 1)
                    for i in range(EPG):
                        n = base + first_slab(i, first)
                        after = n + (4 if first and i == 0 else 6)
                        split_hi(n + 3, j, GROUP_SLABS)
                        wait_slab(act, "slab_used", n + 1, j, GROUP_SLABS)
                        V.upto("gate_added", i - 1, j)
                        low_rows(low_g, bank[0], "gate_low")
                        if after == n + 6:
                            split_hi(n + 4, j, GROUP_SLABS)
                        V.upto("gate_added", i, j)
                        nc.scalar.activation(hg, hg, ACT.Silu).then_inc(V.sem("silu_done"), 1)
                        if after == n + 6:
                            turned_hi(i - 1, j)
                        V.upto("dispatched", i, j)
                        nc.scalar.copy(slot_to_token[:, i % 2, :], bank[3][:, 0:SEQ])\
                            .then_inc(V.sem("dispatch_copied"), 1)
                        nc.scalar.copy(slot_gate[:, i % 2:i % 2 + 1], bank[3][:, bass.ds(g * EPG + (SEQ + i), 1)])\
                            .then_inc(V.sem("dispatch_copied"), 1)
                        if after == n + 6:
                            split_hi(n + 5, j, GROUP_SLABS)
                        split_hi(after, j, GROUP_SLABS)
                        wait_slab(act, "slab_used", n + 3, j, GROUP_SLABS)
                        low_rows(low_u, bank[1], "up_low")
                        split_hi(after + 1, j, GROUP_SLABS)
                        if i < EPG - 1:
                            if after == n + 6:
                                out_copied(n + 5, j)
                            split_hi(after + 2, j, GROUP_SLABS)

                def finish(j, j0):
                    out_copied(base + PER_ROUND - 3, j0)
                    turned_hi(EPG - 1, j)
                    out_copied(base + PER_ROUND - 1, j0)

                more = over_experts(act, layer, start, group, finish)
                split[0] = b + PER_LAYER
                splits_to(b + PER_LAYER + 1)
                centred_squares()

        @block.vector
        def _(dve):
            w = Waits(dve, S)
            split = [0]
            tt = nc.vector.tensor_tensor

            def split_lo(n, j=None, per=0, size=SLAB):
                wait_slab(dve, "hi_done", n, j, per)
                tt(lo[:, n % RING, 0:size], raw_slots[slot_of(n)][:, 0:size], hi[:, n % RING, 0:size].bitcast(F32),
                   ALU.subtract).then_inc(ring("lo_done", n)[0], 1)

            def splits_to(n):
                while split[0] <= min(n, S_END - 1):
                    m = split[0]
                    short = (m - S_BLOCK2) % PER_LAYER if m >= S_BLOCK2 else -1
                    size = {L_IN_C: DC * (IN2 - D - 512), L_UK: 1024, L_UV: 1024}.get(short, SLAB)
                    size = 3 * 4 * MLA_D if short in (L_QUP, L_QUP + 1) else size
                    split_lo(m, size=size)
                    split[0] += 1

            def mean_square(parts, eps, signals):
                if signals:
                    w.next("squares_summed", signals)
                for i, (at, k, n) in enumerate(parts):
                    ins = nc.vector.tensor_scalar(stat[:, 1, at:at + k], stat[:, 0, at:at + k], 1.0 / n, eps,
                                                  ALU.mult, ALU.add)
                    if i == len(parts) - 1:
                        ins.then_inc(S["mean_square"], 1)

            fm = [0]

            def feature_major(chunks, gain=None):
                for b in range(0, chunks, 2):
                    k = min(2, chunks - b)
                    w.next("fm_hi", 1 if gain is None else k)
                    src = bank[6 + fm[0] % 2][:, 0:k * SEQ].rearrange("p (c t) -> p c t", c=k)
                    if gain is None:
                        tt(xs[:, b:b + k, SEQ:2 * SEQ], src, xs[:, b:b + k, 0:SEQ].bitcast(F32), ALU.subtract)\
                            .then_inc(S["fm_lo"], 1)
                    else:
                        for c in range(k):
                            ins = nc.vector.scalar_tensor_tensor(
                                out=xs[:, b + c, SEQ:2 * SEQ], in0=src[:, c, :],
                                scalar=vec[:, gain(b + c):gain(b + c) + 1],
                                in1=xs[:, b + c, 0:SEQ].bitcast(F32), op0=ALU.mult, op1=ALU.subtract)
                        ins.then_inc(S["fm_lo"], 1)
                    fm[0] += 1

            def rotate(x1, x2, c, s, tmp, shape, step="rope"):
                c, s = (t.unsqueeze(2).broadcast_to(shape) for t in (c, s))
                for dst, a, t in ((0, x1, c), (1, x2, s), (2, x2, c), (3, x1, s)):
                    tt(tmp(dst), a, t, ALU.mult).then_inc(S["rope_products"], 1)
                w.next("rope_products", 4)
                tt(x1, tmp(0), tmp(1), ALU.subtract).then_inc(S["rope_summed"], 1)
                tt(x2, tmp(2), tmp(3), ALU.add).then_inc(S["rope_summed"], 1)

            units = [0]

            def attention(scale, col, sparse=False, before=None, after=None):
                base = units[0]

                def logits(i):
                    half, h = divmod(i, HEADS)
                    keys = P * (half + 1)
                    m = mask[:, half, 0:keys]
                    if sparse:
                        w.upto("logits", base + i - 1)
                        nc.vector.scalar_tensor_tensor(out=prob_bias(i, keys), in0=dist[:, half, 0:keys],
                                                       scalar=SLOPES[h] / scale, in1=sel_score[:, half, 0:keys],
                                                       op0=ALU.mult, op1=ALU.add).then_inc(S["bias_ready"], 1)
                        w.next("bias_ready")
                        m = prob_bias(i, keys)
                    dve.wait_ge(S["scores"], base + i + 1)
                    w.upto("probs", base + i - 1)
                    nc.vector.tensor_tensor_reduce(logit[:, i % 2, 0:keys], bank[i % 2][:, 0:keys], m, -scale, 3e38,
                                                   ALU.add, ALU.min, row_min[:, i:i + 1]).then_inc(S["logits"], 1)

                def save(half):
                    at = slice(HEADS * half, HEADS * (half + 1))
                    dve.wait_ge(S["probs"], base + HEADS * (half + 1))
                    nc.vector.reciprocal(row_inv[:, at], row_sum[:, at]).then_inc(S["sums_inverted"], 1)
                    w.next("sums_inverted")
                    dve.wait_ge(S["weighted"], base + HEADS * (half + 1))
                    tt(xn[:, half, col:col + WIDTH].rearrange("p (h d) -> p h d", h=HEADS),
                       bank[4 + half][:].rearrange("p (h d) -> p h d", h=HEADS),
                       row_inv[:, at].unsqueeze(2).broadcast_to([P, HEADS, HD]), ALU.mult)\
                        .then_inc(S["heads_saved"], 1)

                for i in range(2 * HEADS):
                    if before:
                        before(i)
                    logits(i)
                    if after:
                        after(i)
                    if i == HEADS + 4:
                        save(0)
                save(1)
                units[0] += 2 * HEADS

            def prob_bias(i, keys):
                return spare[:, (i % 2) * SEQ:(i % 2) * SEQ + keys]

            def save_half(n, name, saves):
                wait_slab(dve, "slab_used", n)
                for dst, src in saves:
                    nc.vector.tensor_copy(dst, src).then_inc(S[name], 1)

            def router():
                def step(ins):
                    ins.then_inc(S["router_step"], 1)
                    w.next("router_step")

                r = [route[:, i, :] for i in range(8)]
                n_groups = HALVES * EGROUPS

                def by_group(t):
                    return t.rearrange("p (g e) -> p g e", e=EPG)

                def against(t, n):
                    shape = [P, n, EPG, EPG]
                    return t.unsqueeze(3).broadcast_to(shape), t.unsqueeze(2).broadcast_to(shape)

                pairs = [route4[:, i, :].rearrange("p (g e j) -> p g e j", e=EPG, j=EPG) for i in range(2)]

                def tri_of(n):
                    return tri.unsqueeze(1).broadcast_to([P, n, EPG, EPG])

                w.next("router_exp")
                step(nc.vector.tensor_scalar(r[1], r[0], 1.0, None, ALU.add))
                step(nc.vector.reciprocal(r[2], r[1]))
                affinity, biased, sel = r[2], r[3], r[4]
                step(tt(biased.rearrange("p (a e) -> p a e", a=HALVES),
                        affinity.rearrange("p (a e) -> p a e", a=HALVES),
                        router_b[:].unsqueeze(1).broadcast_to([P, HALVES, EXPERTS]), ALU.add))
                own, other = against(by_group(biased), n_groups)
                nc.vector.tensor_tensor(pairs[0], other, own, ALU.is_gt)
                step(tt(pairs[1], other, own, ALU.is_equal))
                step(tt(pairs[1], pairs[1], tri_of(n_groups), ALU.mult))
                step(tt(pairs[0], pairs[0], pairs[1], ALU.add))
                step(nc.vector.tensor_reduce(by_group(r[5]), pairs[0], AX.X, ALU.add))
                step(nc.vector.tensor_scalar(sel, r[5], TOP_E - 0.5, None, ALU.is_lt))
                step(tt(r[5], sel, biased, ALU.mult))
                step(nc.vector.tensor_reduce(r[6][:, 0:n_groups], by_group(r[5]), AX.X, ALU.add))
                score = r[6][:, 0:n_groups].rearrange("p (a g) -> p a g", a=HALVES)
                top = r[6][:, n_groups:n_groups + HALVES]
                step(nc.vector.tensor_reduce(top, score, AX.X, ALU.max))
                is_top = r[7][:, 0:n_groups].rearrange("p (a g) -> p a g", a=HALVES)
                step(tt(is_top, score, top.unsqueeze(2).broadcast_to([P, HALVES, EGROUPS]), ALU.is_equal))
                few = pairs[0][:, 0:HALVES]
                step(tt(few, against(is_top, HALVES)[1], tri_of(HALVES), ALU.mult))
                earlier = r[7][:, n_groups:2 * n_groups].rearrange("p (a g) -> p a g", a=HALVES)
                step(nc.vector.tensor_reduce(earlier, few, AX.X, ALU.add))
                step(nc.vector.tensor_scalar(earlier, earlier, 0.5, None, ALU.is_lt))
                step(tt(is_top, is_top, earlier, ALU.mult))
                step(tt(by_group(sel), by_group(sel),
                        r[7][:, 0:n_groups].unsqueeze(2).broadcast_to([P, n_groups, EPG]), ALU.mult))
                step(tt(r[5], sel, affinity, ALU.mult))
                total = r[6][:, n_groups:n_groups + HALVES]
                halves = r[5].rearrange("p (a e) -> p a e", a=HALVES)
                step(nc.vector.tensor_reduce(total, halves, AX.X, ALU.add))
                step(nc.vector.reciprocal(r[6][:, 0:HALVES], total))
                tt(r[0].rearrange("p (a e) -> p a e", a=HALVES), halves,
                   r[6][:, 0:HALVES].unsqueeze(2).broadcast_to([P, HALVES, EXPERTS]), ALU.mult)\
                    .then_inc(S["routed"], 1)

            def places():
                def step(ins):
                    ins.then_inc(S["places_step"], 1)
                    w.next("places_step")

                n = HALVES * EXPERTS
                w.next("counted")
                step(nc.vector.tensor_scalar(route[:, 1, :], route[:, 4, :], -ELSEWHERE, ELSEWHERE,
                                             ALU.mult, ALU.add))
                step(tt(place, route[:, 1, :], bank[3][:, 0:n], ALU.add))
                step(nc.vector.tensor_reduce(route[:, 1, 0:1], bank[3][:, n:n + EXPERTS], AX.X, ALU.max))
                n_full = SEQ // SLOTS - 1
                step(tt(route[:, 1, 1:1 + n_full], route[:, 1, 0:1].broadcast_to([P, n_full]),
                        const[:, C_FULL:C_FOLD], ALU.is_gt))
                step(nc.vector.tensor_reduce(route[:, 1, 0:1], route[:, 1, 1:1 + n_full], AX.X, ALU.add))
                nc.vector.tensor_copy(rounds[:], route[:, 1, 0:1]).then_inc(S["rounds_known"], 1)

            def experts(b, layer):
                base = b + L_MOE
                V = Visits(dve, layer)

                def turned_lo(v, j):
                    V.upto("act_hi", v, j)
                    tt(act_t[:, :, SLOTS:2 * SLOTS], bank[2][:, 0:4 * SLOTS].rearrange("p (c s) -> p c s", c=4),
                       act_t[:, :, 0:SLOTS].bitcast(F32), ALU.subtract).then_inc(V.sem("act_lo"), 1)

                def slots_of(g):
                    at = [EXPERTS * half + EPG * g for half in range(HALVES)]
                    shape = [P, EPG, 2, SLOTS]
                    for half in range(HALVES):
                        own = place[:, bass.ds(at[half], EPG)]
                        tt(one_hot[:, half].rearrange("p e (v s) -> p e v s", v=2),
                           const[:, C_IOTA:C_IOTA + SLOTS].unsqueeze(1).unsqueeze(1).broadcast_to(shape),
                           own.unsqueeze(2).unsqueeze(2).broadcast_to(shape), ALU.is_equal).then_inc(V.sem("one_hot"), 1)

                def move_places(g, j):
                    V.groups("one_hot", j, HALVES, HALVES)
                    for half in range(HALVES):
                        own = place[:, bass.ds(EXPERTS * half + EPG * g, EPG)]
                        nc.vector.tensor_scalar(own, own, -float(SLOTS), None, ALU.add)\
                            .then_inc(V.sem("places_moved"), 1)

                def start(j):
                    pass

                def group(g, j, first):
                    for f in range(4):
                        if f == 2 and j is not None:
                            split_lo(base + first_slab(0, first), j, GROUP_SLABS)
                        V.groups("xg_hi", j, f + 1, 4)
                        tt(xg[:, :, 2 * f:2 * f + 2, SLOTS:2 * SLOTS],
                           bank[f % 2][:].rearrange("p (c e s) -> p e c s", c=2, e=EPG),
                           xg[:, :, 2 * f:2 * f + 2, 0:SLOTS].bitcast(F32), ALU.subtract)\
                            .then_inc(V.sem("xg_lo"), 1)
                    for m in (1, 2) if j is not None else ():
                        split_lo(base + first_slab(0, first) + m, j, GROUP_SLABS)
                    for i in range(EPG):
                        n = base + first_slab(i, first)
                        after = n + (4 if first and i == 0 else 6)
                        split_lo(n + 3, j, GROUP_SLABS)
                        V.upto("gate_low", i, j)
                        V.upto("act_gated", i - 1, j)
                        tt(hg, bank[0][0:SLOTS, :], low_g, ALU.add).then_inc(V.sem("gate_added"), 1)
                        if after == n + 6:
                            split_lo(n + 4, j, GROUP_SLABS)
                            turned_lo(i - 1, j)
                            split_lo(n + 5, j, GROUP_SLABS)
                        if i == EPG - 1:
                            V.upto("dispatched", i, j)
                            V.groups("places_moved", j, 0, HALVES)
                            slots_of(1 if first else (g + 1) % EGROUPS)
                            move_places(1 if first else (g + 1) % EGROUPS, j + 1 if j is not None else 1)
                        if i < EPG - 1:
                            split_lo(after, j, GROUP_SLABS)
                        V.upto("up_low", i, j)
                        tt(hu, bank[1][0:SLOTS, :], low_u, ALU.add).then_inc(V.sem("up_added"), 1)
                        V.upto("up_added", i, j)
                        V.upto("dispatch_copied", i, j, k=2)
                        V.upto("silu_done", i, j)
                        nc.vector.scalar_tensor_tensor(out=act_e, in0=hu, scalar=slot_gate[0:SLOTS, i % 2:i % 2 + 1],
                                                       in1=hg, op0=ALU.mult, op1=ALU.mult)\
                            .then_inc(V.sem("act_gated"), 1)
                        if i < EPG - 1:
                            for m in (1, 2):
                                split_lo(after + m, j, GROUP_SLABS)

                def finish(j, j0):
                    for m in (2, 1):
                        split_lo(base + PER_ROUND - m, j0, GROUP_SLABS)
                    turned_lo(EPG - 1, j)

                slots_of(0)
                move_places(0, None)
                return over_experts(dve, layer, start, group, finish)

            dve.wait_ge(S["x_in"], 16 * HALVES)
            mean_square([(0, HALVES, D)], EPS_RMS, HALVES)
            w.next("rstd_ready")
            for i in range(HALVES):
                nc.vector.tensor_scalar(xn[:, i, :], x[:, i, :], stat[:, 2, i:i + 1], None, ALU.mult)\
                    .then_inc(S["normed"], 1)
            w.next("params_copied")
            feature_major(DC, lambda c: V_G1 + c)
            splits_to(S_QK + 5)
            save_half(S_QK + 3, "qk_saved1", [(qk[:, 1, 512 * i:512 * (i + 1)], bank[2 + i][:]) for i in range(2)])
            w.next("qk_saved0", 2)
            w.next("qk_saved1", 2)
            qk_heads = qk.rearrange("p a (h d) -> p (a h) d", d=HD)
            sq = xn[:].rearrange("p a (h d) -> p (a h) d", d=HD)
            n_rows = HALVES * 2 * HEADS
            tt(sq, qk_heads, qk_heads, ALU.mult).then_inc(S["qk_squared"], 1)
            splits_to(S_VU + 2)
            w.next("qk_squared")
            nc.vector.tensor_reduce(stat[:, 0, 0:n_rows], sq, AX.X, ALU.add).then_inc(S["qk_summed"], 1)
            w.next("qk_summed")
            mean_square([(0, n_rows, HD)], EPS_RMS, 0)
            splits_to(S_VU + 5)
            save_half(S_VU + 3, "vu_saved1", [(vu[:, 1, 512 * i:512 * (i + 1)], bank[6 + i][:]) for i in range(2)])
            splits_to(S_GATE + 2)
            w.next("rstd_ready")
            tt(qk_heads, qk_heads, stat[:, 2, 0:n_rows].unsqueeze(2).broadcast_to([P, n_rows, HD]), ALU.mult)\
                .then_inc(S["qk_scaled"], 1)
            splits_to(S_GATE + 3)
            w.next("qk_scaled")
            for i in range(2):
                part = qk[:, :, WIDTH * i:WIDTH * (i + 1)].rearrange("p a (h d) -> p a h d", d=HD)
                gain = head_gain[:, i, :].unsqueeze(1).unsqueeze(1).broadcast_to([P, HALVES, HEADS, HD])
                tt(part, part, gain, ALU.mult).then_inc(S["qk_gained"], 1)
            splits_to(S_GATE + 4)
            w.next("qk_gained", 2)
            four = qk.rearrange("p a (h d) -> p a h d", d=HD)
            shape = [P, HALVES, 2 * HEADS, ROPE1]

            def tmp1(i):
                n = HALVES * 2 * HEADS * ROPE1
                flat = xn[:].rearrange("p a n -> p (a n)")[:, i * n:(i + 1) * n]
                return flat.rearrange("p (a h d) -> p a h d", a=HALVES, d=ROPE1)

            rotate(four[:, :, :, 0:ROPE1], four[:, :, :, ROPE1:2 * ROPE1], cos1, sin1, tmp1, shape)
            splits_to(S_GATE + 9)
            w.next("mixed_hi", GROUPS)
            for g in range(GROUPS):
                nc.vector.scalar_tensor_tensor(
                    out=xs[:, 4 + g, SEQ:2 * SEQ], in0=bank[6 + g // 2][:, (g % 2) * SEQ:(g % 2 + 1) * SEQ],
                    scalar=vec[:, V_PS + g:V_PS + g + 1], in1=xs[:, 4 + g, 0:SEQ].bitcast(F32),
                    op0=ALU.mult, op1=ALU.subtract).then_inc(S["mixed_lo"], 1)
            splits_to(S_BA + 2)
            attention(SC1, 0)
            feature_major(4)
            splits_to(S_BP + 1)
            dve.wait_ge(S["gates_saved"], 2 * 8)
            for i in range(4):
                dve.wait_ge(S["slab_used"], S_BA + i // 2 + 1)
                tt(mix[:, 2 * i:2 * i + 2, :], bank[i][:].rearrange("p (c t) -> p c t", c=2),
                   gates[:, 2 * i:2 * i + 2, :], ALU.mult).then_inc(S["a_gated"], 1)
            for i in range(4):
                if i % 2 == 0:
                    splits_to(S_OUT + i // 2)
                dve.wait_ge(S["slab_used"], S_BP + i // 2 + 1)
                part = gates[:, DC + 2 * i:DC + 2 * i + 2, :]
                tt(part, bank[4 + i][:].rearrange("p (c t) -> p c t", c=2), part, ALU.mult)\
                    .then_inc(S["b_gated"], 1)
            w.next("a_gated", 4)
            w.next("b_gated", 4)
            for i in range(4):
                part = mix[:, 2 * i:2 * i + 2, :]
                tt(part, part, gates[:, DC + 2 * i:DC + 2 * i + 2, :], ALU.add).then_inc(S["ab_summed"], 1)
            for i in range(4):
                w.next("mixed_hi")
                tt(xs[:, 2 * i:2 * i + 2, SEQ:2 * SEQ], mix[:, 2 * i:2 * i + 2, :],
                   xs[:, 2 * i:2 * i + 2, 0:SEQ].bitcast(F32), ALU.subtract).then_inc(S["mixed_lo"], 1)
            splits_to(S_OUT + 3)

            def add_to_x(first):
                for i in range(4):
                    part = x[:, i // 2, 512 * (i % 2):512 * (i % 2 + 1)]
                    tt(part, part, bank[first + i][:], ALU.add).then_inc(S["x_updated"], 1)
                w.next("x_updated", 4)

            dve.wait_ge(S["slab_used"], S_OUT + 4)
            add_to_x(0)
            mean_square([(0, HALVES, D)], EPS_RMS, HALVES)
            w.next("rstd_ready")
            for i in range(HALVES):
                nc.vector.tensor_scalar(xn[:, i, :], x[:, i, :], stat[:, 2, i:i + 1], None, ALU.mult)\
                    .then_inc(S["normed"], 1)
            splits_to(S_FFN)
            feature_major(DC, lambda c: V_G2 + c)

            def ffn_step(n, par, j, jj=None):
                first = jj is None
                split_lo(n + 1, jj, 6)
                split_lo(n + 2, jj, 6)
                for side, name in ((0, "g"), (1, "v")):
                    if side and not first:
                        split_lo(n + 3, jj, 6)
                    dve.wait_ge(S["tap2_" + name], j * 2 + 2)
                    for t, done in ((1, "tap1_"), (0, "taps_")):
                        back = 2 - t
                        if t == 0:
                            dve.wait_ge(S["tap1_" + name], j * 2 + 2)
                        for c in range(2):
                            dst = y[:, side, c, back:SEQ]
                            nc.vector.scalar_tensor_tensor(
                                out=dst, in0=bank[side][:, c * SEQ:(c + 1) * SEQ - back],
                                scalar=conv[:, t, bass.ds(j * 2 + side * FFC + c, 1)], in1=dst,
                                op0=ALU.mult, op1=ALU.add).then_inc(S[done + name], 1)
                dve.wait_ge(S["silu_done"], j + 1)
                dve.wait_ge(S["taps_v"], j * 2 + 2)
                tt(y[:, 1, :, :], y[:, 0, :, :], y[:, 1, :, :], ALU.mult).then_inc(S["act_ready"], 1)
                dve.wait_ge(S["act_hi"], j + 1)
                tt(act_s[:, par, :, SEQ:2 * SEQ], y[:, 1, :, :], act_s[:, par, :, 0:SEQ].bitcast(F32), ALU.subtract)\
                    .then_inc(S["act_lo"], 1)

            ffn_step(S_FFN, 0, 0)
            with dve.Fori(0, (N_FF - 1) // 2) as jj:
                for s in range(2):
                    ffn_step(S_FFN_LOOP + 3 * s, (1 + s) % 2, jj * 2 + (1 + s), jj)
            split[0] = S_BLOCK2
            splits_to(S_BLOCK2 + L_IN + 1)
            w.next("acc_closed")
            add_to_x(4)

            for layer in range(LAYERS):
                b = layer_base(layer)
                feature_major(DC)
                splits_to(b + L_IN + 5)
                save_half(b + L_IN + 3, "in_saved1", [(proj[:, 1, 512 * i:512 * (i + 1)], bank[2 + i][:]) for i in range(2)])
                splits_to(b + L_IN_C + 1)
                save_half(b + L_IN_C, "in_saved1", [(proj[:, 1, D:D + 512], bank[5][:])])
                for i in range(HALVES):
                    nc.vector.tensor_copy(proj[:, i, D + 512:IN2], bank[6 + i][:, 0:IN2 - D - 512])\
                        .then_inc(S["in_saved1"], 1)
                w.next("in_saved1", 5)
                w.next("in_saved0", 3)
                mean_square([(0, 2, Q_LORA), (2, 2, KV_LORA)], EPS_RMS, 2 * HALVES)
                kr = proj[:, :, AT_KR:AT_KR + KR]
                spare4 = spare.rearrange("p (i n) -> p i n", i=4)

                def tmp_k(i):
                    return spare4[:, i, 0:HALVES * ROPE2].rearrange("p (a h d) -> p a h d", a=HALVES, h=1)

                kr4 = kr.unsqueeze(2)
                rotate(kr4[:, :, :, 0:ROPE2], kr4[:, :, :, ROPE2:KR], cos2, sin2, tmp_k, [P, HALVES, 1, ROPE2])
                nc.vector.tensor_scalar(idx_w[:], proj[:, :, AT_IW:IN2], IDX_HEADS ** -0.5, None, ALU.mult)\
                    .then_inc(S["idx_weights"], 1)
                w.next("rstd_ready")
                for p_, (at, n) in enumerate(((0, Q_LORA), (AT_KVA, KV_LORA))):
                    for i in range(HALVES):
                        nc.vector.tensor_scalar(xn[:, i, at:at + n], proj[:, i, at:at + n],
                                                stat[:, 2, 2 * p_ + i:2 * p_ + i + 1], None, ALU.mult)\
                            .then_inc(S["normed"], 1)
                feature_major(QC + KVC, lambda c: V_QA + QC * layer + c if c < QC else V_KVA + KVC * layer + c - QC)
                splits_to(b + L_UV)
                w.next("pads_zero", 2)
                w.next("rope_summed", 2 if layer else 4)
                nc.vector.tensor_copy(k_up[:, :, :, HD:MLA_D], kr.unsqueeze(2).broadcast_to([P, HALVES, HEADS, KR]))\
                    .then_inc(S["kr_spread"], 1)
                for i in range(2):
                    save_half(b + L_QUP + i, "qup_saved1",
                              [(q_up[:, 1, 4 * i:4 * i + 4, 0:MLA_D],
                                bank[2 * i + 1][:, 0:4 * MLA_D].rearrange("p (h d) -> p h d", h=4))])
                w.next("qup_saved0", 2)
                w.next("qup_saved1", 2)

                save_half(b + L_UK, "uk_saved1",
                          [(k_up[:, 1, :, 0:HD], bank[5][:].rearrange("p (h d) -> p h d", h=HEADS))])
                save_half(b + L_UV, "uv_saved1", [(value[:, 1, :], bank[7][:])])
                def tmp_q(i):
                    return spare4[:, i, :].rearrange("p (a h d) -> p a h d", a=HALVES, h=HEADS)

                rotate(q_up[:, :, :, HD:HD + ROPE2], q_up[:, :, :, HD + ROPE2:MLA_D], cos2, sin2, tmp_q,
                       [P, HALVES, HEADS, ROPE2])
                w.skip("rope_summed", 2)
                for i in range(3):
                    w.next("turned_b", 2)
                    nc.vector.tensor_copy(sparse_t[:, 4 * i + 2:4 * i + 4, :], bank[7][:].rearrange("p (c t) -> p c t", c=2))\
                        .then_inc(S["copied_odd"], 1)

                w.next("idx_weights")
                score = sel_score
                for i in range(HALVES * IDX_HEADS):
                    half, h = divmod(i, IDX_HEADS)
                    keys = P * (half + 1)
                    dst = score[:, half, 0:keys]
                    w.next("idx_relu")
                    weight = idx_w[:, half, h:h + 1]
                    if h == 0:
                        nc.vector.tensor_scalar(dst, logit[:, i % 2, 0:keys], weight, None, ALU.mult)\
                            .then_inc(S["idx_added"], 1)
                    else:
                        nc.vector.scalar_tensor_tensor(out=dst, in0=logit[:, i % 2, 0:keys], scalar=weight, in1=dst,
                                                       op0=ALU.mult, op1=ALU.add).then_inc(S["idx_added"], 1)
                    w.next("idx_added")
                for half in range(HALVES):
                    keys = P * (half + 1)
                    dst = score[:, half, 0:keys]
                    tt(dst, dst, mask[:, half, 0:keys], ALU.add).then_inc(S["idx_masked"], 1)
                for i in range(4):
                    w.next("turned_a", 2)
                    nc.vector.tensor_copy(k_t[:, 2 * i:2 * i + 2, :], bank[7][:].rearrange("p (c t) -> p c t", c=2))\
                        .then_inc(S["copied_k"], 1)
                w.next("idx_masked", HALVES)

                assert KEEP // 8 == HEADS

                def largest(i):
                    half = i // HEADS
                    if i:
                        w.next("topk_step")
                    nc.vector.max(best, score[:, half, 0:P * (half + 1)]).then_inc(S["topk_step"], 1)

                def take(i):
                    dst = score[:, i // HEADS, 0:P * (i // HEADS + 1)]
                    w.next("topk_step")
                    nc.vector.match_replace(dst, best, dst, TAKEN).then_inc(S["topk_step"], 1)

                attention(SC_MLA, 0, before=largest, after=take)
                w.next("topk_step")
                for half in range(HALVES):
                    keys = P * (half + 1)
                    dst = score[:, half, 0:keys]
                    nc.vector.tensor_scalar(dst, dst, TAKEN * 0.5, -NEG, ALU.is_le, ALU.mult).then_inc(S["sel_step"], 1)
                w.next("sel_step", HALVES)
                for half in range(HALVES):
                    keys = P * (half + 1)
                    dst = score[:, half, 0:keys]
                    nc.vector.scalar_tensor_tensor(out=dst, in0=dst, scalar=NEG, in1=mask[:, half, 0:keys],
                                                   op0=ALU.add, op1=ALU.add).then_inc(S["sel_step"], 1)
                w.next("sel_step", HALVES)
                w.next("router_w_hi")
                tt(router_s[:, :, EXPERTS:2 * EXPERTS], router_w[:], router_s[:, :, 0:EXPERTS].bitcast(F32),
                   ALU.subtract).then_inc(S["router_w_lo"], 1)
                attention(SC_DSA, WIDTH, sparse=True,
                          after=lambda i: splits_to(b + L_O + L_O_AFTER.index(i)) if i in L_O_AFTER else None)
                feature_major(DC)
                splits_to(b + L_O + 3)
                wait_slab(dve, "slab_used", b + L_O + 3)
                for norm in range(2):
                    if norm:
                        feature_major(DC)
                        splits_to(b + L_MOE + 1)
                        router()
                        splits_to(b + L_MOE + 2)
                        w.next("rows_hi")
                        tt(x_rows[:, 1], x[:], x_rows[:, 0].bitcast(F32), ALU.subtract).then_inc(S["rows_lo"], 1)
                        places()
                        experts(b, layer)
                        split[0] = b + PER_LAYER
                        splits_to(b + PER_LAYER + 1)
                        w.next("acc_closed")
                    for i in range(4):
                        part = x[:, i // 2, 512 * (i % 2):512 * (i % 2 + 1)]
                        nc.vector.scalar_tensor_tensor(out=part, in0=part, scalar=ALPHA,
                                                       in1=bank[4 * norm + i][:], op0=ALU.mult, op1=ALU.add,
                                                       accum_out=stat[:, 0, i:i + 1]).then_inc(S["ln_added"], 1)
                    w.next("ln_added", 4)
                    tt(stat[:, 1, 0:2], stat[:, 0, 0:4:2], stat[:, 0, 1:4:2], ALU.add).then_inc(S["ln_mean_step"], 1)
                    w.next("ln_mean_step")
                    nc.vector.tensor_scalar(stat[:, 1, 2:4], stat[:, 1, 0:2], -1.0 / D, None, ALU.mult)\
                        .then_inc(S["ln_mean_step"], 1)
                    w.next("ln_mean_step")
                    w.next("ln_in", 32)
                    for i in range(HALVES):
                        nc.vector.scalar_tensor_tensor(out=xn[:, i, :], in0=x[:, i, :], scalar=stat[:, 1, 2 + i:3 + i],
                                                       in1=ln_gb[:, 0, :], op0=ALU.add, op1=ALU.mult)\
                            .then_inc(S["ln_scaled"], 1)
                    w.next("squares_summed", HALVES)
                    nc.vector.tensor_scalar(stat[:, 1, 0:2], stat[:, 0, 4:6], 1.0 / D, EPS_LN, ALU.mult, ALU.add)\
                        .then_inc(S["mean_square"], 1)
                    w.next("rstd_ready")
                    w.next("ln_scaled", HALVES)
                    for i in range(HALVES):
                        nc.vector.scalar_tensor_tensor(out=x[:, i, :], in0=xn[:, i, :], scalar=stat[:, 2, i:i + 1],
                                                       in1=ln_gb[:, 1, :], op0=ALU.mult, op1=ALU.add)\
                            .then_inc(S["ln_done"], 1)
                    w.next("ln_done", HALVES)
        @block.tensor
        def _(pe):
            w = Waits(pe, S)
            mm = nc.tensor.matmul

            def turn(dst, src):
                return nc.tensor.transpose(dst, src, ident[0:src.shape[0], 0:src.shape[0]])

            fm = [0]

            def feature_major(chunks, src):
                for b in range(0, chunks, 2):
                    w.upto("fm_lo", fm[0] - 1)
                    for c in range(b, min(b + 2, chunks)):
                        for half in range(HALVES):
                            at = (c - b) * SEQ + half * P
                            ins = turn(bank[6 + fm[0] % 2][:, at:at + P], src(c, half))
                    ins.then_inc(S["fm_turned"], 1)
                    fm[0] += 1

            def fm_ready():
                w.upto("fm_lo", fm[0])

            def products(out_, lhs_hi, lhs_lo, rhs_hi, rhs_lo, first, last):
                mm(out_, lhs_hi, rhs_hi, start=first, stop=False)
                mm(out_, lhs_lo, rhs_hi, start=False, stop=False)
                return mm(out_, lhs_hi, rhs_lo, start=False, stop=last)

            def token_major(n, slabs, k_per, widths, banks, chunk=0, lhs=xs, j=None, per=0, open_=True, close=True,
                            ready=None):
                for s in range(slabs):
                    if ready:
                        ready()
                    wait_slab(pe, "lo_done", n + s, j, per)
                    wh, wl = (slab_of(t, n + s, k_per)(sum(widths)) for t in (hi, lo))
                    for k in range(k_per):
                        kk = s * k_per + k
                        first, last = open_ and kk == 0, close and kk == slabs * k_per - 1
                        for half in range(HALVES):
                            at = half * P
                            a_hi = lhs[:, chunk + kk, at:at + P]
                            a_lo = lhs[:, chunk + kk, SEQ + at:SEQ + at + P]
                            for i, width in enumerate(widths):
                                c0 = sum(widths[:i])
                                ins = products(banks[half][i][:, 0:width], a_hi, a_lo, wh[:, k, c0:c0 + width],
                                               wl[:, k, c0:c0 + width], first, last)
                    ins.then_inc(ring("slab_used", n + s)[0], 1)

            def feature_slab(n, k_chunks, columns, banks, chunk=0, j=None, per=0):
                wait_slab(pe, "lo_done", n, j, per)
                wh, wl = (slab_of(t, n, k_chunks)(columns) for t in (hi, lo))
                for c in range(columns // P):
                    dst = banks[c // 2][:, (c % 2) * SEQ:(c % 2 + 1) * SEQ]
                    for k in range(k_chunks):
                        x_hi, x_lo = xs[:, chunk + k, 0:SEQ], xs[:, chunk + k, SEQ:2 * SEQ]
                        col = slice(c * P, (c + 1) * P)
                        mm(dst, wh[:, k, col], x_hi, start=k == 0, stop=False)
                        mm(dst, wh[:, k, col], x_lo, start=False, stop=False)
                        ins = mm(dst, wl[:, k, col], x_hi, start=False, stop=k == k_chunks - 1)
                ins.then_inc(ring("slab_used", n)[0], 1)

            units = [0]

            def attention(q, k, v):
                base, n = units[0], 2 * HEADS

                def score(i):
                    half, h = divmod(i, HEADS)
                    if i >= 2:
                        pe.wait_ge(S["logits"], base + i - 1)
                    keys = P * (half + 1)
                    mm(bank[i % 2][:, 0:keys], q(h, half), k(h)[:, 0:keys], start=True, stop=True)\
                        .then_inc(S["scores"], 1)

                def flip(i):
                    pe.wait_ge(S["probs"], base + i + 1)
                    if i >= 2:
                        pe.wait_ge(S["probs_turned"], base + i - 1)
                    for c in range(i // HEADS + 1):
                        ins = turn(bank[2 + i % 2][:, c * P:(c + 1) * P], prob[:, i % 2, c * P:(c + 1) * P])
                    ins.then_inc(S["flipped"], 1)

                def weigh(i):
                    half, h = divmod(i, HEADS)
                    pe.wait_ge(S["probs_turned"], base + i + 1)
                    for c in range(half + 1):
                        ins = mm(bank[4 + half][:, h * HD:(h + 1) * HD], prob_t[:, i % 2, c, :], v(h, c),
                                 start=c == 0, stop=c == half)
                    ins.then_inc(S["weighted"], 1)

                for i in range(n + 3):
                    if i < n:
                        score(i)
                    if 2 <= i < n + 2:
                        flip(i - 2)
                    if i >= 3:
                        weigh(i - 3)
                units[0] += n

            halves4 = [[bank[0], bank[1]], [bank[2], bank[3]]]
            acc = [[bank[4], bank[5]], [bank[6], bank[7]]]

            def open_acc():
                for half in range(HALVES):
                    for i in range(2):
                        mm(acc[half][i][:], zeros[:], zeros[:, 0:1].broadcast_to([P, 512]), start=True, stop=False)

            def close_acc():
                for half in range(HALVES):
                    for i in range(2):
                        ins = mm(acc[half][i][:], zeros[:], zeros[:, 0:1].broadcast_to([P, 512]), start=False, stop=True)
                ins.then_inc(S["acc_closed"], 1)

            w.next("first_in", 16 * N_FIRST)
            turn(bank[0][:, 0:V_N], rows).then_inc(S["turned_params"], 1)
            w.next("normed", HALVES)
            feature_major(DC, lambda c, half: xn[:, half, c * P:(c + 1) * P])
            w.next("params_in", 16 * N_PARAMS)
            for t in range(TAPS + 1):
                ins = turn(bank[1][:, t * 2 * FFC:(t + 1) * 2 * FFC], conv_rows[:, t, :])
            ins.then_inc(S["turned_params"], 1)
            fm_ready()
            w.next("params_copied", 2)
            token_major(S_QK, 4, 2, [512, 512], halves4)
            token_major(S_VU, 4, 2, [512, 512], acc)
            for i in range(8):
                if i == 0:
                    w.next("qk_saved0", 2)
                    w.next("qk_saved1", 2)
                if i >= 4:
                    pe.wait_ge(S["gates_saved"], 2 * (i - 3))
                feature_slab(S_GATE + i, DC, 256, [bank[i % 4]])
            w.next("vu_saved0", 2)
            w.next("vu_saved1", 2)
            for g in range(GROUPS):
                dst = bank[4 + g // 2][:, (g % 2) * SEQ:(g % 2 + 1) * SEQ]
                for half in range(HALVES):
                    ins = mm(dst, vu[:, half, WIDTH + g * P:WIDTH + (g + 1) * P], band[:, g, half, :],
                             start=half == 0, stop=half == HALVES - 1)
            ins.then_inc(S["pooled_summed"], 1)
            w.next("pooled_copied", 2)
            for g in range(GROUPS):
                ins = mm(bank[6 + g // 2][:, (g % 2) * SEQ:(g % 2 + 1) * SEQ], w_pool[:, g, :], pooled[:, g, :],
                         start=True, stop=True)
            ins.then_inc(S["mixed_summed"], 1)
            w.next("rope_summed", 2)
            w.next("gates_saved", 2 * 8)
            for b in range(4):
                w.upto("pairs_copied", (0, 0, 1, 2)[b])
                for c in range(2):
                    for half in range(HALVES):
                        at = c * SEQ + half * P
                        col = (2 * b + c) * P
                        ins = turn(bank[b % 2][:, at:at + P], qk[:, half, col:col + P])
                ins.then_inc(S["pairs_turned"], 1)
            w.next("pairs_copied", 6)
            attention(lambda h, half: q_t[:, h // 2, half * P:(half + 1) * P],
                      lambda h: k_t[:, h, :],
                      lambda h, c: vu[:, c, h * HD:(h + 1) * HD])
            w.next("mixed_lo", GROUPS)
            w.next("heads_saved", 2)
            feature_major(4, lambda c, half: xn[:, half, c * P:(c + 1) * P])
            fm_ready()
            for i in range(2):
                feature_slab(S_BA + i, 4, 512, bank[2 * i:2 * i + 2])
            for i in range(2):
                feature_slab(S_BP + i, 4, 512, bank[4 + 2 * i:6 + 2 * i], chunk=4)
            token_major(S_OUT, 4, 2, [512, 512], halves4, ready=lambda: w.next("mixed_lo"))
            w.next("normed", HALVES)
            feature_major(DC, lambda c, half: xn[:, half, c * P:(c + 1) * P])
            fm_ready()
            pe.wait_ge(S["fills_set"], 3)
            open_acc()

            def down(n, par, j, jj=None):
                pe.wait_ge(S["act_lo"], j)
                token_major(n, 1, 2, [512, 512], acc, lhs=act_s[:, par], j=jj, per=6, open_=False, close=False)

            feature_slab(S_FFN, DC, 256, [bank[0]])
            feature_slab(S_FFN + 1, DC, 256, [bank[1]])
            with pe.Fori(0, (N_FF - 1) // 2) as jj:
                for s in range(2):
                    n, j = S_FFN_LOOP + 3 * s, jj * 2 + (1 + s)
                    pe.wait_ge(S["taps_g"], j * 2)
                    feature_slab(n, DC, 256, [bank[0]], j=jj, per=6)
                    pe.wait_ge(S["taps_v"], j * 2)
                    feature_slab(n + 1, DC, 256, [bank[1]], j=jj, per=6)
                    down(n + 2, s, j, jj)
            down(S_BLOCK2 - 1, 0, N_FF)
            close_acc()
            w.next("x_updated", 8)

            for layer in range(LAYERS):
                b = layer_base(layer)
                feature_major(DC, lambda c, half: x[:, half, c * P:(c + 1) * P])
                fm_ready()
                token_major(b + L_IN, 4, 2, [512, 512], halves4)
                token_major(b + L_IN_B, 2, 4, [512], [[bank[4]], [bank[5]]])
                token_major(b + L_IN_C, 1, DC, [IN2 - D - 512], [[bank[6]], [bank[7]]])
                w.next("normed", 2 * HALVES)
                feature_major(QC + KVC, lambda c, half: xn[:, half, c * P:(c + 1) * P])
                fm_ready()
                for i in range(2):
                    token_major(b + L_QUP + i, 1, QC, [4 * MLA_D], [[bank[2 * i]], [bank[2 * i + 1]]])
                token_major(b + L_UK, 1, KVC, [WIDTH], [[bank[4]], [bank[5]]], chunk=QC)
                token_major(b + L_UV, 1, KVC, [WIDTH], [[bank[6]], [bank[7]]], chunk=QC)
                for name in ("qup_saved0", "qup_saved1"):
                    w.next(name, 2)
                for name in ("uk_saved0", "uk_saved1", "uv_saved0", "uv_saved1"):
                    w.next(name)

                def sparse_src(c, half):
                    if c < T_DK:
                        return proj[:, half, AT_DQ + c * P:AT_DQ + (c + 1) * P]
                    if c < T_IQ:
                        return stage[:, half, c - T_DK, :]
                    return proj[:, half, AT_IQ + (c - T_IQ) * P:AT_IQ + (c - T_IQ + 1) * P]

                w.next("staged", 6)
                for i in range(6):
                    w.upto(("copied_even", "copied_odd")[i % 2], 3 * layer + i // 2)
                    for c in range(2):
                        for half in range(HALVES):
                            at = c * SEQ + half * P
                            ins = turn(bank[6 + i % 2][:, at:at + P], sparse_src(2 * i + c, half))
                    ins.then_inc(S["turned_b"], 1)
                w.next("copied_even", 3)
                w.next("copied_odd", 3)
                n_idx = HALVES * IDX_HEADS
                for i in range(n_idx):
                    half, h = divmod(i, IDX_HEADS)
                    keys = P * (half + 1)
                    if i >= 2:
                        pe.wait_ge(S["idx_relu"], n_idx * layer + i - 1)
                    mm(bank[i % 2][:, 0:keys], sparse_t[:, T_IQ + h // 4, half * P:(half + 1) * P],
                       sparse_t[:, T_IK + h % 4, 0:keys], start=True, stop=True).then_inc(S["idx_scores"], 1)
                w.next("idx_relu", n_idx)
                pe.wait_ge(S["rope_summed"], 2 + 4 * (layer + 1))
                w.next("kr_spread")
                w.next("pads_zero", 2)
                for i in range(4):
                    for src, to, copied in ((q_up, bank[6], "copied_q"), (k_up, bank[7], "copied_k")):
                        w.upto(copied, 4 * layer + i)
                        for c in range(2):
                            for half in range(HALVES):
                                at = c * SEQ + half * P
                                ins = turn(to[:, at:at + P], src[:, half, 2 * i + c, :])
                        ins.then_inc(S["turned_a"], 1)
                w.next("copied_q", 4)
                w.next("copied_k", 4)
                attention(lambda h, half: q_t[:, h, half * P:(half + 1) * P],
                          lambda h: k_t[:, h, :],
                          lambda h, c: value[:, c, h * HD:(h + 1) * HD])

                w.next("heads_saved", 2)
                attention(lambda h, half: sparse_t[:, T_DQ + h // 2, half * P:(half + 1) * P],
                          lambda h: sparse_t[:, T_DK + h % 2, :],
                          lambda h, c: proj[:, c, AT_DV:AT_DV + HD])
                w.next("heads_saved", 2)
                feature_major(DC, lambda c, half: xn[:, half, c * P:(c + 1) * P])
                fm_ready()
                token_major(b + L_O, 4, 2, [512, 512], halves4)
                pe.wait_ge(S["ln_done"], 2 * HALVES * layer + HALVES)
                feature_major(DC, lambda c, half: x[:, half, c * P:(c + 1) * P])
                fm_ready()
                w.next("router_w_hi")
                w.next("router_w_lo")
                for k in range(DC):
                    for part in range(2):
                        ins = mm(bank[0][:, 0:SEQ], router_s[:, k, :], xs[:, k, part * SEQ:(part + 1) * SEQ],
                                 start=k == 0 and part == 0, stop=k == DC - 1 and part == 1)
                ins.then_inc(S["router_parts"], 1)
                w.next("parts_copied")
                for half in range(HALVES):
                    ins = mm(bank[1][:, EXPERTS * half:EXPERTS * (half + 1)], logit_parts[:, half * P:(half + 1) * P],
                             const[0:2 * EXPERTS, C_FOLD:C_KEPT], start=True, stop=True)
                ins.then_inc(S["router_logits"], 1)
                w.next("routed")
                picked = route[:, 4, :].rearrange("p (a e) -> p a e", a=HALVES)
                all_ones = one.broadcast_to([P, P])
                mm(bank[3][:, 0:EXPERTS], before, picked[:, 0, :], start=True, stop=True)
                mm(bank[3][:, EXPERTS:2 * EXPERTS], all_ones, picked[:, 0, :], start=True, stop=False)
                mm(bank[3][:, EXPERTS:2 * EXPERTS], before, picked[:, 1, :], start=False, stop=True)
                for half in range(HALVES):
                    ins = mm(bank[3][:, 2 * EXPERTS:3 * EXPERTS], all_ones, picked[:, half, :], start=half == 0,
                             stop=half == HALVES - 1)
                ins.then_inc(S["counted"], 1)
                open_acc()
                w.next("rows_lo")
                base = b + L_MOE
                V = Visits(pe, layer)

                def wide_product(n, j, lhs, k_per, to, between=None):
                    for s in range(2):
                        if s and between:
                            between()
                        wait_slab(pe, "lo_done", n + s, j, GROUP_SLABS)
                        wh, wl = (slab_of(t, n + s, k_per)(512 * len(to)) for t in (hi, lo))
                        for k in range(k_per):
                            kk = s * k_per + k
                            for c, dst in enumerate(to):
                                col = slice(512 * c, 512 * (c + 1))
                                mm(dst[:], lhs(kk), wh[:, k, col], start=kk == 0, stop=False)
                                ins = mm(dst[:], lhs(kk), wl[:, k, col], start=False, stop=kk == 2 * k_per - 1)
                        ins.then_inc(ring("slab_used", n + s)[0], 1)

                def scatter(v, j, halves=range(HALVES)):
                    V.upto("expert_out", v, j, k=2)
                    for half in halves:
                        for c in range(2):
                            mm(acc[half][c][:], slot_to_token[:, v % 2, half * P:(half + 1) * P],
                               expert_out[:, c, :], start=False, stop=False)

                def act_there(v, j):
                    V.upto("act_gated", v, j)
                    V.upto("expert_out", v - 1, j, k=2)

                def turn_act(v, j):
                    for c in range(4):
                        ins = turn(bank[2][:, c * SLOTS:(c + 1) * SLOTS], act_e[:, c * P:(c + 1) * P])
                    ins.then_inc(V.sem("act_turned"), 1)

                def down(v, n, j, jn):
                    V.upto("act_lo", v, j)
                    wide_product(n, jn, lambda k: act_t[:, k, :], 2, [bank[2], bank[3]])

                def start(j):
                    pass

                def group(g, j, first):
                    V.groups("one_hot", j, 2, 2)
                    V.upto("gate_added", -1, j)
                    V.upto("up_added", -1, j)
                    for f in range(4):
                        if f >= 2:
                            V.groups("xg_lo", j, f - 1, 4)
                        for c in range(2):
                            chunk = slice((2 * f + c) * P, (2 * f + c + 1) * P)
                            for half in range(HALVES):
                                for part in range(2):
                                    ins = mm(bank[f % 2][:, c * 256:(c + 1) * 256], x_rows[:, part, half, chunk],
                                             one_hot[:, half, :, 0:SLOTS], start=half == 0 and part == 0,
                                             stop=half == 1 and part == 1)
                        ins.then_inc(V.sem("gathered"), 1)
                    V.groups("xg_lo", j, 4, 4)
                    for i in range(EPG):
                        n = base + first_slab(i, first)
                        second = not (first and i == 0)
                        V.upto("gate_added", i - 1, j)
                        out_there = not (first and i <= 1)
                        wide_product(n, j, lambda k: xg[:, i, k, :], 4, [bank[0]],
                                     (lambda: scatter(i - 2, j, [0])) if out_there else None)
                        if out_there:
                            scatter(i - 2, j, [1])
                        if second:
                            act_there(i - 1, j)
                        V.upto("expert_out", i - 2, j, k=2)
                        if first and i == 1:
                            V.upto("dispatch_copied", 0, j, k=2)
                        hot = [one_hot[:, half, i, :].bitcast(F32) for half in range(HALVES)]
                        for half in range(HALVES):
                            mm(bank[3][:, half * P:(half + 1) * P], hot[half], ident, start=True, stop=True)
                        for half in range(HALVES):
                            ins = mm(bank[3][:, SEQ:SEQ + EXPERTS], hot[half],
                                     route[:, 0, EXPERTS * half:EXPERTS * (half + 1)], start=half == 0, stop=half == 1)
                        ins.then_inc(V.sem("dispatched"), 1)
                        if second:
                            turn_act(i - 1, j)
                        V.upto("up_added", i - 1, j)
                        wide_product(n + 2, j, lambda k: xg[:, i, k, :], 4, [bank[1]])
                        if second:
                            V.upto("dispatch_copied", i, j, k=2)
                            down(i - 1, n + 4, j, j)

                def finish(j, j0):
                    act_there(EPG - 1, j)
                    scatter(EPG - 2, j)
                    turn_act(EPG - 1, j)
                    down(EPG - 1, base + PER_ROUND - 2, j, j0)
                    scatter(EPG - 1, j)

                over_experts(pe, layer, start, group, finish)
                close_acc()
                pe.wait_ge(S["ln_done"], 2 * HALVES * (layer + 1))


def kernel(**inputs):
    import numpy as _np
    import concourse.bacc as _bacc
    from concourse import mybir as _mybir
    from concourse.bass_utils import run_bass_kernel_spmd as _run

    nc = _bacc.Bacc("TRN2", target_bir_lowering=False, num_devices=1)
    arrays = {name: _np.ascontiguousarray(value) for name, value in inputs.items()}
    arrays["constants"] = constants()
    aps = {name: nc.dram_tensor(f"in_{name}", a.shape, _mybir.dt.from_np(a.dtype), kind="ExternalInput").ap()
           for name, a in arrays.items()}
    out = nc.dram_tensor("out", (1, SEQ, D), F32, kind="ExternalOutput").ap()
    build(nc, aps, out)
    r = _run(nc, [{f"in_{name}": a for name, a in arrays.items()}], core_ids=[0])
    return r.results[0]["out"]
```
